# Optimizing a Trainium2 kernel written in Bass

```python
import jax, jax.numpy as jnp
from jax import lax
import numpy as np
import math

D_MODEL = 1024
BATCH = 1
SEQ = 256
DEPTH = 2

NSA_HEADS = 8
NSA_HEAD_DIM = 64
NSA_KV_HEADS = 2
NSA_GROUP = NSA_HEADS // NSA_KV_HEADS
NSA_WIDTH = NSA_HEADS * NSA_HEAD_DIM
KV_WIDTH = NSA_KV_HEADS * NSA_HEAD_DIM
CMP_LEN = 32
CMP_STRIDE = 16
CMP_HIDDEN = 256
SLC_LEN = 64
SLC_TOPN = 16
WINDOW = 512
Q_BLOCK = 128
RET_HEADS = 4
RET_HEAD_DIM = 128
RET_WIDTH = RET_HEADS * RET_HEAD_DIM
RET_CHUNK = 128
MEM_LEN = 256
MEM_HEADS = 4
MEM_HEAD_DIM = D_MODEL // MEM_HEADS
D_FF = 2816
EPS = 1e-6
NEG = -1e30

IN_SIZES = (NSA_WIDTH,
            KV_WIDTH, KV_WIDTH,
            KV_WIDTH, KV_WIDTH,
            KV_WIDTH, KV_WIDTH,
            NSA_HEADS * 3,
            RET_WIDTH, RET_WIDTH, RET_WIDTH, RET_WIDTH)
IN_WIDTH = sum(IN_SIZES)
IN_OFFSETS = tuple(int(o) for o in np.cumsum(IN_SIZES)[:-1])


def rms_norm(x, g):
    xf = x.astype(jnp.float32)
    y = xf * lax.rsqrt(jnp.mean(xf * xf, axis=-1, keepdims=True) + EPS)
    return (y * g.astype(jnp.float32)).astype(x.dtype)

def swiglu(x, w_gate, w_up, w_down):
    return (jax.nn.silu(x @ w_gate) * (x @ w_up)) @ w_down

def masked_softmax(s, mask):
    s = jnp.where(mask, s, NEG)
    m = jnp.max(s, axis=-1, keepdims=True)
    p = jnp.where(mask, jnp.exp(s - m), 0.0)
    return p / jnp.maximum(jnp.sum(p, axis=-1, keepdims=True), 1e-30)

def alibi_slopes(n):
    return jnp.asarray(2.0 ** (-8.0 * np.arange(1, n + 1) / n), dtype=jnp.float32)

def compress(kv, pe, w1, w2):
    B, T, G, dh = kv.shape
    nc = (T - CMP_LEN) // CMP_STRIDE + 1
    idx = np.arange(nc)[:, None] * CMP_STRIDE + np.arange(CMP_LEN)[None, :]
    blocks = kv[:, idx] + pe[None, None, :, None, :]
    flat = blocks.transpose(0, 1, 3, 2, 4).reshape(B, nc, G, CMP_LEN * dh)
    return jax.nn.silu(flat @ w1) @ w2

def nsa_mixer(q, k_cmp, v_cmp, k_slc, v_slc, k_win, v_win, gates, cmp_pe, cmp_w1, cmp_w2):
    B, T = q.shape[:2]
    G, R, dh = NSA_KV_HEADS, NSA_GROUP, NSA_HEAD_DIM
    scale = dh ** -0.5
    slopes = alibi_slopes(NSA_HEADS).reshape(G, R)

    kc = compress(k_cmp, cmp_pe[0], cmp_w1[0], cmp_w2[0])
    vc = compress(v_cmp, cmp_pe[1], cmp_w1[1], cmp_w2[1])
    nc = kc.shape[1]
    nsel = T // SLC_LEN
    n_top = min(SLC_TOPN, nsel)

    c_start_np = np.arange(nc) * CMP_STRIDE
    c_end_np = c_start_np + CMP_LEN - 1
    s_start_np = np.arange(nsel) * SLC_LEN
    s_end_np = s_start_np + SLC_LEN - 1
    overlap = jnp.asarray(np.clip(np.minimum(c_end_np[:, None], s_end_np[None, :])
                                  - np.maximum(c_start_np[:, None], s_start_np[None, :]) + 1,
                                  0, None) / CMP_LEN, dtype=jnp.float32)
    c_end = jnp.asarray(c_end_np, dtype=jnp.int32)
    c_mid = jnp.asarray(c_start_np + (CMP_LEN - 1) / 2.0, dtype=jnp.float32)

    k_blocks = k_slc.reshape(B, nsel, SLC_LEN, G, dh).transpose(0, 3, 1, 2, 4)
    v_blocks = v_slc.reshape(B, nsel, SLC_LEN, G, dh).transpose(0, 3, 1, 2, 4)
    k_win_p = jnp.pad(k_win, ((0, 0), (WINDOW, 0), (0, 0), (0, 0)))
    v_win_p = jnp.pad(v_win, ((0, 0), (WINDOW, 0), (0, 0), (0, 0)))

    nb = T // Q_BLOCK
    qb = q.reshape(B, nb, Q_BLOCK, G, R, dh).transpose(1, 0, 2, 3, 4, 5)
    gb = gates.reshape(B, nb, Q_BLOCK, G, R, 3).transpose(1, 0, 2, 3, 4, 5)
    b_ix = jnp.arange(B)[:, None, None, None]
    g_ix = jnp.arange(G)[None, None, :, None]
    jb = jnp.arange(nsel)

    def block_fn(args):
        i, qi, gi = args
        t = i * Q_BLOCK + jnp.arange(Q_BLOCK)
        tf = t.astype(jnp.float32)

        s_c = jnp.einsum('bqgrd,bngd->bgrqn', qi, kc).astype(jnp.float32) * scale
        s_c = s_c - slopes[None, :, :, None, None] * (tf[:, None] - c_mid[None, :])
        p_c = masked_softmax(s_c, (c_end[None, :] <= t[:, None])[None, None, None])
        o_c = jnp.einsum('bgrqn,bngd->bqgrd', p_c.astype(vc.dtype), vc)

        imp = jnp.einsum('bgrqn,nj->bqgj', p_c, overlap)
        cur = t // SLC_LEN
        forced = (jb[None, :] == 0) | (jb[None, :] == cur[:, None]) | (jb[None, :] == cur[:, None] - 1)
        valid = jb[None, :] <= cur[:, None]
        imp = jnp.where(forced[None, :, None, :], 1e4,
                        jnp.where(valid[None, :, None, :], imp, -1.0))
        _, idx = lax.top_k(imp, n_top)

        ks = k_blocks[b_ix, g_ix, idx].reshape(B, Q_BLOCK, G, n_top * SLC_LEN, dh)
        vs = v_blocks[b_ix, g_ix, idx].reshape(B, Q_BLOCK, G, n_top * SLC_LEN, dh)
        spos = (idx[..., None] * SLC_LEN + jnp.arange(SLC_LEN)).reshape(B, Q_BLOCK, G, 1, n_top * SLC_LEN)
        dist_s = t[None, :, None, None, None] - spos
        s_s = jnp.einsum('bqgrd,bqgmd->bqgrm', qi, ks).astype(jnp.float32) * scale
        s_s = s_s - slopes[None, None, :, :, None] * dist_s.astype(jnp.float32)
        p_s = masked_softmax(s_s, dist_s >= 0)
        o_s = jnp.einsum('bqgrm,bqgmd->bqgrd', p_s.astype(vs.dtype), vs)

        kw = lax.dynamic_slice_in_dim(k_win_p, i * Q_BLOCK, WINDOW + Q_BLOCK, axis=1)
        vw = lax.dynamic_slice_in_dim(v_win_p, i * Q_BLOCK, WINDOW + Q_BLOCK, axis=1)
        kpos = i * Q_BLOCK - WINDOW + jnp.arange(WINDOW + Q_BLOCK)
        dist_w = t[:, None] - kpos[None, :]
        mask_w = (dist_w >= 0) & (dist_w < WINDOW) & (kpos[None, :] >= 0)
        s_w = jnp.einsum('bqgrd,bkgd->bqgrk', qi, kw).astype(jnp.float32) * scale
        s_w = s_w - slopes[None, None, :, :, None] * dist_w[None, :, None, None, :].astype(jnp.float32)
        p_w = masked_softmax(s_w, mask_w[None, :, None, None, :])
        o_w = jnp.einsum('bqgrk,bkgd->bqgrd', p_w.astype(vw.dtype), vw)

        gs = jax.nn.sigmoid(gi.astype(jnp.float32))
        o = (gs[..., 0:1] * o_c.astype(jnp.float32) + gs[..., 1:2] * o_s.astype(jnp.float32)
             + gs[..., 2:3] * o_w.astype(jnp.float32))
        return o.reshape(B, Q_BLOCK, NSA_WIDTH).astype(q.dtype)

    out = lax.map(block_fn, (jnp.arange(nb), qb, gb))
    return out.transpose(1, 0, 2, 3).reshape(B, T, NSA_WIDTH)

def retention(q, k, v, g, gn_gain):
    B, T, Hr, d = q.shape
    C = RET_CHUNK
    nch = T // C
    log_g = jnp.log(1.0 - jnp.exp2(-5.0 - jnp.arange(Hr, dtype=jnp.float32)))
    pos = jnp.arange(C, dtype=jnp.float32)
    diff = pos[:, None] - pos[None, :]
    decay_mask = jnp.where(diff >= 0, jnp.exp(jnp.maximum(diff, 0.0) * log_g[:, None, None]), 0.0)
    q_dec = jnp.exp((pos + 1.0) * log_g[:, None])
    k_dec = jnp.exp((C - 1.0 - pos) * log_g[:, None])
    chunk_dec = jnp.exp(C * log_g)

    def to_chunks(a):
        return a.astype(jnp.float32).reshape(B, nch, C, Hr, d).transpose(1, 0, 3, 2, 4)
    qc, kc, vc = to_chunks(q), to_chunks(k * (d ** -0.5)), to_chunks(v)

    def step(state, xs):
        qi, ki, vi = xs
        s = jnp.einsum('bhnd,bhmd->bhnm', qi, ki) * decay_mask[None]
        inner = jnp.einsum('bhnm,bhmd->bhnd', s, vi)
        cross = jnp.einsum('bhnd,bhde->bhne', qi, state) * q_dec[None, :, :, None]
        new_state = (state * chunk_dec[None, :, None, None]
                     + jnp.einsum('bhmd,bhme->bhde', ki * k_dec[None, :, :, None], vi))
        return new_state, inner + cross

    state0 = jnp.zeros((B, Hr, d, d), jnp.float32)
    _, o = lax.scan(step, state0, (qc, kc, vc))
    o = o.transpose(1, 0, 3, 2, 4).reshape(B, T, Hr, d)
    mu = jnp.mean(o, axis=-1, keepdims=True)
    var = jnp.mean(jnp.square(o - mu), axis=-1, keepdims=True)
    o = (o - mu) * lax.rsqrt(var + EPS) * gn_gain.astype(jnp.float32).reshape(Hr, d)
    o = o.reshape(B, T, RET_WIDTH) * jax.nn.silu(g.astype(jnp.float32))
    return o.astype(q.dtype)

def hybrid_mixer(h, w_in, cmp_pe, cmp_w1, cmp_w2, nsa_out_g, ret_gn_g, w_out):
    B, T, _ = h.shape
    parts = jnp.split(h @ w_in, IN_OFFSETS, axis=-1)
    q_n, kc, vc, ks, vs, kw, vw, gates, q_r, k_r, v_r, g_r = parts
    kvs = lambda a: a.reshape(B, T, NSA_KV_HEADS, NSA_HEAD_DIM)
    o_nsa = nsa_mixer(q_n.reshape(B, T, NSA_HEADS, NSA_HEAD_DIM), kvs(kc), kvs(vc), kvs(ks), kvs(vs),
                      kvs(kw), kvs(vw), gates.reshape(B, T, NSA_HEADS, 3), cmp_pe, cmp_w1, cmp_w2)
    o_nsa = rms_norm(o_nsa, nsa_out_g)
    rs = lambda a: a.reshape(B, T, RET_HEADS, RET_HEAD_DIM)
    o_ret = retention(rs(q_r), rs(k_r), rs(v_r), g_r, ret_gn_g)
    return jnp.concatenate([o_nsa, o_ret], axis=-1) @ w_out

def memory_xattn(h, m, wq, wk, wv, wo):
    B, T, _ = h.shape
    M = m.shape[1]
    q = (h @ wq).reshape(B, T, MEM_HEADS, MEM_HEAD_DIM)
    k = (m @ wk).reshape(B, M, MEM_HEADS, MEM_HEAD_DIM)
    v = (m @ wv).reshape(B, M, MEM_HEADS, MEM_HEAD_DIM)
    s = jnp.einsum('bthd,bmhd->bhtm', q, k).astype(jnp.float32) * (MEM_HEAD_DIM ** -0.5)
    p = jax.nn.softmax(s, axis=-1)
    o = jnp.einsum('bhtm,bmhd->bthd', p.astype(v.dtype), v).reshape(B, T, D_MODEL)
    return o @ wo

def first_inputs(seed: int = 0) -> dict:
    key = jax.random.key(seed)
    ks = jax.random.split(key, 28)
    f32 = jnp.float32

    def dense(k, shape, fan_in):
        return jax.random.normal(k, shape, f32) * (fan_in ** -0.5)

    def gain(k, n):
        return 1.0 + 0.02 * jax.random.normal(k, (DEPTH, n), f32)

    L, dh = CMP_LEN, NSA_HEAD_DIM
    return {
        "x": jax.random.normal(ks[0], (BATCH, SEQ, D_MODEL), f32),
        "mem": jax.random.normal(ks[1], (BATCH, MEM_LEN, D_MODEL), f32),
        "ffn1_pre_g": gain(ks[2], D_MODEL),
        "ffn1_w_gate": dense(ks[3], (DEPTH, D_MODEL, D_FF), D_MODEL),
        "ffn1_w_up": dense(ks[4], (DEPTH, D_MODEL, D_FF), D_MODEL),
        "ffn1_w_down": dense(ks[5], (DEPTH, D_FF, D_MODEL), D_FF),
        "ffn1_post_g": gain(ks[6], D_MODEL),
        "mix_pre_g": gain(ks[7], D_MODEL),
        "w_in": dense(ks[8], (DEPTH, D_MODEL, IN_WIDTH), D_MODEL),
        "cmp_pe": 0.5 * jax.random.normal(ks[9], (DEPTH, 2, L, dh), f32),
        "cmp_w1": dense(ks[10], (DEPTH, 2, L * dh, CMP_HIDDEN), L * dh),
        "cmp_w2": dense(ks[11], (DEPTH, 2, CMP_HIDDEN, dh), CMP_HIDDEN),
        "nsa_out_g": gain(ks[12], NSA_WIDTH),
        "ret_gn_g": gain(ks[13], RET_WIDTH),
        "w_out": dense(ks[14], (DEPTH, NSA_WIDTH + RET_WIDTH, D_MODEL), NSA_WIDTH + RET_WIDTH),
        "mix_post_g": gain(ks[15], D_MODEL),
        "xa_pre_g": gain(ks[16], D_MODEL),
        "xa_mem_g": gain(ks[17], D_MODEL),
        "xa_wq": dense(ks[18], (DEPTH, D_MODEL, D_MODEL), D_MODEL),
        "xa_wk": dense(ks[19], (DEPTH, D_MODEL, D_MODEL), D_MODEL),
        "xa_wv": dense(ks[20], (DEPTH, D_MODEL, D_MODEL), D_MODEL),
        "xa_wo": dense(ks[21], (DEPTH, D_MODEL, D_MODEL), D_MODEL),
        "xa_post_g": gain(ks[22], D_MODEL),
        "ffn2_pre_g": gain(ks[23], D_MODEL),
        "ffn2_w_gate": dense(ks[24], (DEPTH, D_MODEL, D_FF), D_MODEL),
        "ffn2_w_up": dense(ks[25], (DEPTH, D_MODEL, D_FF), D_MODEL),
        "ffn2_w_down": dense(ks[26], (DEPTH, D_FF, D_MODEL), D_FF),
        "ffn2_post_g": gain(ks[27], D_MODEL),
    }

def first_block(x, mem, ffn1_pre_g, ffn1_w_gate, ffn1_w_up, ffn1_w_down, ffn1_post_g,
              mix_pre_g, w_in, cmp_pe, cmp_w1, cmp_w2, nsa_out_g, ret_gn_g, w_out, mix_post_g,
              xa_pre_g, xa_mem_g, xa_wq, xa_wk, xa_wv, xa_wo, xa_post_g,
              ffn2_pre_g, ffn2_w_gate, ffn2_w_up, ffn2_w_down, ffn2_post_g):
    for l in range(DEPTH):
        y = swiglu(rms_norm(x, ffn1_pre_g[l]), ffn1_w_gate[l], ffn1_w_up[l], ffn1_w_down[l])
        x = x + 0.5 * rms_norm(y, ffn1_post_g[l])
        y = hybrid_mixer(rms_norm(x, mix_pre_g[l]), w_in[l], cmp_pe[l], cmp_w1[l], cmp_w2[l],
                         nsa_out_g[l], ret_gn_g[l], w_out[l])
        x = x + rms_norm(y, mix_post_g[l])
        y = memory_xattn(rms_norm(x, xa_pre_g[l]), rms_norm(mem, xa_mem_g[l]),
                         xa_wq[l], xa_wk[l], xa_wv[l], xa_wo[l])
        x = x + rms_norm(y, xa_post_g[l])
        y = swiglu(rms_norm(x, ffn2_pre_g[l]), ffn2_w_gate[l], ffn2_w_up[l], ffn2_w_down[l])
        x = x + 0.5 * rms_norm(y, ffn2_post_g[l])
    return x


CHUNK = 64
POOL_WIDTH = D_MODEL // 2
POOL_WINDOWS = (2, 4, 8, 16)
N_POOL_GROUPS = len(POOL_WINDOWS)
POOL_GROUP = POOL_WIDTH // N_POOL_GROUPS
ATTN_WIDTH = D_MODEL - POOL_WIDTH
HEAD_DIM = 64
N_HEADS = ATTN_WIDTH // HEAD_DIM
ROPE_DIM = HEAD_DIM // 4
ROPE_THETA = 500000.0
IDX_HEADS = 8
IDX_DIM = 64
IDX_ROPE_DIM = IDX_DIM // 4
TOPK_MAX = 256
Q_BLOCK_2 = 64
D_FF_2 = 4 * D_MODEL

SPLITS = (POOL_WIDTH, ATTN_WIDTH, ATTN_WIDTH, ATTN_WIDTH, IDX_HEADS * IDX_DIM, IDX_DIM, IDX_HEADS)
IN_WIDTH_2 = sum(SPLITS)
SPLIT_POINTS = tuple(int(v) for v in np.cumsum(SPLITS)[:-1])


def rms_norm_2(x, g):
    xf = x.astype(jnp.float32)
    y = xf * lax.rsqrt(jnp.mean(xf * xf, axis=-1, keepdims=True) + EPS)
    return (y * g.astype(jnp.float32)).astype(x.dtype)

def rope_partial(x, pos, rot_dim):
    half = rot_dim // 2
    inv = ROPE_THETA ** (-jnp.arange(half, dtype=jnp.float32) / half)
    ang = pos.astype(jnp.float32)[..., None] * inv
    cos = jnp.cos(ang)[:, :, None, :]
    sin = jnp.sin(ang)[:, :, None, :]
    x1 = x[..., :half].astype(jnp.float32)
    x2 = x[..., half:rot_dim].astype(jnp.float32)
    rot = jnp.concatenate([x1 * cos - x2 * sin, x2 * cos + x1 * sin], axis=-1)
    return jnp.concatenate([rot.astype(x.dtype), x[..., rot_dim:]], axis=-1)

def pool_mixer(u, w_pool, pool_scale):
    B, S, _ = u.shape
    ug = u.reshape(B, S, N_POOL_GROUPS, POOL_GROUP)
    cs = jnp.cumsum(ug.astype(jnp.float32), axis=1)
    t = jnp.arange(S)
    outs = []
    for g, w in enumerate(POOL_WINDOWS):
        c = cs[:, :, g]
        lagged = jnp.pad(c, ((0, 0), (w, 0), (0, 0)))[:, :S]
        cnt = jnp.minimum(t + 1, w).astype(jnp.float32)[None, :, None]
        outs.append((c - lagged) / cnt - ug[:, :, g].astype(jnp.float32))
    d = jnp.stack(outs, axis=2).astype(u.dtype)
    y = jnp.einsum('bsgc,gcd->bsgd', d, w_pool)
    return y.reshape(B, S, POOL_WIDTH) * pool_scale

def dsa_attention(q, k, v, iq, ik, iw, topk):
    B, S = q.shape[0], q.shape[1]
    n_blocks = S // Q_BLOCK_2
    key_chunk = jnp.arange(S) // CHUNK
    ik32 = ik.astype(jnp.float32)

    def block(i):
        start = i * Q_BLOCK_2
        qb = lax.dynamic_slice_in_dim(q, start, Q_BLOCK_2, axis=1)
        iqb = lax.dynamic_slice_in_dim(iq, start, Q_BLOCK_2, axis=1).astype(jnp.float32)
        iwb = lax.dynamic_slice_in_dim(iw, start, Q_BLOCK_2, axis=1).astype(jnp.float32)
        q_chunk = (start + jnp.arange(Q_BLOCK_2)) // CHUNK
        allowed = key_chunk[None, :] <= q_chunk[:, None]
        logits = jnp.einsum('bqhd,bsd->bqhs', iqb, ik32) * (IDX_DIM ** -0.5)
        score = jnp.einsum('bqh,bqhs->bqs', iwb, jax.nn.relu(logits))
        score = jnp.where(allowed[None], score, -jnp.inf)
        top_val, top_idx = lax.top_k(score, topk)
        valid = jnp.isfinite(top_val)
        kg = jax.vmap(lambda kk, idx: kk[idx])(k, top_idx)
        vg = jax.vmap(lambda vv, idx: vv[idx])(v, top_idx)
        s = jnp.einsum('bqhd,bqkhd->bqhk', qb.astype(jnp.float32), kg.astype(jnp.float32)) * (HEAD_DIM ** -0.5)
        s = jnp.where(valid[:, :, None, :], s, -jnp.inf)
        p = jax.nn.softmax(s, axis=-1)
        o = jnp.einsum('bqhk,bqkhd->bqhd', p, vg.astype(jnp.float32))
        return o.astype(q.dtype)

    out = lax.map(block, jnp.arange(n_blocks))
    return jnp.transpose(out, (1, 0, 2, 3, 4)).reshape(B, S, N_HEADS * HEAD_DIM)

def second_inputs(seed: int = 0) -> dict:
    key = jax.random.key(seed)
    ks = jax.random.split(key, 12)
    f32 = jnp.float32
    def gain(k):
        return 1.0 + 0.02 * jax.random.normal(k, (DEPTH, D_MODEL), f32)
    x = jax.random.normal(ks[0], (BATCH, SEQ, D_MODEL), f32)
    positions = jnp.broadcast_to(jnp.arange(SEQ, dtype=jnp.int32)[None, :], (BATCH, SEQ)).astype(jnp.int32)
    return {
        "x": x,
        "positions": positions,
        "g_pre_mix": gain(ks[1]),
        "w_in": jax.random.normal(ks[2], (DEPTH, D_MODEL, IN_WIDTH_2), f32) * D_MODEL ** -0.5,
        "w_pool": jax.random.normal(ks[3], (DEPTH, N_POOL_GROUPS, POOL_GROUP, POOL_GROUP), f32) * POOL_GROUP ** -0.5,
        "pool_scale": 1.0 + 0.02 * jax.random.normal(ks[4], (DEPTH, POOL_WIDTH), f32),
        "w_out": jax.random.normal(ks[5], (DEPTH, D_MODEL, D_MODEL), f32) * D_MODEL ** -0.5,
        "g_post_mix": gain(ks[6]),
        "g_pre_ffn": gain(ks[7]),
        "w_ff1": jax.random.normal(ks[8], (DEPTH, D_MODEL, D_FF_2), f32) * D_MODEL ** -0.5,
        "w_ff2": jax.random.normal(ks[9], (DEPTH, D_FF_2, D_MODEL), f32) * D_FF_2 ** -0.5,
        "g_post_ffn": gain(ks[10]),
    }

def second_block(x, positions, g_pre_mix, w_in, w_pool, pool_scale, w_out, g_post_mix,
              g_pre_ffn, w_ff1, w_ff2, g_post_ffn):
    B, S, _ = x.shape
    topk = min(TOPK_MAX, S // 4)
    for l in range(DEPTH):
        h = rms_norm_2(x, g_pre_mix[l])
        proj = h @ w_in[l]
        u_pool, q, k, v, iq, ik, iw = jnp.split(proj, SPLIT_POINTS, axis=-1)
        q = rope_partial(q.reshape(B, S, N_HEADS, HEAD_DIM), positions, ROPE_DIM)
        k = rope_partial(k.reshape(B, S, N_HEADS, HEAD_DIM), positions, ROPE_DIM)
        v = v.reshape(B, S, N_HEADS, HEAD_DIM)
        iq = rope_partial(iq.reshape(B, S, IDX_HEADS, IDX_DIM), positions, IDX_ROPE_DIM)
        ik = rope_partial(ik[:, :, None, :], positions, IDX_ROPE_DIM)[:, :, 0, :]
        iw = iw * (IDX_HEADS ** -0.5)
        a_out = pool_mixer(u_pool, w_pool[l], pool_scale[l])
        b_out = dsa_attention(q, k, v, iq, ik, iw, topk)
        mix = jnp.concatenate([a_out, b_out], axis=-1) @ w_out[l]
        x = x + rms_norm_2(mix, g_post_mix[l])
        h = rms_norm_2(x, g_pre_ffn[l])
        f = jnp.square(jax.nn.relu(h @ w_ff1[l])) @ w_ff2[l]
        x = x + rms_norm_2(f, g_post_ffn[l])
    return x


def setup_inputs(seed=0):
    out = dict(first_inputs(seed))
    for name, value in second_inputs(seed + 1).items():
        if name != "x":
            out[name + "_2"] = value
    return out


def reference(
    x, mem, ffn1_pre_g, ffn1_w_gate, ffn1_w_up, ffn1_w_down, ffn1_post_g, mix_pre_g, w_in,
    cmp_pe, cmp_w1, cmp_w2, nsa_out_g, ret_gn_g, w_out, mix_post_g, xa_pre_g, xa_mem_g, xa_wq,
    xa_wk, xa_wv, xa_wo, xa_post_g, ffn2_pre_g, ffn2_w_gate, ffn2_w_up, ffn2_w_down,
    ffn2_post_g, positions_2, g_pre_mix_2, w_in_2, w_pool_2, pool_scale_2, w_out_2,
    g_post_mix_2, g_pre_ffn_2, w_ff1_2, w_ff2_2, g_post_ffn_2,
):
    x = first_block(
        x, mem, ffn1_pre_g, ffn1_w_gate, ffn1_w_up, ffn1_w_down, ffn1_post_g, mix_pre_g, w_in,
        cmp_pe, cmp_w1, cmp_w2, nsa_out_g, ret_gn_g, w_out, mix_post_g, xa_pre_g, xa_mem_g,
        xa_wq, xa_wk, xa_wv, xa_wo, xa_post_g, ffn2_pre_g, ffn2_w_gate, ffn2_w_up, ffn2_w_down,
        ffn2_post_g,
    )
    return second_block(
        x, positions_2, g_pre_mix_2, w_in_2, w_pool_2, pool_scale_2, w_out_2, g_post_mix_2,
        g_pre_ffn_2, w_ff1_2, w_ff2_2, g_post_ffn_2,
    )


_drawn_inputs = setup_inputs


def setup_inputs(seed=0):
    import zlib

    import numpy as np

    out = dict(_drawn_inputs(seed))
    spreads = {}
    factors = {'ffn1_post_g': 2.892,
     'ret_gn_g': 3.911,
     'xa_pre_g': 2.73,
     'ffn2_pre_g': 3.61,
     'ffn2_post_g': 4.885,
     'g_pre_mix_2': 3.092,
     'pool_scale_2': 5.69,
     'g_post_mix_2': 4.824,
     'g_pre_ffn_2': 4.545,
     'g_post_ffn_2': 5.03}
    for name, (base, spread) in spreads.items():
        noise = np.random.default_rng([zlib.crc32(name.encode()), seed]).standard_normal(out[name].shape)
        drawn = base * np.exp(spread * noise) if base else spread * noise
        out[name] = __import__('jax').numpy.asarray(drawn.astype(out[name].dtype))
    for name, factor in factors.items():
        out[name] = (out[name] * factor).astype(out[name].dtype)
    return out
```

```python
from contextlib import ExitStack

import numpy as np

import concourse.bass as bass
from concourse import mybir

F32 = mybir.dt.float32
F32R = mybir.dt.float32r
I32 = mybir.dt.int32
ALU = mybir.AluOpType
ACT = mybir.ActivationFunctionType
AX = mybir.AxisListType

T = 256
DM = 1024
EPS = 1e-6
BIG = 1e32
NEG = -1e30
TAKEN = -3.0e38
TWO_PI = 6.283185307179586
PI_A = 6.28125
PI_B = 0.0019340515136718750
PI_C = TWO_PI - PI_A - PI_B
ROUND = 12582912.0
SLOPES = [2.0 ** -(h + 1) for h in range(8)]
POOL_WINDOWS = (2, 4, 8, 16)

NRAW = 5
NSPLIT = 3
AHEAD = 2
NG = 2
NREG = 11200


class Engine:

    def __init__(self, sem, chained=False):
        self.sem = sem
        self.chained = chained
        self.n = 0
        self.steps = []
        self.met = {}

    def wait(self, marks):
        for m in marks:
            if m is None:
                continue
            if isinstance(m, list):
                self.wait(m)
                continue
            sem, value = m
            if self.met.get(sem.name, 0) < value:
                self.met[sem.name] = value
                self.steps.append((0, sem, value))

    def add(self, fn, marks, counted=True):
        self.wait(marks)
        if self.chained and self.n:
            self.wait([(self.sem, self.n)])
        if counted:
            self.n += 1
        self.steps.append((1 if counted else 2, fn, None))
        return (self.sem, self.n) if counted else None

    def load(self, fn, marks, sem, value):
        self.wait(marks)
        self.steps.append((3, fn, sem))
        return (sem, value)

    def play(self, e):
        for kind, a, b in self.steps:
            if kind == 0:
                e.wait_ge(a, b)
            elif kind == 1:
                a(e).then_inc(self.sem, 1)
            elif kind == 2:
                a(e)
            else:
                a(e).then_inc(b, 16)


def constants():
    t = np.arange(T)
    dist = (t[:, None] - t[None, :]).astype(np.float64)
    d = np.where(dist >= 0, -dist, -BIG)
    alibi = np.concatenate([d[0:128, 0:128], d[128:256, :]], axis=1)
    ident = np.eye(128)
    start = np.arange(15) * 16
    mid = start + 15.5
    end = start + 31
    ok = end[None, :] <= t[:, None]
    cb = -np.asarray(SLOPES)[None, :, None] * (t[:, None, None] - mid[None, None, :])
    cb = np.where(ok[:, None, :], cb, NEG)
    cb = cb.reshape(2, 128, 120).transpose(1, 0, 2).reshape(128, 240)
    cm = np.broadcast_to(ok[:, None, :], (T, 8, 15)).astype(np.float64)
    cm = cm.reshape(2, 128, 120).transpose(1, 0, 2).reshape(128, 240)
    chunk = t // 64
    ch = np.where(chunk[None, :] <= chunk[:, None], 0.0, NEG)
    ch = np.concatenate([ch[0:128, 0:128], ch[128:256, :]], axis=1)
    half = np.arange(8)
    inv = np.broadcast_to((500000.0 ** (-half.astype(np.float32) / np.float32(8))).astype(np.float64), (128, 8))
    small = np.concatenate([ident, alibi, cb, cm, ch, inv], axis=1).astype(np.float32)
    dec = []
    for h in range(4):
        g = 1.0 - 2.0 ** (-5.0 - h)
        w = np.where(dist >= 0, g ** np.maximum(dist, 0.0), 0.0) * 128.0 ** -0.5
        dec.append(w.T)
    dec = np.stack(dec)
    decay = np.concatenate(
        [dec[:, 0:128, :].transpose(1, 0, 2).reshape(128, 1024), dec[:, 128:256, 128:256].transpose(1, 0, 2).reshape(128, 512)],
        axis=1,
    ).astype(np.float32)
    pm = []
    for w in POOL_WINDOWS:
        cnt = np.minimum(t + 1, w)[:, None]
        m = np.where((dist >= 0) & (dist < w), 1.0 / cnt, 0.0) - np.eye(T)
        m = m.T
        pm.append(np.concatenate([m[0:128, :], m[128:256, 128:256]], axis=1))
    pool = np.concatenate(pm, axis=1).astype(np.float32)
    return {"c_small": small, "c_decay": decay, "c_pool": pool}


def build(nc, A, out):
    ctx = ExitStack()
    with ctx:
        def sb(name, n, dt=F32):
            return ctx.enter_context(nc.sbuf_tensor(name, [128, n], dt))

        def sem(name):
            return ctx.enter_context(nc.semaphore(name))

        RAW = sb("raw", NRAW * 2048)
        WHI = sb("whi", NSPLIT * 2048, F32R)
        WLO = sb("wlo", NSPLIT * 2048, F32R)
        X = sb("xs", 2 * DM)
        GV = sb("gv", NG * DM)
        XN = sb("xn", 2 * DM)
        AHI = sb("ahi", 8 * T, F32R)
        ALO = sb("alo", 8 * T, F32R)
        MHI = sb("mhi", 8 * T, F32R)
        MLO = sb("mlo", 8 * T, F32R)
        HHI = sb("hhi", 2 * 512, F32R)
        HLO = sb("hlo", 2 * 512, F32R)
        CS = sb("cs", 992)
        W2C = sb("w2c", 512)
        SM = sb("sm", 400)
        R = sb("region", NREG)
        PS = ctx.enter_context(nc.psum_tensor("ps", [128, 8, 512], F32))

        pe, sp = Engine(sem("s_pe")), Engine(sem("s_sp"))
        act, dve, pool = [Engine(sem(n), True) for n in ("s_act", "s_dve", "s_pool")]
        s_raw = [sem(f"s_raw{i}") for i in range(NRAW)]
        s_gv = [sem(f"s_gv{i}") for i in range(NG)]
        s_c = [sem(f"s_c{i}") for i in range(8)]
        s_aux = [sem(f"s_aux{i}") for i in range(2)]
        s_out = sem("s_out")

        def mm(o, l, r, start, stop, w=(), inc=False):
            return pe.add(lambda e: e.matmul(o, l, r, start=start, stop=stop), w, inc)

        def tr(o, i, idn, w=(), inc=False):
            return pe.add(lambda e: e.transpose(o, i, idn), w, inc)

        def av(o, i, f, w=(), **kw):
            return act.add(lambda e: e.activation(o, i, f, **kw), w)

        def tt(o, a, b, op, w=(), q=None):
            return (q or dve).add(lambda e: e.tensor_tensor(o, a, b, op), w)

        def ts(o, a, s1, s2, op0, op1=ALU.bypass, w=(), q=None):
            return (q or dve).add(lambda e: e.tensor_scalar(o, a, s1, s2, op0, op1), w)

        def stt(o, a, s, b, op0, op1, w=()):
            return dve.add(lambda e: e.scalar_tensor_tensor(o, a, s, b, op0, op1), w)

        def cp(o, a, w=(), q=None):
            return (q or dve).add(lambda e: e.tensor_copy(o, a), w)

        def red(o, a, op, w=()):
            return dve.add(lambda e: e.tensor_reduce(o, a, AX.X, op), w)

        def rcp(o, a, w=()):
            return dve.add(lambda e: e.reciprocal(o, a), w)

        def bc(ap, n):
            return ap.unsqueeze(len(ap.shape)).broadcast_to(list(ap.shape) + [n])

        def bm(ap, n):
            return ap.unsqueeze(1).broadcast_to([ap.shape[0], n, ap.shape[1]])

        IDN = CS[:, 0:128]
        ALIBI = CS[:, 128:512]
        CB = CS[:, 512:752].rearrange("p (m c) -> p m c", m=2)
        CM = CS[:, 752:992].rearrange("p (m c) -> p m c", m=2)
        small = sb("small2", 392 + 8 + 32)
        CH = small[:, 0:384]
        INV = small[:, 384:392]
        COS = small[:, 400:416]
        SIN = small[:, 416:432]
        PET = SM[:, 0:64]
        PSC = SM[:, 64:72]
        st = SM[:, 80:400]
        ssq = st[:, 0:2]
        var = st[:, 2:4]
        rstd = st[:, 4:6]
        mx = st[:, 8:16]
        nb = st[:, 16:24]
        den = st[:, 24:32]
        coef = st[:, 32:40]
        gates = st[:, 40:88].rearrange("p (m c) -> p m c", m=2)
        top8 = st[:, 88:96]
        rsum = st[:, 96:100]
        rvar = st[:, 100:104]
        iw = st[:, 104:120].rearrange("p (m c) -> p m c", m=2)
        kcT = st[:, 120:136]
        vcR = st[:, 136:264]
        posf = st[:, 264:266]
        ang = st[:, 268:284]
        nrd = st[:, 284:300]
        MHALF = st[:, 300:304]
        PSC2 = sb("pc", 384)
        PC = PSC2[:, 0:256]
        SC = PSC2[:, 256:384]

        BF = [None] * 8

        items = []

        def item(tag, src, k, n, split=True):
            items.append((tag, src, k, n, split))

        def rows(w, k0, k1, c0, c1):
            return w[k0 * 128:k1 * 128, c0:c1].rearrange("(k p) n -> p k n", p=128)

        def plan():
            for l in range(2):
                for f in ("ffn1", "ffn2"):
                    g, u, d = A[f + "_w_gate"][l, :, :], A[f + "_w_up"][l, :, :], A[f + "_w_down"][l, :, :]
                    for j in range(12):
                        if j < 11:
                            item("gate", rows(g, 0, 8, 256 * j, 256 * j + 256), 8, 256)
                            item("up", rows(u, 0, 8, 256 * j, 256 * j + 256), 8, 256)
                        if j >= 1:
                            item("down", rows(d, 2 * j - 2, 2 * j, 0, 1024), 2, 1024)
                    if f == "ffn2":
                        continue
                    wi = A["w_in"][l, :, :]
                    for c in range(2):
                        item("q_r", rows(wi, 0, 8, 1304 + 256 * c, 1560 + 256 * c), 8, 256)
                    for c in range(2):
                        item("k_r", rows(wi, 0, 8, 1816 + 256 * c, 2072 + 256 * c), 8, 256)
                    for c in range(2):
                        item("v_r", rows(wi, 4 * c, 4 * c + 4, 2328, 2840), 4, 512)
                    for c in range(2):
                        item("g_r", rows(wi, 4 * c, 4 * c + 4, 2840, 3352), 4, 512)
                    item("cmp", rows(wi, 0, 8, 512, 768), 8, 256)
                    for kv in range(2):
                        for c in range(2):
                            item("w1", rows(A["cmp_w1"][l, kv, :, :], 8 * c, 8 * c + 8, 0, 256), 8, 256, False)
                    for c in range(2):
                        item("q_n", (wi, c), 8, 256)
                    item("slc", rows(wi, 0, 8, 768, 1024), 8, 256)
                    item("win", rows(wi, 0, 8, 1024, 1280), 8, 256)
                    item("gates", rows(wi, 0, 8, 1280, 1408), 8, 128)
                    for c in range(4):
                        item("w_out", rows(A["w_out"][l, :, :], 2 * c, 2 * c + 2, 0, 1024), 2, 1024)
                    for c in range(4):
                        item("wk", rows(A["xa_wk"][l, :, :], 0, 8, 256 * c, 256 * c + 256), 8, 256)
                    for c in range(4):
                        item("wv", rows(A["xa_wv"][l, :, :], 2 * c, 2 * c + 2, 0, 1024), 2, 1024)
                    for c in range(4):
                        item("wq", rows(A["xa_wq"][l, :, :], 0, 8, 256 * c, 256 * c + 256), 8, 256)
                    for c in range(4):
                        item("wo", rows(A["xa_wo"][l, :, :], 2 * c, 2 * c + 2, 0, 1024), 2, 1024)
            for l in range(2):
                wi = A["w_in_2"][l, :, :]
                for c in range(2):
                    for s in range(2):
                        item("iq", rows(wi, 4 * s, 4 * s + 4, 2048 + 292 * c, 2340 + 292 * c), 4, 292)
                for tag, c0 in (("q", 512), ("k", 1024), ("v", 1536), ("u", 0)):
                    for s in range(2):
                        item(tag, rows(wi, 4 * s, 4 * s + 4, c0, c0 + 512), 4, 512)
                for c in range(4):
                    item("w_out2", rows(A["w_out_2"][l, :, :], 2 * c, 2 * c + 2, 0, 1024), 2, 1024)
                f1, f2 = A["w_ff1_2"][l, :, :], A["w_ff2_2"][l, :, :]
                for j in range(17):
                    if j < 16:
                        item("ff1", rows(f1, 0, 8, 256 * j, 256 * j + 256), 8, 256)
                    if j >= 1:
                        item("ff2", rows(f2, 2 * j - 2, 2 * j, 0, 1024), 2, 1024)

        plan()
        nsplit = [0]
        slot_of = {}
        landed = {}
        halves = {}
        free_raw = {}
        free_half = {}
        at = {"load": 0, "split": 0, "use": 0}

        def load_more():
            while at["load"] < len(items):
                i = at["load"]
                if i >= NRAW and i - NRAW not in free_raw:
                    return
                tag, src, k, n, _ = items[i]
                dst = RAW[:, (i % NRAW) * 2048:(i % NRAW) * 2048 + k * n].rearrange("p (k n) -> p k n", k=k)
                w = free_raw.get(i - NRAW)
                if tag == "q_n":
                    wi, c = src
                    for f in range(2):
                        for a in range(2):
                            c0 = 256 * a + 128 * c + 64 * f
                            o = dst[:, :, f * 128 + a * 64:f * 128 + a * 64 + 64]
                            s = rows(wi, 0, 8, c0, c0 + 64)
                            sp.load(lambda e, o=o, s=s: e.dma_start(o, s), [w], s_raw[i % NRAW], 0)
                    uses[i % NRAW] += 64
                else:
                    sp.load(lambda e, o=dst, s=src: e.dma_start(o, s), [w], s_raw[i % NRAW], 0)
                    uses[i % NRAW] += 16
                landed[i] = (s_raw[i % NRAW], uses[i % NRAW])
                at["load"] += 1

        uses = [0] * NRAW

        def split_more(upto):
            while at["split"] <= min(upto, len(items) - 1):
                i = at["split"]
                tag, src, k, n, split = items[i]
                load_more()
                if split:
                    s = nsplit[0]
                    nsplit[0] += 1
                    slot_of[i] = s
                    b = (s % NSPLIT) * 2048
                    raw = RAW[:, (i % NRAW) * 2048:(i % NRAW) * 2048 + k * n]
                    hi, lo = WHI[:, b:b + k * n], WLO[:, b:b + k * n]
                    used = free_half.get(s - NSPLIT)
                    a = av(hi, raw, ACT.Copy, [landed[i], used])
                    d = tt(lo, raw, hi.bitcast(F32), ALU.subtract, [landed[i], a])
                    halves[i] = d
                    free_raw[i] = [d]
                at["split"] += 1
            load_more()

        def take(tag):
            i = at["use"]
            assert items[i][0] == tag, (items[i][0], tag)
            at["use"] += 1
            split_more(i + AHEAD)
            k, n = items[i][2:4]
            b = (slot_of[i] % NSPLIT) * 2048
            view = [x[:, b:b + k * n].rearrange("p (k n) -> p k n", k=k) for x in (WHI, WLO)]
            return view[0], view[1], halves[i], i

        def take_raw(tag):
            i = at["use"]
            assert items[i][0] == tag, (items[i][0], tag)
            at["use"] += 1
            split_more(i + AHEAD)
            k, n = items[i][2:4]
            return RAW[:, (i % NRAW) * 2048:(i % NRAW) * 2048 + k * n].rearrange("p (k n) -> p k n", k=k), landed[i], i

        def done(i, mark):
            if i in slot_of:
                free_half[slot_of[i]] = mark
            else:
                free_raw[i] = [mark]
                load_more()

        gains = []

        def gain_plan():
            def g(v):
                gains.append([(0, v)])
            for l in range(2):
                for n in ("ffn1_pre_g", "ffn1_post_g", "mix_pre_g"):
                    g(A[n][l, :])
                gains.append([(0, A["ret_gn_g"][l, :]), (512, A["nsa_out_g"][l, :])])
                for n in ("xa_mem_g", "mix_post_g", "xa_pre_g", "xa_post_g", "ffn2_pre_g", "ffn2_post_g"):
                    g(A[n][l, :])
            for l in range(2):
                for n in ("g_pre_mix_2", "g_post_mix_2", "g_pre_ffn_2", "g_post_ffn_2"):
                    g(A[n][l, :])

        gain_plan()
        gst = {"load": 0, "use": 0}
        guse = [0] * NG
        gfree = {}
        gmark = {}

        def gain_loads():
            while gst["load"] < len(gains):
                i = gst["load"]
                if i >= NG and i - NG not in gfree:
                    return
                s = i % NG
                for off, v in gains[i]:
                    n = v.shape[0]
                    o = GV[:, s * DM + off:s * DM + off + n]
                    pool.load(lambda e, o=o, v=v: e.dma_start(o, v.partition_broadcast(128)), [gfree.get(i - NG)], s_gv[s], 0)
                    guse[s] += 16
                gmark[i] = (s_gv[s], guse[s])
                gst["load"] += 1

        def gain():
            i = gst["use"]
            gst["use"] += 1
            return GV[:, (i % NG) * DM:(i % NG) * DM + DM], gmark[i], i

        def gain_done(i, mark):
            gfree[i] = mark
            gain_loads()

        def cload(k, o, s):
            return act.load(lambda e: e.dma_start(o, s), [], s_c[k], 16)

        c_small = A["c_small"]
        m_cs = cload(0, CS[:, 0:992], c_small[:, 0:992])
        m_x = [cload(1 + m, X[:, m * DM:(m + 1) * DM], A["x"][0, m * 128:(m + 1) * 128, :]) for m in range(2)]
        m_cs2 = cload(3, small[:, 0:392], c_small[:, 992:1384])
        pe_in = R[0:64, 0:128]
        ps_in = R[0:8, 128:256]
        pos_in = R[0:2, 256:384].bitcast(I32)
        pos_row = R[0:2, 384:512]
        m_pe = cload(4, pe_in, A["cmp_pe"].rearrange("l c (k a) d -> (l c k) (a d)", a=2))
        m_ps = cload(5, ps_in, A["pool_scale_2"].rearrange("l (g p) -> (l g) p", p=128))
        m_w2 = cload(6, W2C[:, :].rearrange("p (a d) -> p a d", d=64),
                     A["cmp_w2"].rearrange("l c (k p) d -> p (l c k) d", p=128))
        m_pos = cload(7, pos_in, A["positions_2"].rearrange("o (m p) -> (o m) p", p=128))
        gain_loads()
        m_mh = pool.add(lambda e: e.memset(MHALF, -0.5), [])
        m_sc = pool.add(lambda e: e.memset(SC[:, :], 0.0), [])
        m_pc = pool.add(lambda e: e.memset(PC[:, :], 0.0), [])
        t1 = tr(PS[:, 0, 0:64], pe_in, CS[0:64, 0:64], [m_pe, m_cs])
        t1 = tr(PS[:, 0, 64:72], ps_in, CS[0:8, 0:8], [m_ps], True)
        m_pet = cp(SM[:, 0:72], PS[:, 0, 0:72], [t1])
        BF[0] = m_pet
        p = cp(pos_row, pos_in, [m_pos])
        t1 = tr(PS[:, 0, 128:130], pos_row, CS[0:2, 0:2], [p, m_pet], True)
        p = cp(posf, PS[:, 0, 128:130], [t1])
        BF[0] = p
        for shift, dst in ((0.0, SIN), (0.25 * TWO_PI, COS)):
            a = tt(ang.rearrange("p (m j) -> p m j", m=2), bc(posf, 8), bm(INV, 2), ALU.mult, [p, m_cs2])
            a = ts(nrd, ang, 1.0 / TWO_PI, shift / TWO_PI, ALU.mult, ALU.add, [a])
            a = ts(nrd, nrd, ROUND, None, ALU.add, w=[a])
            a = ts(nrd, nrd, ROUND, None, ALU.subtract, w=[a])
            for c in (PI_A, PI_B, PI_C):
                a = stt(ang, nrd, -c, ang, ALU.mult, ALU.add, [a])
            a = ts(ang, ang, shift, None, ALU.add, w=[a])
            a = ts(ang, ang, 3.14159, -3.14159, ALU.min, ALU.max, [a])
            p = av(dst, ang, ACT.Sin, [a])
        m_rope = p

        S_EPS = EPS

        def to_halves(m, half, hi_t, lo_t, src_mark, old, bank, cols=None):
            for k in range(4):
                c = m * DM + (half * 4 + k) * 128
                t = tr(PS[:, bank, k * 128:(k + 1) * 128], XN[:, c:c + 128], IDN, [src_mark, BF[bank]], k == 3)
            v = PS[:, bank, :].rearrange("p (k n) -> p k n", k=4)
            hi = hi_t[:, :].rearrange("p (k n) -> p k n", k=8)[:, half * 4:half * 4 + 4, m * 128:(m + 1) * 128]
            lo = lo_t[:, :].rearrange("p (k n) -> p k n", k=8)[:, half * 4:half * 4 + 4, m * 128:(m + 1) * 128]
            a = av(hi, v, ACT.Copy, [t, old])
            d = tt(lo, v, hi.bitcast(F32), ALU.subtract, [a, t, old])
            BF[bank] = d
            return d, t

        free = {"xn": None, "a": None, "m": None, "h0": None, "h1": None}

        def mean_root(dst, s, n, w, times=1.0):
            k = times ** -2.0
            a = ts(var[:, 0:1] if dst.shape[1] == 1 else rvar, s, k / n, k * S_EPS, ALU.mult, ALU.add, [w])
            n1 = dst.shape[1]
            return tt(dst, var[:, 0:1] if n1 == 1 else rvar, MHALF[:, 0:n1], ALU.pow, w=[a, m_mh], q=pool)

        def pre_norm(xm):
            g, mg, gi = gain()
            last = []
            for m in range(2):
                xs = X[:, m * DM:(m + 1) * DM]
                xn = XN[:, m * DM:(m + 1) * DM]
                a = av(xn, xs, ACT.Square, [xm[m], free["xn"]], accum_out=ssq[:, m:m + 1])
                r = mean_root(rstd[:, m:m + 1], ssq[:, m:m + 1], DM, a)
                d = stt(xn, xs, rstd[:, m:m + 1], g, ALU.mult, ALU.mult, [r, mg])
                for half in range(2):
                    h, t = to_halves(m, half, AHI, ALO, d, free["a"], 2 * m + half)
                    last.append(h)
            gain_done(gi, d)
            free["xn"] = t
            return last

        def post_norm(y, times):
            g, mg, gi = gain()
            out = []
            for m in range(2):
                ym = PS[:, 4 + 2 * m:6 + 2 * m, :].rearrange("p b n -> p (b n)")
                xs = X[:, m * DM:(m + 1) * DM]
                xn = XN[:, m * DM:(m + 1) * DM]
                a = av(xn, ym, ACT.Square, [y, free["xn"]], accum_out=ssq[:, m:m + 1])
                r = mean_root(rstd[:, m:m + 1], ssq[:, m:m + 1], DM, a, times)
                d = stt(xn, ym, rstd[:, m:m + 1], g, ALU.mult, ALU.mult, [r, mg])
                BF[4 + 2 * m] = BF[5 + 2 * m] = d
                x = tt(xs, xs, xn, ALU.add, [d])
                out.append(x)
            gain_done(gi, d)
            free["xn"] = x
            return out

        def up(tag, bank, rdy, hi_t=AHI, lo_t=ALO, n=2):
            hi, lo, mark, i = take(tag)
            xh = hi_t[:, :].rearrange("p (k n) -> p k n", k=8)
            xl = lo_t[:, :].rearrange("p (k n) -> p k n", k=8)
            for f in range(n):
                o = PS[:, bank, f * 256:(f + 1) * 256]
                for k in range(8):
                    for s, (w, x) in enumerate(((hi, xh), (hi, xl), (lo, xh))):
                        t = mm(o, w[:, k, f * 128:(f + 1) * 128], x[:, k, :], k == 0 and s == 0, k == 7 and s == 2,
                               [mark, rdy, BF[bank]], k == 7 and s == 2)
            done(i, t)
            return t

        def down(tag, c, nk, rdy, ah, al, banks=4):
            hi, lo, mark, i = take(tag)
            for kk in range(2):
                k = 2 * c + kk
                for m in range(2):
                    lh = ah[:, kk, m * 128:(m + 1) * 128]
                    ll = al[:, kk, m * 128:(m + 1) * 128]
                    for n in range(2):
                        b = banks + 2 * m + n
                        o = PS[:, b, :]
                        for s, (x, w) in enumerate(((lh, hi), (lh, lo), (ll, hi))):
                            end = k == nk - 1 and s == 2
                            t = mm(o, x, w[:, kk, n * 512:(n + 1) * 512], k == 0 and s == 0, end,
                                   [mark, rdy, BF[b]], kk == 1 and m == 1 and n == 1 and s == 2)
            done(i, t)
            return t

        def natural(tag, banks, rdy, n=512):
            xh = AHI[:, :].rearrange("p (k n) -> p k n", k=8)
            xl = ALO[:, :].rearrange("p (k n) -> p k n", k=8)
            for c in range(2):
                hi, lo, mark, i = take(tag)
                for kk in range(4):
                    k = 4 * c + kk
                    for m in range(2):
                        ms = slice(m * 128, (m + 1) * 128)
                        for s, (x, w) in enumerate(((xh, hi), (xh, lo), (xl, hi))):
                            t = mm(PS[:, banks[m], 0:n], x[:, k, ms], w[:, kk, :], k == 0 and s == 0, k == 7 and s == 2,
                                   [mark, rdy, BF[banks[m]]], kk == 3 and m == 1 and s == 2)
                done(i, t)
            return t

        def eight(tag, bh, bl, rdy):
            hv = bh[:, :].rearrange("p (k n) -> p k n", k=8)
            lv = bl[:, :].rearrange("p (k n) -> p k n", k=8)
            for c in range(4):
                t = down(tag, c, 8, rdy, hv[:, 2 * c:2 * c + 2, :], lv[:, 2 * c:2 * c + 2, :])
            return t

        def ffn(xm, kind):
            rdy = pre_norm(xm)
            nj = 16 if kind == "relu2" else 11
            H = R[:, 0:1024].rearrange("p (s n) -> p s n", s=2)
            G = R[:, 1024:3072].rearrange("p (s n) -> p s n", s=4)
            hm = {}
            for j in range(nj + 1):
                if j < nj:
                    s = j % 2
                    hf, hh, hl = H[:, s, :], HHI[:, s * 512:(s + 1) * 512], HLO[:, s * 512:(s + 1) * 512]
                    if kind == "relu2":
                        b = j % 4
                        tg = up("ff1", b, rdy)
                        a = av(G[:, s, :], PS[:, b, :], ACT.Relu, [tg, free["region"]])
                        d = tt(hf, G[:, s, :], PS[:, b, :], ALU.mult, [a])
                        BF[b] = d
                    else:
                        bg, bu = 2 * s, 2 * s + 1
                        tg = up("gate", bg, rdy)
                        tu = up("up", bu, rdy)
                        a = av(G[:, s, :], PS[:, bg, :], ACT.Tanh, [tg, free["region"]], scale=0.5)
                        d = stt(G[:, 2 + s, :], G[:, s, :], 1.0, PS[:, bg, :], ALU.add, ALU.mult, [a])
                        BF[bg] = d
                        d = stt(hf, G[:, 2 + s, :], 0.5, PS[:, bu, :], ALU.mult, ALU.mult, [d, tu])
                        BF[bu] = d
                    a = av(hh, hf, ACT.Copy, [d, free["h%d" % s]])
                    hm[j] = tt(hl, hf, hh.bitcast(F32), ALU.subtract, [a], q=pool)
                    rdy_last = tg
                if j >= 1:
                    s = (j - 1) % 2
                    ah, al = [x[:, s * 512:(s + 1) * 512].rearrange("p (k n) -> p k n", k=2) for x in (HHI, HLO)]
                    t = down("ff2" if kind == "relu2" else "down", j - 1, 2 * nj, hm[j - 1], ah, al)
                    free["h%d" % s] = t
            free["a"] = t
            free["region"] = [hm[nj - 1], d, a]
            return post_norm(t, 1.0 if kind == "relu2" else 0.5)

        def soft(P, h, w, scale, ready, old):
            d = red(mx[:, 0:h], P, ALU.max, [ready])
            d = ts(nb[:, 0:h], mx[:, 0:h], -scale, None, ALU.mult, w=[d])
            for i in range(h):
                a = av(P[:, i, :], P[:, i, :], ACT.Exp, [d, old], scale=scale, bias=nb[:, i:i + 1],
                       accum_out=den[:, i:i + 1])
            return a

        def turn(P, PT, h, nk, ready, old, banks=(0, 1)):
            n = 0
            outs = []
            blocks = [(i, k) for i in range(h) for k in range(nk)]
            for b0 in range(0, len(blocks), 4):
                bank = banks[n % len(banks)]
                part = blocks[b0:b0 + 4]
                for j, (i, k) in enumerate(part):
                    t = tr(PS[:, bank, j * 128:(j + 1) * 128], P[:, i, k * 128:(k + 1) * 128], IDN,
                           [ready, BF[bank]], j == len(part) - 1)
                dst = PT[:, b0 * 128:(b0 + len(part)) * 128]
                if n % 2:
                    e = cp(dst, PS[:, bank, 0:len(part) * 128], [t, old])
                else:
                    e = av(dst, PS[:, bank, 0:len(part) * 128], ACT.Copy, [t, old])
                BF[bank] = e
                outs.append(e)
                n += 1
            return outs, t

        def hybrid(l, xm):
            rdy = pre_norm(xm)
            fr = free["region"]
            o = [0]

            def reg(n):
                o[0] += n
                assert o[0] <= NREG
                return R[:, o[0] - n:o[0]]

            qT = reg(1024).rearrange("p (k n) -> p k n", k=4)
            kvT = reg(1024)
            vN = reg(512).rearrange("p (m n) -> p m n", m=2)
            gT = reg(256)
            Bk = reg(960)
            sT = reg(128)
            sTh = reg(128)
            base = o[0]
            qrT = reg(1024).rearrange("p (k n) -> p k n", k=4)
            krT = reg(1024).rearrange("p (k n) -> p k n", k=4)
            ST = reg(1536)
            DEC = reg(1536)
            vr = reg(1024)
            gr = reg(1024)
            P_ = R[:, base:base + 2048].rearrange("p (h n) -> p h n", h=8)
            PT_ = R[:, base + 2048:base + 4096]
            O_ = R[:, base + 4096:base + 5120]
            aux = pool.load(lambda e: e.dma_start(DEC, A["c_decay"]), [fr], s_aux[0], 0)
            auxn[0] += 16
            aux = (s_aux[0], auxn[0])

            for c in range(2):
                t = up("q_r", c, rdy)
                BF[c] = av(qrT[:, 2 * c:2 * c + 2, :].rearrange("p k n -> p (k n)"), PS[:, c, :], ACT.Copy, [t, fr])
            for c in range(2):
                t = up("k_r", 2 + c, rdy)
                BF[2 + c] = av(krT[:, 2 * c:2 * c + 2, :].rearrange("p k n -> p (k n)"), PS[:, 2 + c, :], ACT.Copy, [t, fr])
            qk = BF[3]
            t = natural("v_r", (0, 1), rdy)
            for m in range(2):
                BF[m] = av(vr[:, m * 512:(m + 1) * 512], PS[:, m, :], ACT.Copy, [t, fr])
            vrm = BF[1]
            for h in range(4):
                b = 4 + h // 2
                t = mm(PS[:, b, (h % 2) * 256:(h % 2) * 256 + 256], krT[:, h, 0:128], qrT[:, h, :], True, True, [qk, BF[b]])
                t = mm(PS[:, 6, h * 128:(h + 1) * 128], krT[:, h, 128:256], qrT[:, h, 128:256], True, True, [BF[6]], h == 3)
            t_s = t
            t = natural("g_r", (2, 3), rdy)
            d = tt(ST[:, 0:1024], PS[:, 4:6, :].rearrange("p b n -> p (b n)"), DEC[:, 0:1024], ALU.mult, [t_s, aux, fr])
            BF[4] = BF[5] = d
            d = tt(ST[:, 1024:1536], PS[:, 6, :], DEC[:, 1024:1536], ALU.mult, [t_s])
            BF[6] = d
            st_m = d
            for m in range(2):
                a = av(gr[:, m * 512:(m + 1) * 512], PS[:, 2 + m, :], ACT.Tanh, [t, fr], scale=0.5)
                g2 = stt(gr[:, m * 512:(m + 1) * 512], gr[:, m * 512:(m + 1) * 512], 1.0, PS[:, 2 + m, :], ALU.add, ALU.mult, [a])
                BF[2 + m] = g2
            gg, mg, gi = gain()
            s0 = ST[:, 0:1024].rearrange("p (h n) -> p h n", h=4)
            s1 = ST[:, 1024:1536].rearrange("p (h n) -> p h n", h=4)
            t_o = []
            for m in range(2):
                for h in range(4):
                    ob = PS[:, 4 + m, h * 128:(h + 1) * 128]
                    if m == 0:
                        t = mm(ob, s0[:, h, 0:128], vr[:, h * 128:(h + 1) * 128], True, True, [st_m, vrm, BF[4]], h == 3)
                    else:
                        mm(ob, s0[:, h, 128:256], vr[:, h * 128:(h + 1) * 128], True, False, [st_m, vrm, BF[5]])
                        t = mm(ob, s1[:, h, :], vr[:, 512 + h * 128:512 + (h + 1) * 128], False, True, [], h == 3)
                t_o.append(t)
            ret_pe = t
            for m in range(2):
                ob = PS[:, 4 + m, :].rearrange("p (h n) -> p h n", h=4)
                xn = XN[:, m * DM + 512:(m + 1) * DM]
                xv = xn.rearrange("p (h n) -> p h n", h=4)
                sq = XN[:, m * DM:m * DM + 512]
                d = red(rsum, ob, ALU.add, [t_o[m]])
                d = ts(rsum, rsum, 1.0 / 128, None, ALU.mult, w=[d])
                c = tt(xv, ob, bc(rsum, 128), ALU.subtract, [d, free["xn"]])
                BF[4 + m] = c
                a = av(sq, xn, ACT.Square, [c])
                d = red(rsum, sq.rearrange("p (h n) -> p h n", h=4), ALU.add, [a])
                d = mean_root(rsum, rsum, 128, d, 0.5)
                d = tt(xv, xv, bc(rsum, 128), ALU.mult, [d])
                q = tt(xn, xn, gg[:, 0:512], ALU.mult, [d, mg], q=pool)
                q = tt(xn, xn, gr[:, m * 512:(m + 1) * 512], ALU.mult, [q, g2], q=pool)
            ret_m = q

            t = up("cmp", 0, rdy)
            ck, cv = 0, 1
            out_c = []
            fb = None
            for kv in range(2):
                Bv = Bk[:, kv * 480:(kv + 1) * 480].rearrange("p (k g n) -> p k g n", k=16, g=2)
                for g in range(2):
                    for par in range(2):
                        src = PS[g * 64:(g + 1) * 64, 0, kv * 256:(kv + 1) * 256]
                        parts = []
                        for hi16 in range(2):
                            v = src.rearrange("p (n k a) -> p k n a", k=8, a=2)[:, :, hi16:hi16 + 15, par]
                            pt = PET[par * 64:(par + 1) * 64, (l * 2 + kv) * 16 + hi16 * 8:(l * 2 + kv) * 16 + hi16 * 8 + 8]
                            d = tt(Bv[par * 64:(par + 1) * 64, hi16 * 8:hi16 * 8 + 8, g, :], v, bc(pt, 15), ALU.add, [t, m_pet, fr])
            BF[0] = d
            bm_ = d
            for kv in range(2):
                Bv = Bk[:, kv * 480:(kv + 1) * 480].rearrange("p (k c) -> p k c", k=16)
                for c in range(2):
                    raw, mark, i = take_raw("w1")
                    for ht in range(2):
                        for kk in range(8):
                            k = 8 * c + kk
                            t = mm(PS[:, 2 + ht, kv * 32:kv * 32 + 30], raw[:, kk, ht * 128:(ht + 1) * 128], Bv[:, k, :],
                                   k == 0, k == 15, [mark, bm_, BF[2 + ht]], ht == 1 and kk == 7)
                    done(i, t)
                sv = sT[:, kv * 60:kv * 60 + 60].rearrange("p (h c) -> p h c", h=2)
                pv = PS[:, 2:4, kv * 32:kv * 32 + 30]
                a = av(sv, pv, ACT.Tanh, [t, fr], scale=0.5)
                scv = SC[:, :].rearrange("p (h g n) -> p h g n", h=2, g=2)[:, :, :, 0:15] if kv else None
                if kv == 0:
                    skv = sTh[:, 0:60].rearrange("p (h c) -> p h c", h=2)
                    d = stt(skv, sv, 1.0, pv, ALU.add, ALU.mult, [a])
                    BF[2] = BF[3] = d
                    for g in range(2):
                        for ht in range(2):
                            t = mm(PS[g * 64:(g + 1) * 64, 1, 0:15], W2C[:, ((l * 2) * 2 + ht) * 64:((l * 2) * 2 + ht + 1) * 64],
                                   skv[:, ht, g * 15:(g + 1) * 15], ht == 0, ht == 1, [d, m_w2, BF[1]], g == 1 and ht == 1)
                    k_m = ts(kcT[:, 0:15], PS[:, 1, 0:15], 0.5, None, ALU.mult, w=[t, free_kc[0]])
                    BF[1] = k_m
                else:
                    d = stt(scw(sTh[:, 64:124]), scw(sT[:, 60:120]), 1.0, pv, ALU.add, ALU.mult, [a])
                    BF[2] = BF[3] = d
                    d = cp(scv, sTh[:, 64:124].rearrange("p (h g n) -> p h g n", h=2, g=2), [d, m_sc, free_kc[0]])
                    for i4 in range(4):
                        for g in range(2):
                            for ht in range(2):
                                t = mm(PS[32 * i4:32 * i4 + 32, 1, g * 64:(g + 1) * 64], SC[:, (ht * 2 + g) * 32:(ht * 2 + g + 1) * 32],
                                       W2C[:, ((l * 2 + 1) * 2 + ht) * 64:((l * 2 + 1) * 2 + ht + 1) * 64], ht == 0, ht == 1,
                                       [d, m_w2, BF[1]], i4 == 3 and g == 1 and ht == 1)
                    v_m = ts(vcR, PS[:, 1, 0:128], 0.5, None, ALU.mult, w=[t])
                    BF[1] = v_m

            for c in range(2):
                b = 2 + c
                t = up("q_n", b, rdy)
                BF[b] = av(qT[:, 2 * c:2 * c + 2, :].rearrange("p k n -> p (k n)"), PS[:, b, :], ACT.Copy, [t, fr])
            q_m = BF[3]
            for c, tag in enumerate(("slc", "win")):
                t = up(tag, c, rdy)
                BF[c] = cp(kvT[:, c * 512:(c + 1) * 512], PS[:, c, :], [t, fr])
            kv_m = BF[1]
            t = up("gates", 2, rdy, n=1)
            a = av(gT[0:24, :], PS[0:24, 2, 0:256], ACT.Tanh, [t, fr], scale=0.5)
            BF[2] = a
            free["a"] = t
            for m in range(2):
                t = tr(PS[:, 3, m * 24:m * 24 + 24], gT[0:24, m * 128:(m + 1) * 128], CS[0:24, 0:24], [a, BF[3]], m == 1)
            g_m = ts(gates.rearrange("p m c -> p (m c)"), PS[:, 3, 0:48], 1.0, 0.5, ALU.add, ALU.mult, [t])
            BF[3] = g_m
            kvv = kvT.rearrange("p (b n) -> p b n", b=4)
            for br in range(2):
                for m in range(2):
                    t = tr(PS[:, 2, (m * 2 + br) * 128:(m * 2 + br + 1) * 128], kvv[:, 2 * br + 1, m * 128:(m + 1) * 128], IDN,
                           [kv_m, BF[2]], br == 1 and m == 1)
            BF[2] = vn_m = cp(vN.rearrange("p m n -> p (m n)"), PS[:, 2, :], [t, fr])

            old_p = [ret_pe]
            old_t = [ret_m]
            fin = []
            for m in range(2):
                gm = gates[:, m, :].rearrange("p (h b) -> p h b", b=3)
                om = O_[:, m * 512:(m + 1) * 512].rearrange("p (h d) -> p h d", h=8)
                for h in range(8):
                    r = slice(0, 64) if h < 4 else slice(64, 128)
                    t = mm(PS[:, 4 + h // 4, (h % 4) * 16:(h % 4) * 16 + 15], qT[r, h % 4, m * 128:(m + 1) * 128], kcT[r, 0:15],
                           True, True, [q_m, k_m, BF[4], BF[5]], h == 7)
                pc = PC[:, :].rearrange("p (h n) -> p h n", h=8)[:, :, 0:15]
                cbv = CB[:, m, :].rearrange("p (h n) -> p h n", h=8)
                cmv = CM[:, m, :].rearrange("p (h n) -> p h n", h=8)
                for g in range(2):
                    d = stt(pc[:, 4 * g:4 * g + 4, :], PS[:, 4 + g, 0:64].rearrange("p (h n) -> p h n", h=4)[:, :, 0:15], 0.125,
                            cbv[:, 4 * g:4 * g + 4, :], ALU.mult, ALU.add, [t, m_pc, free_kc[0]])
                BF[4] = BF[5] = d
                d = red(mx, pc, ALU.max, [d])
                d = tt(pc, pc, bc(mx, 15), ALU.subtract, [d])
                a = av(pc, pc, ACT.Exp, [d])
                d = tt(pc, pc, cmv, ALU.mult, [a])
                d = red(den, pc, ALU.add, [d])
                d2 = ts(den, den, 1e-30, None, ALU.max, w=[d])
                d2 = rcp(den, den, [d2])
                d2 = tt(coef, den, gm[:, :, 0], ALU.mult, [d2, g_m])
                for g in range(2):
                    t = tr(PS[:, 6, g * 128:(g + 1) * 128], PC[:, g * 128:(g + 1) * 128], IDN, [d, BF[6]], g == 1)
                free_kc[0] = t
                pct = cp(gT, PS[:, 6, 0:256], [t, old_t])
                BF[6] = pct
                for h in range(8):
                    i4, g = h % 4, h // 4
                    t = mm(PS[:, i4, g * 64:(g + 1) * 64], gT[32 * i4:32 * i4 + 15, g * 128:(g + 1) * 128],
                           vcR[32 * i4:32 * i4 + 15, g * 64:(g + 1) * 64], True, True, [pct, v_m, BF[0], BF[1], BF[2], BF[3]], h == 7)
                old_t = [t]
                for g in range(2):
                    d = tt(om[:, 4 * g:4 * g + 4, :], PS[:, 0:4, g * 64:(g + 1) * 64], bc(coef[:, 4 * g:4 * g + 4], 64), ALU.mult,
                           [t, d2, ret_m])
                BF[0] = BF[1] = BF[2] = BF[3] = d
                nk = m + 1
                for br in range(2):
                    kT = kvv[:, 2 * br, :]
                    for h in range(8):
                        r = slice(0, 64) if h < 4 else slice(64, 128)
                        b = 4 + h // 2
                        t = mm(PS[:, b, (h % 2) * 256:(h % 2) * 256 + nk * 128], qT[r, h % 4, m * 128:(m + 1) * 128],
                               kT[r, 0:nk * 128], True, True, [q_m, kv_m, BF[b]], h == 7)
                    al = ALIBI[:, 0:128] if m == 0 else ALIBI[:, 128:384]
                    for h in range(8):
                        b = 4 + h // 2
                        d = stt(P_[:, h, 0:nk * 128], al, 8.0 * SLOPES[h], PS[:, b, (h % 2) * 256:(h % 2) * 256 + nk * 128],
                                ALU.mult, ALU.add, [t, old_p])
                        if h % 2:
                            BF[b] = d
                    a = soft(P_[:, :, 0:nk * 128], 8, nk * 128, 0.125, d, None)
                    d2 = rcp(den, den, [a])
                    d2 = tt(coef, den, gm[:, :, 1 + br], ALU.mult, [d2])
                    evs, t = turn(P_[:, :, 0:nk * 128], PT_, 8, nk, a, old_t + [ret_m])
                    old_p = [t]
                    for h in range(8):
                        g = h // 4
                        for k in range(nk):
                            t = mm(PS[:, 2, h * 64:(h + 1) * 64], PT_[:, (h * nk + k) * 128:(h * nk + k + 1) * 128],
                                   vN[:, k, br * 128 + g * 64:br * 128 + (g + 1) * 64], k == 0, k == nk - 1,
                                   [evs, vn_m, BF[2]], h == 7 and k == nk - 1)
                    old_t = [t]
                    tmp = R[:, base + 5120 + m * 512:base + 5632 + m * 512].rearrange("p (h d) -> p h d", h=8)
                    d = tt(tmp, PS[:, 2, :].rearrange("p (h d) -> p h d", h=8), bc(coef, 64), ALU.mult, [t, d2, ret_m])
                    BF[2] = d
                    d = tt(om, om, tmp, ALU.add, [d])
                xn = XN[:, m * DM:m * DM + 512]
                of = O_[:, m * 512:(m + 1) * 512]
                a = av(xn, of, ACT.Square, [d, ret_m], accum_out=ssq[:, m:m + 1])
                r = mean_root(rstd[:, m:m + 1], ssq[:, m:m + 1], 512, a)
                fin.append(stt(xn, of, rstd[:, m:m + 1], gg[:, 512:1024], ALU.mult, ALU.mult, [r]))
            gain_done(gi, fin[1])
            rdy2 = []
            for m in range(2):
                for half in range(2):
                    d, t = to_halves(m, half, AHI, ALO, [fin[m], ret_m], free["a"], 2 * m + half)
                    rdy2.append(d)
            free["xn"] = t
            free["region"] = [t, d, a, old_t, old_p, ret_m]
            y = eight("w_out", AHI, ALO, rdy2)
            free["a"] = y
            return y

        auxn = [0, 0]
        free_kc = [None]

        def scw(ap):
            return ap.rearrange("p (h c) -> p h c", h=2)

        def memory(l, xm_fn):
            fr = free["region"]
            MR = R[:, 6144:8192]
            qT = R[:, 0:2048]
            kT = R[:, 2048:4096]
            V = R[:, 4096:6144]
            P_ = R[:, 6144:8192].rearrange("p (m h n) -> p m h n", m=2, h=4)
            PT_ = R[:, 8192:10240].rearrange("p (k h n) -> p k h n", k=2, h=4)
            MN = R[:, 8192:10240]
            pool.load(lambda e: e.dma_start(MR.rearrange("p (m n) -> p m n", m=2), A["mem"][0, :, :].rearrange("(m p) n -> p m n", p=128)),
                      [fr], s_aux[1], 0)
            auxn[1] += 16
            aux = (s_aux[1], auxn[1])
            g, mg, gi = gain()
            rm = []
            for m in range(2):
                a = av(MN[:, m * DM:(m + 1) * DM], MR[:, m * DM:(m + 1) * DM], ACT.Square, [aux, fr], accum_out=ssq[:, m:m + 1])
                r = mean_root(rstd[:, m:m + 1], ssq[:, m:m + 1], DM, a)
                d = stt(MN[:, m * DM:(m + 1) * DM], MR[:, m * DM:(m + 1) * DM], rstd[:, m:m + 1], g, ALU.mult, ALU.mult, [r, mg])
                for half in range(2):
                    bank = 2 * m + half
                    for k in range(4):
                        c = m * DM + (half * 4 + k) * 128
                        t = tr(PS[:, bank, k * 128:(k + 1) * 128], MN[:, c:c + 128], IDN, [d, BF[bank]], k == 3)
                    v = PS[:, bank, :].rearrange("p (k n) -> p k n", k=4)
                    hi, lo = [x[:, :].rearrange("p (k n) -> p k n", k=8)[:, half * 4:half * 4 + 4, m * 128:(m + 1) * 128] for x in (MHI, MLO)]
                    a = av(hi, v, ACT.Copy, [t, free["m"]])
                    e = tt(lo, v, hi.bitcast(F32), ALU.subtract, [a, free["m"]])
                    BF[bank] = e
                    rm.append(e)
            gain_done(gi, d)
            xm = xm_fn()
            for c in range(4):
                t = up("wk", c, rm, MHI, MLO)
                BF[c] = av(kT[:, c * 512:(c + 1) * 512], PS[:, c, :], ACT.Copy, [t, fr])
            km = BF[3]
            hv = MHI[:, :].rearrange("p (k n) -> p k n", k=8)
            lv = MLO[:, :].rearrange("p (k n) -> p k n", k=8)
            for c in range(4):
                t = down("wv", c, 8, rm, hv[:, 2 * c:2 * c + 2, :], lv[:, 2 * c:2 * c + 2, :], 0)
            free["m"] = t
            for m in range(2):
                e = av(V[:, m * DM:(m + 1) * DM], PS[:, 2 * m:2 * m + 2, :].rearrange("p b n -> p (b n)"), ACT.Copy, [t, fr])
                BF[2 * m] = BF[2 * m + 1] = e
            vm = e
            rdy = pre_norm(xm)
            for c in range(4):
                t = up("wq", c, rdy)
                BF[c] = av(qT[:, c * 512:(c + 1) * 512], PS[:, c, :], ACT.Copy, [t, fr])
            qm = BF[3]
            free["a"] = t
            evs = []
            qv = qT.rearrange("p (k n) -> p k n", k=8)
            kv = kT.rearrange("p (k n) -> p k n", k=8)
            ts_ = []
            for m in range(2):
                for h in range(4):
                    b = 4 + 2 * m + h // 2
                    for k in range(2):
                        t = mm(PS[:, b, (h % 2) * 256:(h % 2) * 256 + 256], qv[:, 2 * h + k, m * 128:(m + 1) * 128],
                               kv[:, 2 * h + k, :], k == 0, k == 1, [qm, km, BF[b]], h == 3 and k == 1)
                ts_.append(t)
            for m in range(2):
                S = PS[:, 4 + 2 * m:6 + 2 * m, :].rearrange("p b (h n) -> p (b h) n", h=2)
                o = 4 * m
                d = red(mx[:, o:o + 4], S, ALU.max, [ts_[m]])
                d = ts(nb[:, o:o + 4], mx[:, o:o + 4], -0.0625, None, ALU.mult, w=[d])
                for h in range(4):
                    a = av(P_[:, m, h, :], S[:, h, :], ACT.Exp, [d, rm], scale=0.0625, bias=nb[:, o + h:o + h + 1],
                           accum_out=den[:, o + h:o + h + 1])
                BF[4 + 2 * m] = BF[5 + 2 * m] = a
                d = rcp(den[:, o:o + 4], den[:, o:o + 4], [a])
                for h in range(4):
                    d = ts(P_[:, m, h, :], P_[:, m, h, :], den[:, o + h:o + h + 1], None, ALU.mult, w=[d])
                    bank = h
                    for k in range(2):
                        t = tr(PS[:, bank, (m * 2 + k) * 128:(m * 2 + k + 1) * 128], P_[:, m, h, k * 128:(k + 1) * 128], IDN,
                               [d, BF[bank]], k == 1)
                    dst = PT_[:, :, h, m * 128:(m + 1) * 128]
                    src = PS[:, bank, m * 256:m * 256 + 256].rearrange("p (k n) -> p k n", k=2)
                    if h % 2:
                        e = cp(dst, src, [t])
                    else:
                        e = av(dst, src, ACT.Copy, [t])
                    BF[bank] = e
                    evs.append(e)
            rdy = []
            for c in range(4):
                for j in range(2):
                    f = 2 * c + j
                    for k in range(2):
                        t = mm(PS[:, 4 + c, j * 256:(j + 1) * 256], V[:, k * DM + f * 128:k * DM + (f + 1) * 128],
                               PT_[:, k, c, :], k == 0, k == 1, [evs, vm, BF[4 + c]], j == 1 and k == 1)
                hi, lo = AHI[:, c * 512:(c + 1) * 512], ALO[:, c * 512:(c + 1) * 512]
                a = av(hi, PS[:, 4 + c, :], ACT.Copy, [t, free["a"]])
                e = tt(lo, PS[:, 4 + c, :], hi.bitcast(F32), ALU.subtract, [a, free["a"]])
                BF[4 + c] = e
                rdy.append(e)
            free["region"] = [t, e]
            y = eight("wo", AHI, ALO, rdy)
            free["a"] = y
            return post_norm(y, 1.0)

        def sparse(l, xm):
            rdy = pre_norm(xm)
            fr = free["region"]
            qn = R[:, 0:1024]
            kn = R[:, 1024:2048]
            iqn = R[:, 2048:3072]
            P_ = R[:, 0:2048].rearrange("p (h n) -> p h n", h=8)
            V = R[:, 3072:4096]
            U = R[:, 4096:5120]
            ikn = R[:, 5120:5376]
            ikT = R[:, 5376:5632]
            iqT = R[:, 5632:6656].rearrange("p (k n) -> p k n", k=4)
            qT = R[:, 6656:7680].rearrange("p (k n) -> p k n", k=4)
            kT = R[:, 7680:8704].rearrange("p (k n) -> p k n", k=4)
            PT_ = R[:, 8704:10752]
            SCO = R[:, 10752:11136]
            PM = R[:, 8704:10240]
            WP = R[:, 10240:10752]
            pool.load(lambda e: e.dma_start(PM, A["c_pool"]), [fr], s_aux[0], 0)
            pool.load(lambda e: e.dma_start(WP.rearrange("p (g n) -> p g n", g=4), A["w_pool_2"][l, :, :, :].rearrange("g p n -> p g n")),
                      [fr], s_aux[0], 0)
            auxn[0] += 32
            aux = (s_aux[0], auxn[0])
            cosv = COS.rearrange("p (m j) -> p m j", m=2)
            sinv = SIN.rearrange("p (m j) -> p m j", m=2)
            rt = [XN[:, i * 128:(i + 1) * 128] for i in range(4)]

            def rope(v, h, w):
                def sh(i):
                    return rt[i][:, 0:2 * h * 8].rearrange("p (m h j) -> p m h j", m=2, h=h)
                c = cosv.unsqueeze(2).broadcast_to([128, 2, h, 8])
                s = sinv.unsqueeze(2).broadcast_to([128, 2, h, 8])
                x1, x2 = v[:, :, :, 0:8], v[:, :, :, 8:16]
                ws = [w, m_rope, free["xn"], rope_last[0]]
                tt(sh(0), x1, c, ALU.mult, ws, q=pool)
                tt(sh(1), x2, s, ALU.mult, q=pool)
                tt(sh(2), x2, c, ALU.mult, q=pool)
                p = tt(sh(3), x1, s, ALU.mult, q=pool)
                tt(x1, sh(0), sh(1), ALU.subtract, [p], q=pool)
                p = tt(x2, sh(2), sh(3), ALU.add, q=pool)
                rope_last[0] = p
                return p

            def heads_T(src, dst, ready, bank, w):
                outs = []
                for m in range(2):
                    b = bank + m
                    for k in range(4):
                        t = tr(PS[:, b, k * 128:(k + 1) * 128], src[:, m * 512 + k * 128:m * 512 + (k + 1) * 128], IDN,
                               [ready, BF[b]], k == 3)
                    e = av(dst[:, :, m * 128:(m + 1) * 128], PS[:, b, :].rearrange("p (k n) -> p k n", k=4), ACT.Copy, [t, w])
                    BF[b] = e
                    outs.append(e)
                return outs, t

            t = natural("iq", (0, 1), rdy, 292)
            for m in range(2):
                e = av(iqn[:, m * 512:m * 512 + 292], PS[:, m, 0:292], ACT.Copy, [t, fr])
                BF[m] = e
            t = natural("iq", (2, 3), rdy, 292)
            for m in range(2):
                a = av(iqn[:, m * 512 + 292:(m + 1) * 512], PS[:, 2 + m, 0:220], ACT.Copy, [t, fr])
                d = cp(ikn[:, m * 128:m * 128 + 64], PS[:, 2 + m, 220:284], [a, t, fr])
                e = av(iw[:, m, :], PS[:, 2 + m, 284:292], ACT.Copy, [d], scale=8.0 ** -0.5)
                BF[2 + m] = e
            iqm = rope(iqn.rearrange("p (m h d) -> p m h d", m=2, h=8), 8, e)
            ikv = ikn.rearrange("p (m h d) -> p m h d", m=2, h=2)
            ikm = rope(ikv[:, :, 0:1, :], 1, d)
            ikm = pool.add(lambda e: e.tensor_copy(ikv[:, :, 1, :], ikv[:, :, 0, :]), [ikm])
            t = natural("q", (0, 1), rdy)
            for m in range(2):
                e = av(qn[:, m * 512:(m + 1) * 512], PS[:, m, :], ACT.Copy, [t, fr])
                BF[m] = e
            qm = rope(qn.rearrange("p (m h d) -> p m h d", m=2, h=8), 8, e)
            for m in range(2):
                t = tr(PS[:, 4, m * 128:(m + 1) * 128], ikn[:, m * 128:(m + 1) * 128], IDN, [ikm, BF[4]], m == 1)
            BF[4] = ikt = cp(ikT, PS[:, 4, 0:256], [t, fr])
            iqt, t_i = heads_T(iqn, iqT, iqm, 5, fr)
            t = natural("k", (2, 3), rdy)
            for m in range(2):
                e = av(kn[:, m * 512:(m + 1) * 512], PS[:, 2 + m, :], ACT.Copy, [t, fr])
                BF[2 + m] = e
            km = rope(kn.rearrange("p (m h d) -> p m h d", m=2, h=8), 8, e)
            rope_pool = km

            RL = R[:, 0:2048]
            qt, t_q = heads_T(qn, qT, qm, 0, fr)
            kt_, t_k = heads_T(kn, kT, km, 0, fr)
            sel = []
            relu_free = [t_q, t_k]

            def bank_of(h):
                return 4 + h % 4, (h // 4) * 256

            t_sc = None
            sco = []
            rl = RL.rearrange("p (b a n) -> p b a n", b=4, a=2)
            for m in range(2):
                w = 128 * (m + 1)
                for h in range(8):
                    b, c = bank_of(h)
                    r = slice((h % 2) * 64, (h % 2) * 64 + 64)
                    t = mm(PS[:, b, c:c + w], iqT[r, h // 2, m * 128:(m + 1) * 128], ikT[r, 0:w], True, True,
                           [ikt, iqt, BF[b]], h == 7)
                a = av(rl[:, :, :, 0:w], PS[:, 4:8, :].rearrange("p b (a n) -> p b a n", a=2)[:, :, :, 0:w], ACT.Relu,
                       [t, relu_free], scale=0.125)
                for b in range(4, 8):
                    BF[b] = a
                s = SCO[:, m * 128:m * 128 + w]
                ch = CH[:, 0:128] if m == 0 else CH[:, 128:384]
                d = None
                for h in range(8):
                    rh = rl[:, h % 4, h // 4, 0:w]
                    if h == 0:
                        d = ts(s, rh, iw[:, m, 0:1], None, ALU.mult, w=[a, fr])
                    else:
                        d = stt(s, rh, iw[:, m, h:h + 1], s, ALU.mult, ALU.add, [d])
                relu_free = [d]
                d = tt(s, s, ch, ALU.add, [d])
                for _ in range(8):
                    d = dve.add(lambda e, s=s: e.max(top8, s), [d])
                    d = dve.add(lambda e, s=s: e.match_replace(s, top8, s, TAKEN), [d])
                d = ts(PSC2[:, m * 128:m * 128 + w], s, TAKEN, NEG, ALU.not_equal, ALU.mult, [d])
                sel.append(d)
                if m == 0:
                    t = natural("v", (2, 3), rdy)
                    for mm_ in range(2):
                        e = av(V[:, mm_ * 512:(mm_ + 1) * 512], PS[:, 2 + mm_, :], ACT.Copy, [t, fr])
                        BF[2 + mm_] = e
                    vm = e
                    t = natural("u", (0, 1), rdy)
                    free["a"] = t
                    for mm_ in range(2):
                        e = av(U[:, mm_ * 512:(mm_ + 1) * 512], PS[:, mm_, :], ACT.Copy, [t, fr])
                        BF[mm_] = e
                    um = e
            DT = R[:, 2048:3072]
            dts = []
            for g in range(4):
                b = g // 2
                o = PS[:, b, (g % 2) * 256:(g % 2) * 256 + 256]
                mm(o, U[:, g * 128:(g + 1) * 128], PM[:, g * 384:g * 384 + 256], True, False, [um, aux, BF[b]])
                t = mm(o[:, 128:256], U[:, 512 + g * 128:512 + (g + 1) * 128], PM[:, g * 384 + 256:g * 384 + 384], False, True, [], g % 2 == 1)
                if g % 2:
                    e = av(DT[:, (g // 2) * 512:(g // 2) * 512 + 512], PS[:, b, :], ACT.Copy, [t, t_i, fr])
                    BF[b] = e
            for g in range(4):
                b = 2 + g // 2
                t = mm(PS[:, b, (g % 2) * 256:(g % 2) * 256 + 256], WP[:, g * 128:(g + 1) * 128], DT[:, g * 256:(g + 1) * 256],
                       True, True, [e, BF[b]], True)
            t_pool = t
            rdy2 = []
            for g in range(4):
                b = 2 + g // 2
                y = PS[:, b, (g % 2) * 256:(g % 2) * 256 + 256]
                hi, lo = AHI[:, g * 256:(g + 1) * 256], ALO[:, g * 256:(g + 1) * 256]
                sc = PSC[:, l * 4 + g:l * 4 + g + 1]
                if g == 0:
                    for g_ in range(4):
                        a = av(AHI[:, g_ * 256:(g_ + 1) * 256], PS[:, 2 + g_ // 2, (g_ % 2) * 256:(g_ % 2) * 256 + 256], ACT.Copy,
                               [t, free["a"], m_pet], scale=PSC[:, l * 4 + g_:l * 4 + g_ + 1])
                d = stt(lo, y, sc, hi.bitcast(F32), ALU.mult, ALU.subtract, [a, free["a"]])
                BF[b] = d
                rdy2.append(d)

            old_p = [relu_free, t_q, t_k]
            old_t = [t_pool]
            p4 = R[:, 0:2048].rearrange("p (b a n) -> p b a n", b=4, a=2)
            for m in range(2):
                nk = m + 1
                w = nk * 128
                for h in range(8):
                    b, c = bank_of(h)
                    r = slice((h % 2) * 64, (h % 2) * 64 + 64)
                    t = mm(PS[:, b, c:c + w], qT[r, h // 2, m * 128:(m + 1) * 128], kT[r, h // 2, 0:w], True, True,
                           [qt, kt_, BF[b]], h == 7)
                bi = PSC2[:, m * 128:m * 128 + w]
                for a_ in range(2):
                    sv = PS[:, 4:8, a_ * 256:a_ * 256 + w]
                    d = stt(p4[:, :, a_, 0:w], sv, 0.125, bm(bi, 4), ALU.mult, ALU.add, [t, sel[m], old_p])
                for b in range(4, 8):
                    BF[b] = d
                a = soft(P_[:, :, 0:w], 8, w, 1.0, d, None)
                d2 = rcp(den, den, [a])
                evs, t = turn(P_[:, :, 0:w], PT_, 8, nk, a, old_t)
                old_p = [t]
                for i in range(8):
                    h = (i % 2) * 4 + i // 2
                    for k in range(nk):
                        t = mm(PS[:, 2, i * 64:(i + 1) * 64], PT_[:, (i * nk + k) * 128:(i * nk + k + 1) * 128],
                               V[:, k * 512 + h * 64:k * 512 + (h + 1) * 64], k == 0, k == nk - 1, [evs, vm, BF[2]],
                               i == 7 and k == nk - 1)
                old_t = [t]
                xo = XN[:, m * DM + 512:(m + 1) * DM].rearrange("p (a b d) -> p b a d", a=2, b=4)
                ov = PS[:, 2, :].rearrange("p (b a d) -> p b a d", b=4, a=2)
                dn = den.rearrange("p (b a) -> p b a", a=2)
                for a_ in range(2):
                    d = tt(xo[:, :, a_, :], ov[:, :, a_, :], bc(dn[:, :, a_], 64), ALU.mult, [t, d2, rope_pool, free["xn"]])
                BF[2] = d
                e, t = to_halves(m, 1, AHI, ALO, d, free["a"], m)
                rdy2.append(e)
            free["xn"] = t
            free["region"] = [old_t, old_p, t, e, a, t_pool]
            y = eight("w_out2", AHI, ALO, rdy2)
            free["a"] = y
            return post_norm(y, 1.0)

        rope_last = [None]
        free["region"] = [m_rope, m_pet, (pe.sem, pe.n)]
        xm = m_x
        for l in range(2):
            xm = ffn(xm, "swiglu")
            y = hybrid(l, xm)
            xm = memory(l, lambda: post_norm(y, 1.0))
            xm = ffn(xm, "swiglu")
        for l in range(2):
            xm = sparse(l, xm)
            xm = ffn(xm, "relu2")
        for m in range(2):
            sp.load(lambda e, m=m: e.dma_start(out[0, m * 128:(m + 1) * 128, :], X[:, m * DM:(m + 1) * DM]), [xm[m]], s_out, 0)
        sp.wait([(s_out, 32)])
        assert at["use"] == len(items) and gst["use"] == len(gains)

        block = ctx.enter_context(nc.Block())

        @block.sync
        def _(e):
            sp.play(e)

        @block.gpsimd
        def _(e):
            pool.play(e)

        @block.scalar
        def _(e):
            act.play(e)

        @block.vector
        def _(e):
            dve.play(e)

        @block.tensor
        def _(e):
            pe.play(e)


_INS = ["x", "mem", "ffn1_pre_g", "ffn1_w_gate", "ffn1_w_up", "ffn1_w_down", "ffn1_post_g", "mix_pre_g", "w_in",
        "cmp_pe", "cmp_w1", "cmp_w2", "nsa_out_g", "ret_gn_g", "w_out", "mix_post_g", "xa_pre_g", "xa_mem_g", "xa_wq",
        "xa_wk", "xa_wv", "xa_wo", "xa_post_g", "ffn2_pre_g", "ffn2_w_gate", "ffn2_w_up", "ffn2_w_down",
        "ffn2_post_g", "positions_2", "g_pre_mix_2", "w_in_2", "w_pool_2", "pool_scale_2", "w_out_2",
        "g_post_mix_2", "g_pre_ffn_2", "w_ff1_2", "w_ff2_2", "g_post_ffn_2"]


def kernel(**inputs):
    import concourse.bacc as bacc
    from concourse.bass_utils import run_bass_kernel_spmd as run

    nc = bacc.Bacc("TRN2", target_bir_lowering=False, num_devices=1)
    arrays, aps = {}, {}
    for name in _INS:
        arrays[name] = np.ascontiguousarray(inputs[name])
    arrays.update(constants())
    for name, a in arrays.items():
        aps[name] = nc.dram_tensor(name, a.shape, mybir.dt.from_np(a.dtype), kind="ExternalInput").ap()
    out = nc.dram_tensor("out", (1, T, DM), F32, kind="ExternalOutput").ap()
    build(nc, aps, out)
    r = run(nc, [arrays], core_ids=[0])
    return r.results[0]["out"]
```

```python
from contextlib import ExitStack

import numpy as np

import concourse.bass as bass
from concourse import mybir

F32 = mybir.dt.float32
F32R = mybir.dt.float32r
I32 = mybir.dt.int32
ALU = mybir.AluOpType
ACT = mybir.ActivationFunctionType
AX = mybir.AxisListType

T = 256
DM = 1024
EPS = 1e-6
BIG = 1e32
NEG = -1e30
TAKEN = -3.0e38
TWO_PI = 6.283185307179586
PI_A = 6.28125
PI_B = 0.0019340515136718750
PI_C = TWO_PI - PI_A - PI_B
ROUND = 12582912.0
SLOPES = [2.0 ** -(h + 1) for h in range(8)]
POOL_WINDOWS = (2, 4, 8, 16)

NRAW = 4
NSPLIT = 3
AHEAD = 2
NG = 2
NREG = 13248


class Engine:

    def __init__(self, sem, chained=False):
        self.sem = sem
        self.chained = chained
        self.n = 0
        self.steps = []
        self.met = {}

    def wait(self, marks):
        for m in marks:
            if m is None:
                continue
            if isinstance(m, list):
                self.wait(m)
                continue
            sem, value = m
            if self.met.get(sem.name, 0) < value:
                self.met[sem.name] = value
                self.steps.append((0, sem, value))

    def add(self, fn, marks, counted=True):
        self.wait(marks)
        if self.chained and self.n:
            self.wait([(self.sem, self.n)])
        if counted:
            self.n += 1
        self.steps.append((1 if counted else 2, fn, None))
        return (self.sem, self.n) if counted else None

    def load(self, fn, marks, sem, value):
        self.wait(marks)
        self.steps.append((3, fn, sem))
        return (sem, value)

    def play(self, e):
        for kind, a, b in self.steps:
            if kind == 0:
                e.wait_ge(a, b)
            elif kind == 1:
                a(e).then_inc(self.sem, 1)
            elif kind == 2:
                a(e)
            else:
                a(e).then_inc(b, 16)


def constants():
    t = np.arange(T)
    dist = (t[:, None] - t[None, :]).astype(np.float64)
    d = np.where(dist >= 0, -dist, -BIG)
    alibi = np.concatenate([d[0:128, 0:128], d[128:256, :]], axis=1)
    ident = np.eye(128)
    start = np.arange(15) * 16
    mid = start + 15.5
    end = start + 31
    ok = end[None, :] <= t[:, None]
    cb = -np.asarray(SLOPES)[None, :, None] * (t[:, None, None] - mid[None, None, :])
    cb = np.where(ok[:, None, :], cb, NEG)
    cb = cb.reshape(2, 128, 120).transpose(1, 0, 2).reshape(128, 240)
    cm = np.broadcast_to(ok[:, None, :], (T, 8, 15)).astype(np.float64)
    cm = cm.reshape(2, 128, 120).transpose(1, 0, 2).reshape(128, 240)
    chunk = t // 64
    ch = np.where(chunk[None, :] <= chunk[:, None], 0.0, NEG)
    ch = np.concatenate([ch[0:128, 0:128], ch[128:256, :]], axis=1)
    half = np.arange(8)
    inv = np.broadcast_to((500000.0 ** (-half.astype(np.float32) / np.float32(8))).astype(np.float64), (128, 8))
    small = np.concatenate([ident, alibi, cb, cm, ch, inv], axis=1).astype(np.float32)
    dec = []
    for h in range(4):
        g = 1.0 - 2.0 ** (-5.0 - h)
        w = np.where(dist >= 0, g ** np.maximum(dist, 0.0), 0.0) * 128.0 ** -0.5
        dec.append(w.T)
    dec = np.stack(dec)
    decay = np.concatenate(
        [dec[:, 0:128, :].transpose(1, 0, 2).reshape(128, 1024), dec[:, 128:256, 128:256].transpose(1, 0, 2).reshape(128, 512)],
        axis=1,
    ).astype(np.float32)
    pm = []
    for w in POOL_WINDOWS:
        cnt = np.minimum(t + 1, w)[:, None]
        m = np.where((dist >= 0) & (dist < w), 1.0 / cnt, 0.0) - np.eye(T)
        m = m.T
        pm.append(np.concatenate([m[0:128, :], m[128:256, 128:256]], axis=1))
    pool = np.concatenate(pm, axis=1).astype(np.float32)
    return {"c_small": small, "c_decay": decay, "c_pool": pool}


def build(nc, A, out):
    ctx = ExitStack()
    with ctx:
        def sb(name, n, dt=F32):
            return ctx.enter_context(nc.sbuf_tensor(name, [128, n], dt))

        def sem(name):
            return ctx.enter_context(nc.semaphore(name))

        RAW = sb("raw", NRAW * 2048)
        WHI = sb("whi", NSPLIT * 2048, F32R)
        WLO = sb("wlo", NSPLIT * 2048, F32R)
        X = sb("xs", 2 * DM)
        GV = sb("gv", NG * DM)
        XN = sb("xn", 2 * DM)
        AHI = sb("ahi", 8 * T, F32R)
        ALO = sb("alo", 8 * T, F32R)
        MHI = sb("mhi", 8 * T, F32R)
        MLO = sb("mlo", 8 * T, F32R)
        HHI = sb("hhi", 2 * 512, F32R)
        HLO = sb("hlo", 2 * 512, F32R)
        CS = sb("cs", 992)
        W2C = sb("w2c", 512)
        SM = sb("sm", 400)
        R = sb("region", NREG)
        PS = ctx.enter_context(nc.psum_tensor("ps", [128, 8, 512], F32))

        pe, sp = Engine(sem("s_pe")), Engine(sem("s_sp"))
        act, dve, pool = [Engine(sem(n), True) for n in ("s_act", "s_dve", "s_pool")]
        s_raw = [sem(f"s_raw{i}") for i in range(NRAW)]
        s_gv = [sem(f"s_gv{i}") for i in range(NG)]
        s_c = [sem(f"s_c{i}") for i in range(8)]
        s_aux = [sem(f"s_aux{i}") for i in range(2)]
        s_out = sem("s_out")

        def mm(o, l, r, start, stop, w=(), inc=False):
            return pe.add(lambda e: e.matmul(o, l, r, start=start, stop=stop), w, inc)

        def tr(o, i, idn, w=(), inc=False):
            return pe.add(lambda e: e.transpose(o, i, idn), w, inc)

        def av(o, i, f, w=(), **kw):
            return act.add(lambda e: e.activation(o, i, f, **kw), w)

        def tt(o, a, b, op, w=(), q=None):
            return (q or dve).add(lambda e: e.tensor_tensor(o, a, b, op), w)

        def ts(o, a, s1, s2, op0, op1=ALU.bypass, w=(), q=None):
            return (q or dve).add(lambda e: e.tensor_scalar(o, a, s1, s2, op0, op1), w)

        def stt(o, a, s, b, op0, op1, w=()):
            return dve.add(lambda e: e.scalar_tensor_tensor(o, a, s, b, op0, op1), w)

        def cp(o, a, w=(), q=None):
            return (q or dve).add(lambda e: e.tensor_copy(o, a), w)

        def red(o, a, op, w=()):
            return dve.add(lambda e: e.tensor_reduce(o, a, AX.X, op), w)

        def rcp(o, a, w=()):
            return dve.add(lambda e: e.reciprocal(o, a), w)

        def bc(ap, n):
            return ap.unsqueeze(len(ap.shape)).broadcast_to(list(ap.shape) + [n])

        def bm(ap, n):
            return ap.unsqueeze(1).broadcast_to([ap.shape[0], n, ap.shape[1]])

        IDN = CS[:, 0:128]
        ALIBI = CS[:, 128:512]
        CB = CS[:, 512:752].rearrange("p (m c) -> p m c", m=2)
        CM = CS[:, 752:992].rearrange("p (m c) -> p m c", m=2)
        small = sb("small2", 392 + 8 + 32)
        CH = small[:, 0:384]
        INV = small[:, 384:392]
        COS = small[:, 400:416]
        SIN = small[:, 416:432]
        PET = SM[:, 0:64]
        PSC = SM[:, 64:72]
        st = SM[:, 80:400]
        ssq = st[:, 0:2]
        var = st[:, 2:4]
        rstd = st[:, 4:6]
        mx = st[:, 8:16]
        nb = st[:, 16:24]
        den = st[:, 24:32]
        coef = st[:, 32:40]
        gates = st[:, 40:88].rearrange("p (m c) -> p m c", m=2)
        top8 = st[:, 88:96]
        rsum = st[:, 96:100]
        rvar = st[:, 100:104]
        iw = st[:, 104:120].rearrange("p (m c) -> p m c", m=2)
        kcT = st[:, 120:136]
        vcR = st[:, 136:264]
        posf = st[:, 264:266]
        ang = st[:, 268:284]
        nrd = st[:, 284:300]
        MHALF = st[:, 300:304]
        PSC2 = sb("pc", 384)
        PC = PSC2[:, 0:256]
        SC = PSC2[:, 256:384]

        BF = [None] * 8

        items = []

        def item(tag, src, k, n, split=True):
            items.append((tag, src, k, n, split))

        def rows(w, k0, k1, c0, c1):
            return w[k0 * 128:k1 * 128, c0:c1].rearrange("(k p) n -> p k n", p=128)

        def plan():
            for l in range(2):
                for f in ("ffn1", "ffn2"):
                    g, u, d = A[f + "_w_gate"][l, :, :], A[f + "_w_up"][l, :, :], A[f + "_w_down"][l, :, :]
                    for j in range(12):
                        if j < 11:
                            item("gate", rows(g, 0, 8, 256 * j, 256 * j + 256), 8, 256)
                            item("up", rows(u, 0, 8, 256 * j, 256 * j + 256), 8, 256)
                        if j >= 1:
                            item("down", rows(d, 2 * j - 2, 2 * j, 0, 1024), 2, 1024)
                    if f == "ffn2":
                        continue
                    wi = A["w_in"][l, :, :]
                    item("cmp", rows(wi, 0, 8, 512, 768), 8, 256)
                    for c in range(2):
                        item("q_r", rows(wi, 0, 8, 1304 + 256 * c, 1560 + 256 * c), 8, 256)
                    for c in range(2):
                        item("k_r", rows(wi, 0, 8, 1816 + 256 * c, 2072 + 256 * c), 8, 256)
                    for kv in range(2):
                        for c in range(2):
                            item("w1", rows(A["cmp_w1"][l, kv, :, :], 8 * c, 8 * c + 8, 0, 256), 8, 256, False)
                    for c in range(2):
                        item("v_r", rows(wi, 4 * c, 4 * c + 4, 2328, 2840), 4, 512)
                    for c in range(2):
                        item("g_r", rows(wi, 4 * c, 4 * c + 4, 2840, 3352), 4, 512)
                    for c in range(2):
                        item("q_n", (wi, c), 8, 256)
                    item("slc", rows(wi, 0, 8, 768, 1024), 8, 256)
                    item("win", rows(wi, 0, 8, 1024, 1280), 8, 256)
                    item("gates", rows(wi, 0, 8, 1280, 1408), 8, 128)
                    for c in range(4):
                        item("wk", rows(A["xa_wk"][l, :, :], 0, 8, 256 * c, 256 * c + 256), 8, 256)
                    for n in range(2):
                        for c in range(2):
                            item("wv", rows(A["xa_wv"][l, :, :], 4 * c, 4 * c + 4, 512 * n, 512 * n + 512), 4, 512)
                    for c in (2, 3, 0, 1):
                        item("w_out", rows(A["w_out"][l, :, :], 2 * c, 2 * c + 2, 0, 1024), 2, 1024)
                    for c in range(4):
                        item("wq", rows(A["xa_wq"][l, :, :], 0, 8, 256 * c, 256 * c + 256), 8, 256)
                    for c in range(4):
                        item("wo", rows(A["xa_wo"][l, :, :], 2 * c, 2 * c + 2, 0, 1024), 2, 1024)
            for l in range(2):
                wi = A["w_in_2"][l, :, :]
                for c in range(2):
                    for s in range(2):
                        item("iq", rows(wi, 4 * s, 4 * s + 4, 2048 + 292 * c, 2340 + 292 * c), 4, 292)
                for tag, c0 in (("q", 512), ("k", 1024), ("v", 1536), ("u", 0)):
                    for s in range(2):
                        item(tag, rows(wi, 4 * s, 4 * s + 4, c0, c0 + 512), 4, 512)
                for c in range(4):
                    item("w_out2", rows(A["w_out_2"][l, :, :], 2 * c, 2 * c + 2, 0, 1024), 2, 1024)
                f1, f2 = A["w_ff1_2"][l, :, :], A["w_ff2_2"][l, :, :]
                for j in range(17):
                    if j < 16:
                        item("ff1", rows(f1, 0, 8, 256 * j, 256 * j + 256), 8, 256)
                    if j >= 1:
                        item("ff2", rows(f2, 2 * j - 2, 2 * j, 0, 1024), 2, 1024)

        plan()
        nsplit = [0]
        slot_of = {}
        landed = {}
        halves = {}
        free_raw = {}
        free_half = {}
        at = {"load": 0, "split": 0, "use": 0}

        def load_more():
            while at["load"] < len(items):
                i = at["load"]
                if i >= NRAW and i - NRAW not in free_raw:
                    return
                tag, src, k, n, _ = items[i]
                dst = RAW[:, (i % NRAW) * 2048:(i % NRAW) * 2048 + k * n].rearrange("p (k n) -> p k n", k=k)
                w = free_raw.get(i - NRAW)
                if tag == "q_n":
                    wi, c = src
                    for f in range(2):
                        for a in range(2):
                            c0 = 256 * a + 128 * c + 64 * f
                            o = dst[:, :, f * 128 + a * 64:f * 128 + a * 64 + 64]
                            s = rows(wi, 0, 8, c0, c0 + 64)
                            sp.load(lambda e, o=o, s=s: e.dma_start(o, s), [w], s_raw[i % NRAW], 0)
                    uses[i % NRAW] += 64
                else:
                    sp.load(lambda e, o=dst, s=src: e.dma_start(o, s), [w], s_raw[i % NRAW], 0)
                    uses[i % NRAW] += 16
                landed[i] = (s_raw[i % NRAW], uses[i % NRAW])
                at["load"] += 1

        uses = [0] * NRAW

        def split_more(upto):
            while at["split"] <= min(upto, len(items) - 1):
                i = at["split"]
                tag, src, k, n, split = items[i]
                load_more()
                if split:
                    s = nsplit[0]
                    nsplit[0] += 1
                    slot_of[i] = s
                    b = (s % NSPLIT) * 2048
                    raw = RAW[:, (i % NRAW) * 2048:(i % NRAW) * 2048 + k * n]
                    hi, lo = WHI[:, b:b + k * n], WLO[:, b:b + k * n]
                    used = free_half[s - NSPLIT] if s >= NSPLIT else None
                    a = av(hi, raw, ACT.Copy, [landed[i], used])
                    d = tt(lo, raw, hi.bitcast(F32), ALU.subtract, [landed[i], a])
                    halves[i] = d
                    free_raw[i] = [d]
                at["split"] += 1
            load_more()

        def take(tag, ahead=AHEAD):
            i = at["use"]
            assert items[i][0] == tag, (items[i][0], tag)
            at["use"] += 1
            split_more(i + ahead)
            k, n = items[i][2:4]
            b = (slot_of[i] % NSPLIT) * 2048
            view = [x[:, b:b + k * n].rearrange("p (k n) -> p k n", k=k) for x in (WHI, WLO)]
            return view[0], view[1], halves[i], i

        def take_raw(tag):
            i = at["use"]
            assert items[i][0] == tag, (items[i][0], tag)
            at["use"] += 1
            split_more(i + AHEAD)
            k, n = items[i][2:4]
            return RAW[:, (i % NRAW) * 2048:(i % NRAW) * 2048 + k * n].rearrange("p (k n) -> p k n", k=k), landed[i], i

        def done(i, mark):
            if i in slot_of:
                free_half[slot_of[i]] = mark
            else:
                free_raw[i] = [mark]
                load_more()

        gains = []

        def gain_plan():
            def g(v):
                gains.append([(0, v)])
            for l in range(2):
                for n in ("ffn1_pre_g", "ffn1_post_g", "mix_pre_g"):
                    g(A[n][l, :])
                g(A["xa_mem_g"][l, :])
                gains.append([(0, A["ret_gn_g"][l, :]), (512, A["nsa_out_g"][l, :])])
                for n in ("mix_post_g", "xa_pre_g", "xa_post_g", "ffn2_pre_g", "ffn2_post_g"):
                    g(A[n][l, :])
            for l in range(2):
                for n in ("g_pre_mix_2", "g_post_mix_2", "g_pre_ffn_2", "g_post_ffn_2"):
                    g(A[n][l, :])

        gain_plan()
        gst = {"load": 0, "use": 0}
        guse = [0] * NG
        gfree = {}
        gmark = {}

        def gain_loads():
            while gst["load"] < len(gains):
                i = gst["load"]
                if i >= NG and i - NG not in gfree:
                    return
                s = i % NG
                for off, v in gains[i]:
                    n = v.shape[0]
                    o = GV[:, s * DM + off:s * DM + off + n]
                    pool.load(lambda e, o=o, v=v: e.dma_start(o, v.partition_broadcast(128)), [gfree.get(i - NG)], s_gv[s], 0)
                    guse[s] += 16
                gmark[i] = (s_gv[s], guse[s])
                gst["load"] += 1

        def gain():
            i = gst["use"]
            gst["use"] += 1
            return GV[:, (i % NG) * DM:(i % NG) * DM + DM], gmark[i], i

        def gain_done(i, mark):
            gfree[i] = mark
            gain_loads()

        def cload(k, o, s):
            return sp.load(lambda e: e.dma_start(o, s), [], s_c[k], 16)

        c_small = A["c_small"]
        m_x = [cload(1 + m, X[:, m * DM:(m + 1) * DM], A["x"][0, m * 128:(m + 1) * 128, :]) for m in range(2)]
        m_cs = cload(0, CS[:, 0:992], c_small[:, 0:992])
        load_more()
        m_cs2 = cload(3, small[:, 0:392], c_small[:, 992:1384])
        pe_in = R[0:64, 0:128]
        ps_in = R[0:8, 128:256]
        pos_in = R[0:2, 256:384].bitcast(I32)
        pos_row = R[0:2, 384:512]
        m_pe = cload(4, pe_in, A["cmp_pe"].rearrange("l c (k a) d -> (l c k) (a d)", a=2))
        m_ps = cload(5, ps_in, A["pool_scale_2"].rearrange("l (g p) -> (l g) p", p=128))
        m_w2 = cload(6, W2C[:, :].rearrange("p (a d) -> p a d", d=64),
                     A["cmp_w2"].rearrange("l c (k p) d -> p (l c k) d", p=128))
        m_pos = cload(7, pos_in, A["positions_2"].rearrange("o (m p) -> (o m) p", p=128))
        gain_loads()
        m_mh = pool.add(lambda e: e.memset(MHALF, -0.5), [])
        m_sc = pool.add(lambda e: e.memset(SC[:, :], 0.0), [])
        m_pc = pool.add(lambda e: e.memset(PC[:, :], 0.0), [])
        t1 = tr(PS[:, 0, 0:64], pe_in, CS[0:64, 0:64], [m_pe, m_cs])
        t1 = tr(PS[:, 0, 64:72], ps_in, CS[0:8, 0:8], [m_ps], True)
        m_pet = cp(SM[:, 0:72], PS[:, 0, 0:72], [t1])
        BF[0] = m_pet
        p = cp(pos_row, pos_in, [m_pos])
        t1 = tr(PS[:, 0, 128:130], pos_row, CS[0:2, 0:2], [p, m_pet], True)
        p = cp(posf, PS[:, 0, 128:130], [t1])
        BF[0] = p
        for shift, dst in ((0.0, SIN), (0.25 * TWO_PI, COS)):
            a = tt(ang.rearrange("p (m j) -> p m j", m=2), bc(posf, 8), bm(INV, 2), ALU.mult, [p, m_cs2])
            a = ts(nrd, ang, 1.0 / TWO_PI, shift / TWO_PI, ALU.mult, ALU.add, [a])
            a = ts(nrd, nrd, ROUND, None, ALU.add, w=[a])
            a = ts(nrd, nrd, ROUND, None, ALU.subtract, w=[a])
            for c in (PI_A, PI_B, PI_C):
                a = stt(ang, nrd, -c, ang, ALU.mult, ALU.add, [a])
            a = ts(ang, ang, shift, None, ALU.add, w=[a])
            a = ts(ang, ang, 3.14159, -3.14159, ALU.min, ALU.max, [a])
            p = av(dst, ang, ACT.Sin, [a])
        m_rope = p

        S_EPS = EPS

        def to_halves(m, half, hi_t, lo_t, src_mark, old, bank, cols=None):
            for k in range(4):
                c = m * DM + (half * 4 + k) * 128
                t = tr(PS[:, bank, k * 128:(k + 1) * 128], XN[:, c:c + 128], IDN, [src_mark, BF[bank]], k == 3)
            v = PS[:, bank, :].rearrange("p (k n) -> p k n", k=4)
            hi = hi_t[:, :].rearrange("p (k n) -> p k n", k=8)[:, half * 4:half * 4 + 4, m * 128:(m + 1) * 128]
            lo = lo_t[:, :].rearrange("p (k n) -> p k n", k=8)[:, half * 4:half * 4 + 4, m * 128:(m + 1) * 128]
            a = av(hi, v, ACT.Copy, [t, old])
            d = tt(lo, v, hi.bitcast(F32), ALU.subtract, [a, t, old])
            BF[bank] = d
            return d, t

        SQ = R[:, 6144:7168]
        free = {"xn": None, "a": None, "m": None, "h0": None, "h1": None}

        def mean_root(dst, s, n, w, times=1.0):
            k = times ** -2.0
            a = ts(var[:, 0:1] if dst.shape[1] == 1 else rvar, s, k / n, k * S_EPS, ALU.mult, ALU.add, [w])
            n1 = dst.shape[1]
            return tt(dst, var[:, 0:1] if n1 == 1 else rvar, MHALF[:, 0:n1], ALU.pow, w=[a, m_mh], q=pool)

        def pre_norm(xm):
            g, mg, gi = gain()
            last = []
            sq, xs = [], []
            for m in range(2):
                x = X[:, m * DM:(m + 1) * DM]
                xn = XN[:, m * DM:(m + 1) * DM]
                sq.append(av(xn, x, ACT.Square, [xm[m], free["xn"]], accum_out=ssq[:, m:m + 1]))
            for m in range(2):
                x = X[:, m * DM:(m + 1) * DM]
                xn = XN[:, m * DM:(m + 1) * DM]
                r = mean_root(rstd[:, m:m + 1], ssq[:, m:m + 1], DM, sq[m])
                xs.append(stt(xn, x, rstd[:, m:m + 1], g, ALU.mult, ALU.mult, [r, mg]))
            for m in range(2):
                for half in range(2):
                    h, t = to_halves(m, half, AHI, ALO, xs[m], free["a"], 2 * m + half)
                    last.append(h)
            gain_done(gi, xs[1])
            free["xn"] = t
            return last[2:]

        def post_norm(y, times):
            g, mg, gi = gain()
            out = []
            for m in range(2):
                ym = PS[:, 4 + 2 * m:6 + 2 * m, :].rearrange("p b n -> p (b n)")
                x = X[:, m * DM:(m + 1) * DM]
                xn = XN[:, m * DM:(m + 1) * DM]
                a = av(SQ, ym, ACT.Square, [y[m], free["region"]], accum_out=ssq[:, m:m + 1])
                d = tt(xn, ym, g, ALU.mult, [a, mg, free["xn"]])
                BF[4 + 2 * m] = BF[5 + 2 * m] = d
                r = mean_root(rstd[:, m:m + 1], ssq[:, m:m + 1], DM, a, times)
                out.append(stt(x, xn, rstd[:, m:m + 1], x, ALU.mult, ALU.add, [d, r]))
            gain_done(gi, d)
            free["xn"] = out[1]
            return out

        def up(tag, bank, rdy, hi_t=AHI, lo_t=ALO, n=2):
            hi, lo, mark, i = take(tag)
            for f in range(n):
                t = up_tile(hi, lo, mark, f, bank, f, rdy, hi_t, lo_t)
            done(i, t)
            return t

        def up_tile(hi, lo, mark, f, bank, half, rdy, hi_t, lo_t):
            xh = hi_t[:, :].rearrange("p (k n) -> p k n", k=8)
            xl = lo_t[:, :].rearrange("p (k n) -> p k n", k=8)
            o = PS[:, bank, half * 256:(half + 1) * 256]
            for k in range(8):
                for s, (w, x) in enumerate(((hi, xh), (hi, xl), (lo, xh))):
                    t = mm(o, w[:, k, f * 128:(f + 1) * 128], x[:, k, :], k == 0 and s == 0, k == 7 and s == 2,
                           [mark, rdy[k // 4], BF[bank]], k == 7 and s == 2)
            return t

        def down(tag, rdy, ah, al, first, last):
            hi, lo, mark, i = take(tag)
            ts_ = []
            for m in range(2):
                for kk in range(2):
                    lh = ah[:, kk, m * 128:(m + 1) * 128]
                    ll = al[:, kk, m * 128:(m + 1) * 128]
                    for n in range(2):
                        b = 4 + 2 * m + n
                        for s, (x, w) in enumerate(((lh, hi), (lh, lo), (ll, hi))):
                            t = mm(PS[:, b, :], x, w[:, kk, n * 512:(n + 1) * 512], first and kk == 0 and s == 0,
                                   last and kk == 1 and s == 2, [mark, rdy, BF[b]], kk == 1 and n == 1 and s == 2)
                ts_.append(t)
            done(i, t)
            return ts_

        def natural(tag, banks, rdy, n=512):
            xh = AHI[:, :].rearrange("p (k n) -> p k n", k=8)
            xl = ALO[:, :].rearrange("p (k n) -> p k n", k=8)
            for c in range(2):
                hi, lo, mark, i = take(tag)
                for kk in range(4):
                    k = 4 * c + kk
                    for m in range(2):
                        ms = slice(m * 128, (m + 1) * 128)
                        for s, (x, w) in enumerate(((xh, hi), (xh, lo), (xl, hi))):
                            t = mm(PS[:, banks[m], 0:n], x[:, k, ms], w[:, kk, :], k == 0 and s == 0, k == 7 and s == 2,
                                   [mark, rdy[c], BF[banks[m]]], kk == 3 and m == 1 and s == 2)
                done(i, t)
            return t

        def eight(tag, bh, bl, rdy, order=(0, 1, 2, 3), between=None):
            hv = bh[:, :].rearrange("p (k n) -> p k n", k=8)
            lv = bl[:, :].rearrange("p (k n) -> p k n", k=8)
            for n, c in enumerate(order):
                t = down(tag, rdy[c], hv[:, 2 * c:2 * c + 2, :], lv[:, 2 * c:2 * c + 2, :], n == 0, n == 3)
                if between and n in between:
                    between[n]()
            return t

        def ffn(xm, kind):
            rdy = pre_norm(xm)
            nj = 16 if kind == "relu2" else 11
            H = R[:, 0:1024].rearrange("p (s n) -> p s n", s=2)
            G = R[:, 1024:3072].rearrange("p (s n) -> p s n", s=4)
            hm = {}
            for j in range(nj + 1):
                if j < nj:
                    s = j % 2
                    hf, hh, hl = H[:, s, :], HHI[:, s * 512:(s + 1) * 512], HLO[:, s * 512:(s + 1) * 512]
                    if kind == "relu2":
                        b = j % 4
                        tg = up("ff1", b, rdy)
                        a = av(G[:, s, :], PS[:, b, :], ACT.Relu, [tg, free["region"]])
                        d = tt(hf, G[:, s, :], PS[:, b, :], ALU.mult, [a])
                        BF[b] = d
                    else:
                        bg, bu = 2 * s, 2 * s + 1
                        tg = up("gate", bg, rdy)
                        tu = up("up", bu, rdy)
                        a = av(G[:, s, :], PS[:, bg, :], ACT.Tanh, [tg, free["region"]], scale=0.5)
                        d = stt(G[:, 2 + s, :], G[:, s, :], 1.0, PS[:, bg, :], ALU.add, ALU.mult, [a])
                        BF[bg] = d
                        d = stt(hf, G[:, 2 + s, :], 0.5, PS[:, bu, :], ALU.mult, ALU.mult, [d, tu])
                        BF[bu] = d
                    a = av(hh, hf, ACT.Copy, [d, free["h%d" % s]])
                    hm[j] = tt(hl, hf, hh.bitcast(F32), ALU.subtract, [a], q=pool)
                    rdy_last = tg
                if j >= 1:
                    s = (j - 1) % 2
                    ah, al = [x[:, s * 512:(s + 1) * 512].rearrange("p (k n) -> p k n", k=2) for x in (HHI, HLO)]
                    t = down("ff2" if kind == "relu2" else "down", hm[j - 1], ah, al, j == 1, j == nj)
                    free["h%d" % s] = t[1]
            free["a"] = t[1]
            free["region"] = [hm[nj - 1], d, a]
            return post_norm(t, 1.0 if kind == "relu2" else 0.5)

        def run_units(units, P2, PT2, fill):
            n = len(units)
            marks = [None] * n
            pfree, tfree = [None, None], [None, None]

            def head(u):
                q = units[u]
                s = u % 2
                t = q["scores"](4 + 2 * s)
                P = P2[s]
                d = q["shift"](4 + 2 * s, P, [t, pfree[s], q["old"]])
                BF[4 + 2 * s] = BF[5 + 2 * s] = d
                P = P[:, :, 0:q["w"]]
                d = red(mx[:, 4 * s:4 * s + 4], P, ALU.max, [d])
                marks[u] = ts(nb[:, 4 * s:4 * s + 4], mx[:, 4 * s:4 * s + 4], -q["scale"], None, ALU.mult, w=[d])

            def exps(u):
                q = units[u]
                s = u % 2
                P = P2[s][:, :, 0:q["w"]]
                for i in range(4):
                    a = av(P[:, i, :], P[:, i, :], ACT.Exp, [marks[u]], scale=q["scale"], bias=nb[:, 4 * s + i:4 * s + i + 1],
                           accum_out=den[:, 4 * s + i:4 * s + i + 1])
                return a

            head(0)
            em = exps(0)
            for u in range(n):
                q = units[u]
                s = u % 2
                nk = q["w"] // 128
                if u + 1 < n:
                    head(u + 1)
                if fill:
                    fill.pop(0)()
                evs = []
                for k in range(nk):
                    for i in range(4):
                        t = tr(PS[:, k, i * 128:(i + 1) * 128], P2[s][:, i, k * 128:(k + 1) * 128], IDN, [em, BF[k]], i == 3)
                    pt = PT2[s][:, k * 512:(k + 1) * 512]
                    if k:
                        e = cp(pt, PS[:, k, :], [t, tfree[s], q["old"]])
                    else:
                        e = av(pt, PS[:, k, :], ACT.Copy, [t, tfree[s], q["old"]])
                    BF[k] = e
                    evs.append(e)
                pfree[s] = t
                e_now = em
                if u + 1 < n:
                    em = exps(u + 1)
                if fill:
                    fill.pop(0)()
                tfree[s] = q["values"](s, PT2[s], evs, e_now)
            while fill:
                fill.pop(0)()
            return [tfree[0], tfree[1]]

        def hybrid(l, xm):
            rdy = pre_norm(xm)
            fr = free["region"]
            qT = R[:, 0:1024].rearrange("p (k n) -> p k n", k=4)
            kvT = R[:, 1024:2048]
            vN = R[:, 2048:2560].rearrange("p (m n) -> p m n", m=2)
            gT = R[:, 2560:2816]
            Bk = R[:, 2816:3776]
            sT = R[:, 3776:3904]
            sTh = R[:, 3904:4032]
            tmp = R[:, 2816:3840]
            qrT = R[:, 4032:5056].rearrange("p (k n) -> p k n", k=4)
            krT = R[:, 5056:6080].rearrange("p (k n) -> p k n", k=4)
            ST = R[:, 6080:7616]
            DEC = R[:, 7616:9152]
            vr = R[:, 9152:10176]
            gr = R[:, 10176:11200]
            P2 = [R[:, 4032 + 1024 * i:5056 + 1024 * i].rearrange("p (h n) -> p h n", h=4) for i in range(2)]
            PT2 = [R[:, 6080 + 1024 * i:7104 + 1024 * i] for i in range(2)]
            O_ = R[:, 8128:9152]
            mkT = R[:, 9152:11200]
            mV = R[:, 11200:13248]
            pool.load(lambda e: e.dma_start(DEC, A["c_decay"]), [fr], s_aux[0], 0)
            auxn[0] += 16
            aux = (s_aux[0], auxn[0])

            t = up("cmp", 0, rdy)
            for kv in range(2):
                Bv = Bk[:, kv * 480:(kv + 1) * 480].rearrange("p (k g n) -> p k g n", k=16, g=2)
                for g in range(2):
                    src = PS[g * 64:(g + 1) * 64, 0, kv * 256:(kv + 1) * 256]
                    for par in range(2):
                        for hi16 in range(2):
                            v = src.rearrange("p (n k a) -> p k n a", k=8, a=2)[:, :, hi16:hi16 + 15, par]
                            c0 = (l * 2 + kv) * 16 + hi16 * 8
                            pt = PET[par * 64:(par + 1) * 64, c0:c0 + 8]
                            d = tt(Bv[par * 64:(par + 1) * 64, hi16 * 8:hi16 * 8 + 8, g, :], v, bc(pt, 15), ALU.add, [t, m_pet, fr])
            BF[0] = bm_ = d

            for c in range(2):
                b = 1 + c
                t = up("q_r", b, rdy)
                BF[b] = av(qrT[:, 2 * c:2 * c + 2, :].rearrange("p k n -> p (k n)"), PS[:, b, :], ACT.Copy, [t, fr])
            pool.load(lambda e: e.dma_start(XN[:, :].rearrange("p (m n) -> p m n", m=2), A["mem"][0, :, :].rearrange("(m p) n -> p m n", p=128)),
                      [free["xn"]], s_aux[1], 0)
            auxn[1] += 16
            mem_in = (s_aux[1], auxn[1])
            g, mg, gi = gain()
            mn = []
            for m in range(2):
                x = XN[:, m * DM:(m + 1) * DM]
                a = av(R[:, 12224:13248], x, ACT.Square, [mem_in, fr], accum_out=ssq[:, m:m + 1])
                q = mean_root(rstd[:, m:m + 1], ssq[:, m:m + 1], DM, a)
                mn.append(stt(x, x, rstd[:, m:m + 1], g, ALU.mult, ALU.mult, [q, mg]))
            gain_done(gi, mn[1])
            for c in range(2):
                b = (3, 0)[c]
                t = up("k_r", b, rdy)
                BF[b] = av(krT[:, 2 * c:2 * c + 2, :].rearrange("p k n -> p (k n)"), PS[:, b, :], ACT.Copy, [t, fr])
            qk = BF[0]

            for kv in range(2):
                Bv = Bk[:, kv * 480:(kv + 1) * 480].rearrange("p (k c) -> p k c", k=16)
                for c in range(2):
                    raw, mark, i = take_raw("w1")
                    for ht in range(2):
                        for kk in range(8):
                            k = 8 * c + kk
                            t = mm(PS[:, 4 + 2 * kv + ht, 0:30], raw[:, kk, ht * 128:(ht + 1) * 128], Bv[:, k, :],
                                   k == 0, k == 15, [mark, bm_, BF[4 + 2 * kv + ht]], ht == 1 and kk == 7)
                    done(i, t)
                sv = sT[:, kv * 60:kv * 60 + 60].rearrange("p (h c) -> p h c", h=2)
                sh = sTh[:, kv * 60:kv * 60 + 60].rearrange("p (h c) -> p h c", h=2)
                pv = PS[:, 4 + 2 * kv:6 + 2 * kv, 0:30]
                a = av(sv, pv, ACT.Tanh, [t, fr], scale=0.5)
                d = stt(sh, sv, 1.0, pv, ALU.add, ALU.mult, [a])
                BF[4 + 2 * kv] = BF[5 + 2 * kv] = d
                if kv == 0:
                    kh, kh_m = sh, d
            scv = SC[:, :].rearrange("p (h g n) -> p h g n", h=2, g=2)[:, :, :, 0:15]
            vh_m = cp(scv, sTh[:, 60:120].rearrange("p (h g n) -> p h g n", h=2, g=2), [d, m_sc, free_kc[0]])
            rm = []
            for m in range(2):
                for half in range(2):
                    h_, t = to_halves(m, half, MHI, MLO, mn[m], free["m"], 1 + half)
                    rm.append(h_)
            free["xn"] = t
            rm = rm[2:]

            t = natural("v_r", (1, 2), rdy)
            for m in range(2):
                BF[1 + m] = av(vr[:, m * 512:(m + 1) * 512], PS[:, 1 + m, :], ACT.Copy, [t, fr])
            vrm = BF[2]
            for g in range(2):
                for ht in range(2):
                    w0 = ((l * 2) * 2 + ht) * 64
                    t = mm(PS[g * 64:(g + 1) * 64, 6, 0:15], W2C[:, w0:w0 + 64], kh[:, ht, g * 15:(g + 1) * 15],
                           ht == 0, ht == 1, [kh_m, m_w2, BF[6]], g == 1 and ht == 1)
            for i4 in range(4):
                for g in range(2):
                    for ht in range(2):
                        w0 = ((l * 2 + 1) * 2 + ht) * 64
                        t2 = mm(PS[32 * i4:32 * i4 + 32, 7, g * 64:(g + 1) * 64], SC[:, (ht * 2 + g) * 32:(ht * 2 + g + 1) * 32],
                                W2C[:, w0:w0 + 64], ht == 0, ht == 1, [vh_m, BF[7]], i4 == 3 and g == 1 and ht == 1)
            BF[6] = k_m = ts(kcT[:, 0:15], PS[:, 6, 0:15], 0.5, None, ALU.mult, w=[t, free_kc[0]])
            BF[7] = v_m = ts(vcR, PS[:, 7, 0:128], 0.5, None, ALU.mult, w=[t2])

            for h in range(4):
                b = 4 + h // 2
                t = mm(PS[:, b, (h % 2) * 256:(h % 2) * 256 + 256], krT[:, h, 0:128], qrT[:, h, :], True, True, [qk, BF[b]])
            for h in range(4):
                t = mm(PS[:, 6, h * 128:(h + 1) * 128], krT[:, h, 128:256], qrT[:, h, 128:256], True, True, [BF[6]], h == 3)
            d = tt(ST[:, 0:1024], PS[:, 4:6, :].rearrange("p b n -> p (b n)"), DEC[:, 0:1024], ALU.mult, [t, aux, fr])
            BF[4] = BF[5] = d
            BF[6] = st_m = tt(ST[:, 1024:1536], PS[:, 6, :], DEC[:, 1024:1536], ALU.mult, [t])
            t = natural("g_r", (3, 0), rdy)
            for m in range(2):
                b = (3, 0)[m]
                a = av(gr[:, m * 512:(m + 1) * 512], PS[:, b, :], ACT.Tanh, [t, fr], scale=0.5)
                g2 = stt(gr[:, m * 512:(m + 1) * 512], gr[:, m * 512:(m + 1) * 512], 1.0, PS[:, b, :], ALU.add, ALU.mult, [a])
                BF[b] = g2
            s0 = ST[:, 0:1024].rearrange("p (h n) -> p h n", h=4)
            s1 = ST[:, 1024:1536].rearrange("p (h n) -> p h n", h=4)
            t_o = []
            for m in range(2):
                for h in range(4):
                    ob = PS[:, 4 + m, h * 128:(h + 1) * 128]
                    if m == 0:
                        t = mm(ob, s0[:, h, 0:128], vr[:, h * 128:(h + 1) * 128], True, True, [st_m, vrm, BF[4]], h == 3)
                    else:
                        mm(ob, s0[:, h, 128:256], vr[:, h * 128:(h + 1) * 128], True, False, [st_m, vrm, BF[5]])
                        t = mm(ob, s1[:, h, :], vr[:, 512 + h * 128:512 + (h + 1) * 128], False, True, [], h == 3)
                t_o.append(t)
            ret_pe = t

            for c in range(2):
                b = 1 + c
                t = up("q_n", b, rdy)
                BF[b] = av(qT[:, 2 * c:2 * c + 2, :].rearrange("p k n -> p (k n)"), PS[:, b, :], ACT.Copy, [t, fr])
            q_m = BF[2]
            gg, mg, gi = gain()
            ret_x = []
            for m in range(2):
                ob = PS[:, 4 + m, :].rearrange("p (h n) -> p h n", h=4)
                xn = XN[:, m * DM + 512:(m + 1) * DM]
                xv = xn.rearrange("p (h n) -> p h n", h=4)
                sq = XN[:, m * DM:m * DM + 512]
                d = red(rsum, ob, ALU.add, [t_o[m]])
                d = ts(rsum, rsum, 1.0 / 128, None, ALU.mult, w=[d])
                c = tt(xv, ob, bc(rsum, 128), ALU.subtract, [d, free["xn"]])
                BF[4 + m] = c
                a = av(sq, xn, ACT.Square, [c])
                d = red(rsum, sq.rearrange("p (h n) -> p h n", h=4), ALU.add, [a])
                d = mean_root(rsum, rsum, 128, d, 0.5)
                q = tt(xn, xn, gg[:, 0:512], ALU.mult, [c, a, mg], q=pool)
                q = tt(xn, xn, gr[:, m * 512:(m + 1) * 512], ALU.mult, [q, g2], q=pool)
                ret_x.append(tt(xv, xv, bc(rsum, 128), ALU.mult, [d, q]))
            ret_m = ret_x[1]
            for c, tag in enumerate(("slc", "win")):
                b = (3, 0)[c]
                t = up(tag, b, rdy)
                BF[b] = av(kvT[:, c * 512:(c + 1) * 512], PS[:, b, :], ACT.Copy, [t, fr])
            kv_m = BF[0]
            t = up("gates", 1, rdy, n=1)
            free["a"] = t
            a = av(gT[0:24, :], PS[0:24, 1, 0:256], ACT.Tanh, [t, fr], scale=0.5)
            BF[1] = a
            kvv = kvT.rearrange("p (b n) -> p b n", b=4)
            for br in range(2):
                for m in range(2):
                    t = tr(PS[:, 2, (m * 2 + br) * 128:(m * 2 + br + 1) * 128], kvv[:, 2 * br + 1, m * 128:(m + 1) * 128], IDN,
                           [kv_m, BF[2]], br == 1 and m == 1)
            BF[2] = vn_m = cp(vN.rearrange("p m n -> p (m n)"), PS[:, 2, :], [t, fr])
            for m in range(2):
                t = tr(PS[:, 3, m * 24:m * 24 + 24], gT[0:24, m * 128:(m + 1) * 128], CS[0:24, 0:24], [a, BF[3]], m == 1)
            g_m = ts(gates.rearrange("p m c -> p (m c)"), PS[:, 3, 0:48], 1.0, 0.5, ALU.add, ALU.mult, [t])
            BF[3] = g_m
            wrdy = [None] * 4
            for m in range(2):
                d, t = to_halves(m, 1, AHI, ALO, ret_x[m], free["a"], m)
            wrdy[2] = wrdy[3] = d
            ret_t = t

            old_t = None
            for m in range(2):
                gm = gates[:, m, :].rearrange("p (h b) -> p h b", b=3)
                om = O_[:, m * 512:(m + 1) * 512].rearrange("p (h d) -> p h d", h=8)
                for h in range(8):
                    r = slice(0, 64) if h < 4 else slice(64, 128)
                    t = mm(PS[:, 4 + h // 4, (h % 4) * 16:(h % 4) * 16 + 15], qT[r, h % 4, m * 128:(m + 1) * 128], kcT[r, 0:15],
                           True, True, [q_m, k_m, BF[4], BF[5]], h == 7)
                pc = PC[:, :].rearrange("p (h n) -> p h n", h=8)[:, :, 0:15]
                cbv = CB[:, m, :].rearrange("p (h n) -> p h n", h=8)
                cmv = CM[:, m, :].rearrange("p (h n) -> p h n", h=8)
                for g in range(2):
                    d = stt(pc[:, 4 * g:4 * g + 4, :], PS[:, 4 + g, 0:64].rearrange("p (h n) -> p h n", h=4)[:, :, 0:15], 0.125,
                            cbv[:, 4 * g:4 * g + 4, :], ALU.mult, ALU.add, [t, m_pc, free_kc[0]])
                BF[4] = BF[5] = d
                d = red(mx, pc, ALU.max, [d])
                d = tt(pc, pc, bc(mx, 15), ALU.subtract, [d])
                a = av(pc, pc, ACT.Exp, [d])
                d = tt(pc, pc, cmv, ALU.mult, [a])
                d1 = d
                d = red(den, pc, ALU.add, [d])
                d2 = ts(den, den, 1e-30, None, ALU.max, w=[d])
                d2 = rcp(den, den, [d2])
                d2 = tt(coef, den, gm[:, :, 0], ALU.mult, [d2, g_m])
                fill_mem[0](l, rm, mkT, mV, [fr, ret_pe, ret_m])
                for g in range(2):
                    t = tr(PS[:, 6, g * 128:(g + 1) * 128], PC[:, g * 128:(g + 1) * 128], IDN, [d1, BF[6]], g == 1)
                free_kc[0] = t
                pct = cp(gT, PS[:, 6, 0:256], [t, old_t, g_m])
                BF[6] = pct
                for h in range(8):
                    i4, g = h % 4, h // 4
                    b = (0, 1, 2, 7)[i4]
                    t = mm(PS[:, b, g * 64:(g + 1) * 64], gT[32 * i4:32 * i4 + 15, g * 128:(g + 1) * 128],
                           vcR[32 * i4:32 * i4 + 15, g * 64:(g + 1) * 64], True, True, [pct, v_m, BF[0], BF[1], BF[2], BF[7]], h == 7)
                old_t = t
                for g in range(2):
                    d = tt(om[:, 4 * g:4 * g + 3, :], PS[:, 0:3, g * 64:(g + 1) * 64], bc(coef[:, 4 * g:4 * g + 3], 64), ALU.mult,
                           [t, d2, ret_m, st_m])
                    d = tt(om[:, 4 * g + 3, :], PS[:, 7, g * 64:(g + 1) * 64], coef[:, 4 * g + 3:4 * g + 4].broadcast_to([128, 64]),
                           ALU.mult, [])
                BF[0] = BF[1] = BF[2] = BF[7] = d
            free_kc[0] = old_t

            units = []
            om_m = [None]

            def unit(m, g, br):
                w = 128 * (m + 1)
                rs = slice(g * 64, g * 64 + 64)
                kT = kvv[:, 2 * br, :]
                al = ALIBI[:, 0:128] if m == 0 else ALIBI[:, 128:384]
                gm = gates[:, m, :].rearrange("p (h b) -> p h b", b=3)
                om = O_[:, m * 512 + g * 256:m * 512 + g * 256 + 256].rearrange("p (h d) -> p h d", h=4)

                def scores(b):
                    for i in range(4):
                        t = mm(PS[:, b + i // 2, (i % 2) * 256:(i % 2) * 256 + w], qT[rs, i, m * 128:(m + 1) * 128], kT[rs, 0:w],
                               True, True, [q_m, kv_m, BF[b + i // 2]], i == 3)
                    return t

                def shift(b, P, marks):
                    for i in range(4):
                        d = stt(P[:, i, 0:w], al, 8.0 * SLOPES[4 * g + i], PS[:, b + i // 2, (i % 2) * 256:(i % 2) * 256 + w],
                                ALU.mult, ALU.add, marks)
                    return d

                def values(s, PT, evs, em):
                    d2 = rcp(den[:, 4 * s:4 * s + 4], den[:, 4 * s:4 * s + 4], [em])
                    d2 = tt(coef[:, 4 * s:4 * s + 4], den[:, 4 * s:4 * s + 4], gm[:, 4 * g:4 * g + 4, 1 + br], ALU.mult, [d2])
                    for i in range(4):
                        for k in range(m + 1):
                            t = mm(PS[:, 2, s * 256 + i * 64:s * 256 + (i + 1) * 64], PT[:, (k * 4 + i) * 128:(k * 4 + i + 1) * 128],
                                   vN[:, k, br * 128 + g * 64:br * 128 + (g + 1) * 64], k == 0, k == m,
                                   [evs, vn_m, BF[2]], i == 3 and k == m)
                    tm = tmp[:, s * 256:(s + 1) * 256]
                    d = tt(tm.rearrange("p (h d) -> p h d", h=4), PS[:, 2, s * 256:(s + 1) * 256].rearrange("p (h d) -> p h d", h=4),
                           bc(coef[:, 4 * s:4 * s + 4], 64), ALU.mult, [t, d2, om_m[0]])
                    BF[2] = d
                    om_m[0] = tt(om, om, tm.rearrange("p (h d) -> p h d", h=4), ALU.add, [d], q=pool)
                    omr[m] = om_m[0]
                    return t

                units.append({"scores": scores, "shift": shift, "values": values, "scale": 0.125, "w": w,
                              "old": [ret_pe, ret_m, st_m]})

            omr = [None, None]
            for m in range(2):
                for g in range(2):
                    for br in range(2):
                        unit(m, g, br)
            tf = run_units(units, P2, PT2, fills)
            fin = []
            for m in range(2):
                xn = XN[:, m * DM:m * DM + 512]
                of = O_[:, m * 512:(m + 1) * 512]
                a = av(xn, of, ACT.Square, [omr[m], ret_t], accum_out=ssq[:, m:m + 1])
                r = mean_root(rstd[:, m:m + 1], ssq[:, m:m + 1], 512, a)
                fin.append(stt(xn, of, rstd[:, m:m + 1], gg[:, 512:1024], ALU.mult, ALU.mult, [r]))
            gain_done(gi, fin[1])

            def last_tiles():
                for m in range(2):
                    d, t = to_halves(m, 0, AHI, ALO, fin[m], free["a"], m)
                wrdy[0] = wrdy[1] = d
                free["xn"] = t

            y = eight("w_out", AHI, ALO, wrdy, (2, 3, 0, 1), {1: last_tiles})
            free["region"] = [tf, fin[1], free["xn"], wrdy[0]]
            free["a"] = y[1]
            return y

        auxn = [0, 0]
        free_kc = [None]
        fills = []
        fill_mem = [None]
        mem_done = {}

        def memory_products(l, rm, mkT, mV, old):
            if l in mem_done:
                return
            mem_done[l] = {}

            def key(c, f, st_):
                def go():
                    if f == 0:
                        st_["w"] = take("wk")
                    hi, lo, mark, i = st_["w"]
                    t = up_tile(hi, lo, mark, f, 3, 0, rm, MHI, MLO)
                    if f == 1:
                        done(i, t)
                    BF[3] = av(mkT[:, (2 * c + f) * 256:(2 * c + f + 1) * 256], PS[:, 3, 0:256], ACT.Copy, [t, old])
                    mem_done[l]["k"] = BF[3]
                return go

            def value(n, m, c, st_):
                def go():
                    if m == 0:
                        st_[c] = take("wv", AHEAD - c)
                    hi, lo, mark, i = st_[c]
                    xh = MHI[:, :].rearrange("p (k n) -> p k n", k=8)
                    xl = MLO[:, :].rearrange("p (k n) -> p k n", k=8)
                    ms = slice(m * 128, (m + 1) * 128)
                    for kk in range(4):
                        k = 4 * c + kk
                        for s, (x, w) in enumerate(((xh, hi), (xh, lo), (xl, hi))):
                            t = mm(PS[:, 3, :], x[:, k, ms], w[:, kk, :], k == 0 and s == 0, k == 7 and s == 2,
                                   [mark, rm, BF[3]], kk == 3 and s == 2)
                    if m == 1:
                        done(i, t)
                    if c == 1:
                        BF[3] = av(mV[:, m * DM + n * 512:m * DM + (n + 1) * 512], PS[:, 3, :], ACT.Copy, [t, old])
                        mem_done[l]["v"] = BF[3]
                    free["m"] = t
                return go

            for c in range(4):
                st_ = {}
                for f in range(2):
                    fills.append(key(c, f, st_))
            for n in range(2):
                st_ = {}
                for m in range(2):
                    for c in range(2):
                        fills.append(value(n, m, c, st_))

        fill_mem[0] = memory_products

        def memory(l, xm):
            fr = free["region"]
            kT = R[:, 9152:11200]
            V = R[:, 11200:13248]
            km, vm = mem_done[l]["k"], mem_done[l]["v"]
            qT = R[:, 0:2048]
            P_ = R[:, 2048:4096].rearrange("p (s m n) -> p s m n", s=4, m=2)
            PT_ = R[:, 4096:6144].rearrange("p (h k n) -> p h k n", k=2, h=4)
            rdy = pre_norm(xm)
            qv = qT.rearrange("p (k n) -> p k n", k=8)
            kv = kT.rearrange("p (k n) -> p k n", k=8)
            pm, ordy = {}, [None] * 4

            def scores(c):
                b = (4, 5, 6, 0)[c]
                for m in range(2):
                    for k in range(2):
                        t = mm(PS[:, b, m * 256:(m + 1) * 256], qv[:, 2 * c + k, m * 128:(m + 1) * 128], kv[:, 2 * c + k, :],
                               k == 0, k == 1, [qm[c], km, BF[b]], m == 1 and k == 1)
                S = PS[:, b, :].rearrange("p (m n) -> p m n", m=2)
                o = 2 * (c % 2)
                d = red(mx[:, o:o + 2], S, ALU.max, [t])
                d = ts(nb[:, o:o + 2], mx[:, o:o + 2], -0.0625, None, ALU.mult, w=[d])
                for m in range(2):
                    a = av(P_[:, c, m, :], S[:, m, :], ACT.Exp, [d, fr], scale=0.0625, bias=nb[:, o + m:o + m + 1],
                           accum_out=den[:, o + m:o + m + 1])
                BF[b] = a
                d = rcp(den[:, o:o + 2], den[:, o:o + 2], [a])
                for m in range(2):
                    d = ts(P_[:, c, m, :], P_[:, c, m, :], den[:, o + m:o + m + 1], None, ALU.mult, w=[d])
                pm[c] = d

            def turn(c):
                for m in range(2):
                    for k in range(2):
                        t = tr(PS[:, 2, (k * 2 + m) * 128:(k * 2 + m + 1) * 128], P_[:, c, m, k * 128:(k + 1) * 128], IDN,
                               [pm[c], BF[2]], m == 1 and k == 1)
                BF[2] = pm[c] = av(PT_[:, c, :, :].rearrange("p k n -> p (k n)"), PS[:, 2, :], ACT.Copy, [t, fr])

            def outs(c):
                for j in range(2):
                    f = 2 * c + j
                    for k in range(2):
                        t = mm(PS[:, 3, j * 256:(j + 1) * 256], V[:, k * DM + f * 128:k * DM + (f + 1) * 128],
                               PT_[:, c, k, :], k == 0, k == 1, [pm[c], vm, BF[3]], j == 1 and k == 1)
                hi, lo = MHI[:, c * 512:(c + 1) * 512], MLO[:, c * 512:(c + 1) * 512]
                a = av(hi, PS[:, 3, :], ACT.Copy, [t, free["m"]])
                BF[3] = ordy[c] = tt(lo, PS[:, 3, :], hi.bitcast(F32), ALU.subtract, [a, free["m"]])
                free["region"] = [t]

            qm = {}
            for c in range(4):
                b = c % 2
                t = up("wq", b, rdy)
                BF[b] = qm[c] = av(qT[:, c * 512:(c + 1) * 512], PS[:, b, :], ACT.Copy, [t, fr])
                if c >= 1:
                    turn(c - 1)
                scores(c)
                if c >= 1:
                    outs(c - 1)
            free["a"] = t
            y = eight("wo", MHI, MLO, ordy, (0, 1, 2, 3), {0: lambda: turn(3), 1: lambda: outs(3)})
            free["m"] = y[1]
            return post_norm(y, 1.0)

        def sparse(l, xm):
            rdy = pre_norm(xm)
            fr = free["region"]
            qn = R[:, 0:1024]
            kn = R[:, 1024:2048]
            iqn = R[:, 2048:3072]
            P2 = [R[:, 1024 * i:1024 * i + 1024].rearrange("p (h n) -> p h n", h=4) for i in range(2)]
            V = R[:, 3072:4096]
            U = R[:, 4096:5120]
            ikn = R[:, 5120:5376]
            ikT = R[:, 5376:5632]
            iqT = R[:, 5632:6656].rearrange("p (k n) -> p k n", k=4)
            qT = R[:, 6656:7680].rearrange("p (k n) -> p k n", k=4)
            kT = R[:, 7680:8704].rearrange("p (k n) -> p k n", k=4)
            PT2 = [R[:, 8704 + 1024 * i:9728 + 1024 * i] for i in range(2)]
            SCO = R[:, 10752:11136]
            PM = R[:, 8704:10240]
            WP = R[:, 10240:10752]
            pool.load(lambda e: e.dma_start(PM, A["c_pool"]), [fr], s_aux[0], 0)
            pool.load(lambda e: e.dma_start(WP.rearrange("p (g n) -> p g n", g=4), A["w_pool_2"][l, :, :, :].rearrange("g p n -> p g n")),
                      [fr], s_aux[0], 0)
            auxn[0] += 32
            aux = (s_aux[0], auxn[0])
            cosv = COS.rearrange("p (m j) -> p m j", m=2)
            sinv = SIN.rearrange("p (m j) -> p m j", m=2)
            rt = [XN[:, i * 128:(i + 1) * 128] for i in range(4)]

            def rope(v, h, w):
                def sh(i):
                    return rt[i][:, 0:2 * h * 8].rearrange("p (m h j) -> p m h j", m=2, h=h)
                c = cosv.unsqueeze(2).broadcast_to([128, 2, h, 8])
                s = sinv.unsqueeze(2).broadcast_to([128, 2, h, 8])
                x1, x2 = v[:, :, :, 0:8], v[:, :, :, 8:16]
                ws = [w, m_rope, free["xn"], rope_last[0]]
                tt(sh(0), x1, c, ALU.mult, ws, q=pool)
                tt(sh(1), x2, s, ALU.mult, q=pool)
                tt(sh(2), x2, c, ALU.mult, q=pool)
                p = tt(sh(3), x1, s, ALU.mult, q=pool)
                tt(x1, sh(0), sh(1), ALU.subtract, [p], q=pool)
                p = tt(x2, sh(2), sh(3), ALU.add, q=pool)
                rope_last[0] = p
                return p

            def heads_T(src, dst, ready, bank, w):
                outs = []
                for m in range(2):
                    b = bank + m
                    for k in range(4):
                        t = tr(PS[:, b, k * 128:(k + 1) * 128], src[:, m * 512 + k * 128:m * 512 + (k + 1) * 128], IDN,
                               [ready, BF[b]], k == 3)
                    e = av(dst[:, :, m * 128:(m + 1) * 128], PS[:, b, :].rearrange("p (k n) -> p k n", k=4), ACT.Copy, [t, w])
                    BF[b] = e
                    outs.append(e)
                return outs, t

            t = natural("iq", (0, 1), rdy, 292)
            for m in range(2):
                e = av(iqn[:, m * 512:m * 512 + 292], PS[:, m, 0:292], ACT.Copy, [t, fr])
                BF[m] = e
            t = natural("iq", (2, 3), rdy, 292)
            for m in range(2):
                a = av(iqn[:, m * 512 + 292:(m + 1) * 512], PS[:, 2 + m, 0:220], ACT.Copy, [t, fr])
                d = cp(ikn[:, m * 128:m * 128 + 64], PS[:, 2 + m, 220:284], [a, t, fr])
                e = av(iw[:, m, :], PS[:, 2 + m, 284:292], ACT.Copy, [d], scale=8.0 ** -0.5)
                BF[2 + m] = e
            iqm = rope(iqn.rearrange("p (m h d) -> p m h d", m=2, h=8), 8, e)
            ikv = ikn.rearrange("p (m h d) -> p m h d", m=2, h=2)
            ikm = rope(ikv[:, :, 0:1, :], 1, d)
            ikm = pool.add(lambda e: e.tensor_copy(ikv[:, :, 1, :], ikv[:, :, 0, :]), [ikm])
            t = natural("q", (0, 1), rdy)
            for m in range(2):
                e = av(qn[:, m * 512:(m + 1) * 512], PS[:, m, :], ACT.Copy, [t, fr])
                BF[m] = e
            qm = rope(qn.rearrange("p (m h d) -> p m h d", m=2, h=8), 8, e)
            for m in range(2):
                t = tr(PS[:, 4, m * 128:(m + 1) * 128], ikn[:, m * 128:(m + 1) * 128], IDN, [ikm, BF[4]], m == 1)
            BF[4] = ikt = cp(ikT, PS[:, 4, 0:256], [t, fr])
            iqt, t_i = heads_T(iqn, iqT, iqm, 5, fr)
            t = natural("k", (2, 3), rdy)
            for m in range(2):
                e = av(kn[:, m * 512:(m + 1) * 512], PS[:, 2 + m, :], ACT.Copy, [t, fr])
                BF[2 + m] = e
            km = rope(kn.rearrange("p (m h d) -> p m h d", m=2, h=8), 8, e)
            rope_pool = km

            qt, t_q = heads_T(qn, qT, qm, 0, fr)
            rls, relu_m = [], []
            for m in range(2):
                w = 128 * (m + 1)
                RL = R[:, 0:1024] if m == 0 else R[:, 11136:13184]
                rl = RL.rearrange("p (b a n) -> p b a n", b=4, a=2)
                for h in range(8):
                    b = 4 + h % 4
                    c = (h // 4) * 256
                    r = slice((h % 2) * 64, (h % 2) * 64 + 64)
                    t = mm(PS[:, b, c:c + w], iqT[r, h // 2, m * 128:(m + 1) * 128], ikT[r, 0:w], True, True,
                           [ikt, iqt, BF[b]], h == 7)
                a = av(rl, PS[:, 4:8, :].rearrange("p b (a n) -> p b a n", a=2)[:, :, :, 0:w], ACT.Relu,
                       [t, t_q, fr], scale=0.125)
                for b in range(4, 8):
                    BF[b] = a
                rls.append(rl)
                relu_m.append(a)
            kt_, t_k = heads_T(kn, kT, km, 0, fr)
            sel = []
            for m in range(2):
                w = 128 * (m + 1)
                rl = rls[m]
                s = SCO[:, m * 128:m * 128 + w]
                ch = CH[:, 0:128] if m == 0 else CH[:, 128:384]
                for h in range(8):
                    rh = rl[:, h % 4, h // 4, :]
                    if h == 0:
                        d = stt(s, rh, iw[:, m, 0:1], ch, ALU.mult, ALU.add, [relu_m[m], fr])
                    else:
                        d = stt(s, rh, iw[:, m, h:h + 1], s, ALU.mult, ALU.add, [d])
                sc_m = d
                for _ in range(8):
                    d = dve.add(lambda e, s=s: e.max(top8, s), [d])
                    d = dve.add(lambda e, s=s: e.match_replace(s, top8, s, TAKEN), [d])
                d = ts(PSC2[:, m * 128:m * 128 + w], s, TAKEN, NEG, ALU.not_equal, ALU.mult, [d])
                sel.append(d)
            t = natural("v", (2, 3), rdy)
            for m in range(2):
                e = av(V[:, m * 512:(m + 1) * 512], PS[:, 2 + m, :], ACT.Copy, [t, fr])
                BF[2 + m] = e
            vm = e
            t = natural("u", (0, 1), rdy)
            free["a"] = t
            for m in range(2):
                e = av(U[:, m * 512:(m + 1) * 512], PS[:, m, :], ACT.Copy, [t, fr])
                BF[m] = e
            um = e
            DT = R[:, 2048:3072]
            dts = []
            for g in range(4):
                b = g // 2
                o = PS[:, b, (g % 2) * 256:(g % 2) * 256 + 256]
                mm(o, U[:, g * 128:(g + 1) * 128], PM[:, g * 384:g * 384 + 256], True, False, [um, aux, BF[b]])
                t = mm(o[:, 128:256], U[:, 512 + g * 128:512 + (g + 1) * 128], PM[:, g * 384 + 256:g * 384 + 384], False, True, [], g % 2 == 1)
                if g % 2:
                    e = av(DT[:, (g // 2) * 512:(g // 2) * 512 + 512], PS[:, b, :], ACT.Copy, [t, t_i, fr])
                    BF[b] = e
            for g in range(4):
                b = 2 + g // 2
                t = mm(PS[:, b, (g % 2) * 256:(g % 2) * 256 + 256], WP[:, g * 128:(g + 1) * 128], DT[:, g * 256:(g + 1) * 256],
                       True, True, [e, BF[b]], True)
            t_pool = t
            rdy2 = []
            for g in range(4):
                b = 2 + g // 2
                y = PS[:, b, (g % 2) * 256:(g % 2) * 256 + 256]
                hi, lo = AHI[:, g * 256:(g + 1) * 256], ALO[:, g * 256:(g + 1) * 256]
                sc = PSC[:, l * 4 + g:l * 4 + g + 1]
                if g == 0:
                    for g_ in range(4):
                        a = av(AHI[:, g_ * 256:(g_ + 1) * 256], PS[:, 2 + g_ // 2, (g_ % 2) * 256:(g_ % 2) * 256 + 256], ACT.Copy,
                               [t, free["a"], m_pet], scale=PSC[:, l * 4 + g_:l * 4 + g_ + 1])
                d = stt(lo, y, sc, hi.bitcast(F32), ALU.mult, ALU.subtract, [a, free["a"]])
                BF[b] = d
                rdy2.append(d)

            units, tl = [], []

            def unit(m, g):
                w = 128 * (m + 1)

                def scores(b):
                    for i in range(4):
                        r = slice((i % 2) * 64, (i % 2) * 64 + 64)
                        c = (i // 2) * 256
                        t = mm(PS[:, b + i % 2, c:c + w], qT[r, 2 * g + i // 2, m * 128:(m + 1) * 128],
                               kT[r, 2 * g + i // 2, 0:w], True, True, [qt, kt_, BF[b + i % 2]], i == 3)
                    return t

                def shift(b, P, marks):
                    bi = PSC2[:, m * 128:m * 128 + w]
                    for i in range(2):
                        sv = PS[:, b + i, :].rearrange("p (a n) -> p a n", a=2)[:, :, 0:w]
                        d = stt(P[:, 2 * i:2 * i + 2, 0:w], sv, 0.125, bm(bi, 2), ALU.mult, ALU.add, [marks, sel[m]])
                    return d

                def values(s, PT, evs, em):
                    d2 = rcp(den[:, 4 * s:4 * s + 4], den[:, 4 * s:4 * s + 4], [em])
                    for i in range(4):
                        h = 4 * g + 2 * (i % 2) + i // 2
                        for k in range(m + 1):
                            t = mm(PS[:, 2, s * 256 + i * 64:s * 256 + (i + 1) * 64], PT[:, (k * 4 + i) * 128:(k * 4 + i + 1) * 128],
                                   V[:, k * 512 + h * 64:k * 512 + (h + 1) * 64], k == 0, k == m,
                                   [evs, vm, BF[2]], i == 3 and k == m)
                    x0 = m * DM + 512 + g * 256
                    xo = XN[:, x0:x0 + 256].rearrange("p (a b d) -> p b a d", a=2, b=2)
                    ov = PS[:, 2, s * 256:(s + 1) * 256].rearrange("p (b a d) -> p b a d", b=2, a=2)
                    dn = den[:, 4 * s:4 * s + 4].rearrange("p (b a) -> p b a", a=2)
                    d = tt(xo, ov, bc(dn, 64), ALU.mult, [t, d2, rope_pool, free["xn"]])
                    BF[2] = d
                    tl.append(d)
                    return t

                units.append({"scores": scores, "shift": shift, "values": values, "scale": 1.0, "w": w,
                              "old": [t_pool, t_q, t_k, sc_m]})

            for m in range(2):
                for g in range(2):
                    unit(m, g)
            tf = run_units(units, P2, PT2, [])
            e, t = to_halves(0, 1, AHI, ALO, tl[1], free["a"], 0)

            def last_tile():
                ew, tw = to_halves(1, 1, AHI, ALO, tl[3], free["a"], 1)
                wrdy[2] = wrdy[3] = ew
                free["xn"] = tw

            wrdy = [rdy2[3], rdy2[3], None, None]
            y = eight("w_out2", AHI, ALO, wrdy, (0, 1, 2, 3), {0: last_tile})
            free["region"] = [tf, t_pool, wrdy[2], free["xn"], e]
            free["a"] = y[1]
            return post_norm(y, 1.0)

        rope_last = [None]
        free["region"] = [m_rope, m_pet, (pe.sem, pe.n)]
        xm = m_x
        for l in range(2):
            xm = ffn(xm, "swiglu")
            y = hybrid(l, xm)
            xm = memory(l, post_norm(y, 1.0))
            xm = ffn(xm, "swiglu")
        for l in range(2):
            xm = sparse(l, xm)
            xm = ffn(xm, "relu2")
        for m in range(2):
            sp.load(lambda e, m=m: e.dma_start(out[0, m * 128:(m + 1) * 128, :], X[:, m * DM:(m + 1) * DM]), [xm[m]], s_out, 0)
        sp.wait([(s_out, 32)])
        assert at["use"] == len(items) and gst["use"] == len(gains)

        block = ctx.enter_context(nc.Block())

        @block.sync
        def _(e):
            sp.play(e)

        @block.gpsimd
        def _(e):
            pool.play(e)

        @block.scalar
        def _(e):
            act.play(e)

        @block.vector
        def _(e):
            dve.play(e)

        @block.tensor
        def _(e):
            pe.play(e)


_INS = ["x", "mem", "ffn1_pre_g", "ffn1_w_gate", "ffn1_w_up", "ffn1_w_down", "ffn1_post_g", "mix_pre_g", "w_in",
        "cmp_pe", "cmp_w1", "cmp_w2", "nsa_out_g", "ret_gn_g", "w_out", "mix_post_g", "xa_pre_g", "xa_mem_g", "xa_wq",
        "xa_wk", "xa_wv", "xa_wo", "xa_post_g", "ffn2_pre_g", "ffn2_w_gate", "ffn2_w_up", "ffn2_w_down",
        "ffn2_post_g", "positions_2", "g_pre_mix_2", "w_in_2", "w_pool_2", "pool_scale_2", "w_out_2",
        "g_post_mix_2", "g_pre_ffn_2", "w_ff1_2", "w_ff2_2", "g_post_ffn_2"]


def kernel(**inputs):
    import concourse.bacc as bacc
    from concourse.bass_utils import run_bass_kernel_spmd as run

    nc = bacc.Bacc("TRN2", target_bir_lowering=False, num_devices=1)
    arrays, aps = {}, {}
    for name in _INS:
        arrays[name] = np.ascontiguousarray(inputs[name])
    arrays.update(constants())
    for name, a in arrays.items():
        aps[name] = nc.dram_tensor(name, a.shape, mybir.dt.from_np(a.dtype), kind="ExternalInput").ap()
    out = nc.dram_tensor("out", (1, T, DM), F32, kind="ExternalOutput").ap()
    build(nc, aps, out)
    r = run(nc, [arrays], core_ids=[0])
    return r.results[0]["out"]
```

```python
from contextlib import ExitStack

import numpy as np

import concourse.bass as bass
from concourse import mybir

F32 = mybir.dt.float32
F32R = mybir.dt.float32r
I32 = mybir.dt.int32
ALU = mybir.AluOpType
ACT = mybir.ActivationFunctionType
AX = mybir.AxisListType

T = 256
DM = 1024
EPS = 1e-6
BIG = 1e32
NEG = -1e30
TAKEN = -3.0e38
TWO_PI = 6.283185307179586
PI_A = 6.28125
PI_B = 0.0019340515136718750
PI_C = TWO_PI - PI_A - PI_B
ROUND = 12582912.0
SLOPES = [2.0 ** -(h + 1) for h in range(8)]
POOL_WINDOWS = (2, 4, 8, 16)

NRAW = 4
NSPLIT = 3
AHEAD = 2
NG = 2
NREG = 13248
WARM_A = 5
WARM_B = 2
BEFORE = 1
PACE = [1] * 8 + [2] + [1] * 2 + [2] + [1] * 4
RET_AT = ((0, 0), (4, 1), (6, 2))
BEFORE2 = 0
PACE2 = [2] + [1] * 7


class Engine:

    def __init__(self, sem, chained=False):
        self.sem = sem
        self.chained = chained
        self.n = 0
        self.steps = []
        self.met = {}

    def wait(self, marks):
        for m in marks:
            if m is None:
                continue
            if isinstance(m, list):
                self.wait(m)
                continue
            sem, value = m
            if self.met.get(sem.name, 0) < value:
                self.met[sem.name] = value
                self.steps.append((0, sem, value))

    def add(self, fn, marks, counted=True):
        self.wait(marks)
        if self.chained and self.n:
            self.wait([(self.sem, self.n)])
        if counted:
            self.n += 1
        self.steps.append((1 if counted else 2, fn, None))
        return (self.sem, self.n) if counted else None

    def load(self, fn, marks, sem, value):
        self.wait(marks)
        self.steps.append((3, fn, sem))
        return (sem, value)

    def play(self, e):
        for kind, a, b in self.steps:
            if kind == 0:
                e.wait_ge(a, b)
            elif kind == 1:
                a(e).then_inc(self.sem, 1)
            elif kind == 2:
                a(e)
            else:
                a(e).then_inc(b, 16)


def constants():
    t = np.arange(T)
    dist = (t[:, None] - t[None, :]).astype(np.float64)
    d = np.where(dist >= 0, -dist, -BIG)
    alibi = np.concatenate([d[0:128, 0:128], d[128:256, :]], axis=1)
    ident = np.eye(128)
    start = np.arange(15) * 16
    mid = start + 15.5
    end = start + 31
    ok = end[None, :] <= t[:, None]
    cb = -np.asarray(SLOPES)[None, :, None] * (t[:, None, None] - mid[None, None, :])
    cb = np.where(ok[:, None, :], cb, NEG)
    cb = cb.reshape(2, 128, 120).transpose(1, 0, 2).reshape(128, 240)
    cm = np.broadcast_to(ok[:, None, :], (T, 8, 15)).astype(np.float64)
    cm = cm.reshape(2, 128, 120).transpose(1, 0, 2).reshape(128, 240)
    chunk = t // 64
    ch = np.where(chunk[None, :] <= chunk[:, None], 0.0, NEG)
    ch = np.concatenate([ch[0:128, 0:128], ch[128:256, :]], axis=1)
    half = np.arange(8)
    inv = np.broadcast_to((500000.0 ** (-half.astype(np.float32) / np.float32(8))).astype(np.float64), (128, 8))
    small = np.concatenate([ident, alibi, cb, cm, ch, inv], axis=1).astype(np.float32)
    dec = []
    for h in range(4):
        g = 1.0 - 2.0 ** (-5.0 - h)
        w = np.where(dist >= 0, g ** np.maximum(dist, 0.0), 0.0) * 128.0 ** -0.5
        dec.append(w.T)
    dec = np.stack(dec)
    decay = np.concatenate(
        [dec[:, 0:128, :].transpose(1, 0, 2).reshape(128, 1024), dec[:, 128:256, 128:256].transpose(1, 0, 2).reshape(128, 512)],
        axis=1,
    ).astype(np.float32)
    pm = []
    for w in POOL_WINDOWS:
        cnt = np.minimum(t + 1, w)[:, None]
        m = np.where((dist >= 0) & (dist < w), 1.0 / cnt, 0.0) - np.eye(T)
        m = m.T
        pm.append(np.concatenate([m[0:128, :], m[128:256, 128:256]], axis=1))
    pool = np.concatenate(pm, axis=1).astype(np.float32)
    return {"c_small": small, "c_decay": decay, "c_pool": pool}


def build(nc, A, out):
    ctx = ExitStack()
    with ctx:
        def sb(name, n, dt=F32):
            return ctx.enter_context(nc.sbuf_tensor(name, [128, n], dt))

        def sem(name):
            return ctx.enter_context(nc.semaphore(name))

        RAW = sb("raw", NRAW * 2048)
        WHI = sb("whi", NSPLIT * 2048, F32R)
        WLO = sb("wlo", NSPLIT * 2048, F32R)
        X = sb("xs", 2 * DM)
        GV = sb("gv", NG * DM)
        XN = sb("xn", 2 * DM)
        AHI = sb("ahi", 8 * T, F32R)
        ALO = sb("alo", 8 * T, F32R)
        MHI = sb("mhi", 8 * T, F32R)
        MLO = sb("mlo", 8 * T, F32R)
        HHI = sb("hhi", 2 * 512, F32R)
        HLO = sb("hlo", 2 * 512, F32R)
        CS = sb("cs", 992)
        W2C = sb("w2c", 512)
        SM = sb("sm", 400)
        R = sb("region", NREG)
        PS = ctx.enter_context(nc.psum_tensor("ps", [128, 8, 512], F32))

        pe, sp = Engine(sem("s_pe")), Engine(sem("s_sp"))
        act, dve, pool = [Engine(sem(n), True) for n in ("s_act", "s_dve", "s_pool")]
        s_raw = [sem(f"s_raw{i}") for i in range(NRAW)]
        s_gv = [sem(f"s_gv{i}") for i in range(NG)]
        s_c = [sem(f"s_c{i}") for i in range(9)]
        s_aux = [sem(f"s_aux{i}") for i in range(3)]
        s_out = sem("s_out")

        def mm(o, l, r, start, stop, w=(), inc=False):
            return pe.add(lambda e: e.matmul(o, l, r, start=start, stop=stop), w, inc)

        def tr(o, i, idn, w=(), inc=False):
            return pe.add(lambda e: e.transpose(o, i, idn), w, inc)

        def av(o, i, f, w=(), **kw):
            return act.add(lambda e: e.activation(o, i, f, **kw), w)

        def tt(o, a, b, op, w=(), q=None):
            return (q or dve).add(lambda e: e.tensor_tensor(o, a, b, op), w)

        def ts(o, a, s1, s2, op0, op1=ALU.bypass, w=(), q=None):
            return (q or dve).add(lambda e: e.tensor_scalar(o, a, s1, s2, op0, op1), w)

        def stt(o, a, s, b, op0, op1, w=()):
            return dve.add(lambda e: e.scalar_tensor_tensor(o, a, s, b, op0, op1), w)

        def cp(o, a, w=(), q=None):
            return (q or dve).add(lambda e: e.tensor_copy(o, a), w)

        def red(o, a, op, w=()):
            return dve.add(lambda e: e.tensor_reduce(o, a, AX.X, op), w)

        def rcp(o, a, w=()):
            return dve.add(lambda e: e.reciprocal(o, a), w)

        def bc(ap, n):
            return ap.unsqueeze(len(ap.shape)).broadcast_to(list(ap.shape) + [n])

        def bm(ap, n):
            return ap.unsqueeze(1).broadcast_to([ap.shape[0], n, ap.shape[1]])

        IDN = CS[:, 0:128]
        ALIBI = CS[:, 128:512]
        CB = CS[:, 512:752].rearrange("p (m c) -> p m c", m=2)
        CM = CS[:, 752:992].rearrange("p (m c) -> p m c", m=2)
        small = sb("small2", 392 + 8 + 32)
        CH = small[:, 0:384]
        INV = small[:, 384:392]
        COS = small[:, 400:416]
        SIN = small[:, 416:432]
        PET = SM[:, 0:64]
        PSC = SM[:, 64:72]
        st = SM[:, 80:400]
        ssq = st[:, 0:4]
        var = st[:, 4:6]
        rstd = st[:, 6:8]
        mx = st[:, 8:16]
        nb = st[:, 16:24]
        den = st[:, 24:32]
        coef = st[:, 32:40]
        gates = st[:, 40:88].rearrange("p (m c) -> p m c", m=2)
        top8 = st[:, 88:96]
        rsum = st[:, 300:308]
        rvar = st[:, 308:316]
        iw = st[:, 104:120].rearrange("p (m c) -> p m c", m=2)
        kcT = st[:, 120:136]
        vcR = st[:, 136:264]
        posf = st[:, 264:266]
        ang = st[:, 268:284]
        nrd = st[:, 284:300]
        MHALF = st[:, 96:104]
        PSC2 = sb("pc", 384)
        PC = PSC2[:, 0:256]
        SC = PSC2[:, 256:384]

        BF = [None] * 8

        items = []

        def item(tag, src, k, n):
            items.append((tag, src, k, n))

        def rows(w, k0, k1, c0, c1):
            return w[k0 * 128:k1 * 128, c0:c1].rearrange("(k p) n -> p k n", p=128)

        def plan():
            for l in range(2):
                for f in ("ffn1", "ffn2"):
                    g, u, d = A[f + "_w_gate"][l, :, :], A[f + "_w_up"][l, :, :], A[f + "_w_down"][l, :, :]
                    for j in range(12):
                        if j < 11:
                            item("gate", rows(g, 0, 8, 256 * j, 256 * j + 256), 8, 256)
                            item("up", rows(u, 0, 8, 256 * j, 256 * j + 256), 8, 256)
                        if 1 <= j < 10:
                            item("down", rows(d, 2 * j - 2, 2 * j, 0, 1024), 2, 1024)
                    for j in range(9, 11):
                        item("down", rows(d, 2 * j, 2 * j + 2, 0, 1024), 2, 1024)
                    if f == "ffn2":
                        continue
                    wi = A["w_in"][l, :, :]
                    for c in range(2):
                        item("v_r", rows(wi, 4 * c, 4 * c + 4, 2328, 2840), 4, 512)
                    item("cmp", rows(wi, 0, 8, 512, 768), 8, 256)
                    for c in range(2):
                        item("q_n", (wi, c), 8, 256)
                    item("gates", rows(wi, 0, 8, 1280, 1408), 8, 128)
                    for c in range(2):
                        item("q_r", rows(wi, 0, 8, 1304 + 256 * c, 1560 + 256 * c), 8, 256)
                    for c in range(2):
                        item("k_r", rows(wi, 0, 8, 1816 + 256 * c, 2072 + 256 * c), 8, 256)
                    item("slc", rows(wi, 0, 8, 768, 1024), 8, 256)
                    for c in range(2):
                        item("g_r", rows(wi, 4 * c, 4 * c + 4, 2840, 3352), 4, 512)
                    item("win", rows(wi, 0, 8, 1024, 1280), 8, 256)
                    for c in range(4):
                        item("wk", rows(A["xa_wk"][l, :, :], 0, 8, 256 * c, 256 * c + 256), 8, 256)
                    for n in range(2):
                        for c in range(2):
                            item("wv", rows(A["xa_wv"][l, :, :], 4 * c, 4 * c + 4, 512 * n, 512 * n + 512), 4, 512)
                    for c in (2, 3, 0, 1):
                        item("w_out", rows(A["w_out"][l, :, :], 2 * c, 2 * c + 2, 0, 1024), 2, 1024)
                    for c in range(4):
                        item("wq", rows(A["xa_wq"][l, :, :], 0, 8, 256 * c, 256 * c + 256), 8, 256)
                    for c in range(4):
                        item("wo", rows(A["xa_wo"][l, :, :], 2 * c, 2 * c + 2, 0, 1024), 2, 1024)
            for l in range(2):
                wi = A["w_in_2"][l, :, :]
                for tag, c0, n in (("q", 512, 512), ("iq", 2048, 292), ("iq", 2340, 292), ("k", 1024, 512), ("v", 1536, 512), ("u", 0, 512)):
                    for s in range(2):
                        item(tag, rows(wi, 4 * s, 4 * s + 4, c0, c0 + n), 4, n)
                for c in range(4):
                    item("w_out2", rows(A["w_out_2"][l, :, :], 2 * c, 2 * c + 2, 0, 1024), 2, 1024)
                f1, f2 = A["w_ff1_2"][l, :, :], A["w_ff2_2"][l, :, :]
                for j in range(18):
                    if j < 16:
                        item("ff1", rows(f1, 0, 8, 256 * j, 256 * j + 256), 8, 256)
                    if j >= 2:
                        item("ff2", rows(f2, 2 * j - 4, 2 * j - 2, 0, 1024), 2, 1024)

        plan()

        places = [(WHI[:, i * 2048:(i + 1) * 2048], WLO[:, i * 2048:(i + 1) * 2048]) for i in range(NSPLIT)]
        places.append((MHI[:, :], MLO[:, :]))
        place, before = [], []
        taken = [None] * (NSPLIT + 1)
        own, outs_seen = False, 0
        for i, it in enumerate(items):
            if it[0] == "q_r" and not own:
                own, outs_seen = True, 0
            if own and it[0] == "w_out":
                outs_seen += 1
                own = outs_seen < 3
            n = min(range(NSPLIT if own else NSPLIT + 1), key=lambda p: -1 if taken[p] is None else taken[p])
            place.append(n)
            before.append(taken[n])
            taken[n] = i
        landed = {}
        halves = {}
        free_raw = {}
        free_half = {}
        at = {"load": 0, "split": 0, "use": 0}
        free = {"region": None, "xn": None, "a": [None, None], "m": None, "h0": None, "h1": None}

        def load_more(upto=None):
            while at["load"] < (upto or len(items)):
                i = at["load"]
                if i >= NRAW and i - NRAW not in free_raw:
                    return
                tag, src, k, n = items[i]
                dst = RAW[:, (i % NRAW) * 2048:(i % NRAW) * 2048 + k * n].rearrange("p (k n) -> p k n", k=k)
                w = free_raw.get(i - NRAW)
                if tag == "q_n":
                    wi, c = src
                    for f in range(2):
                        for a in range(2):
                            c0 = 256 * a + 128 * c + 64 * f
                            o = dst[:, :, f * 128 + a * 64:f * 128 + a * 64 + 64]
                            s = rows(wi, 0, 8, c0, c0 + 64)
                            sp.load(lambda e, o=o, s=s: e.dma_start(o, s), [w], s_raw[i % NRAW], 0)
                    uses[i % NRAW] += 64
                else:
                    sp.load(lambda e, o=dst, s=src: e.dma_start(o, s), [w], s_raw[i % NRAW], 0)
                    uses[i % NRAW] += 16
                landed[i] = (s_raw[i % NRAW], uses[i % NRAW])
                at["load"] += 1

        uses = [0] * NRAW

        def split_more(upto):
            while at["split"] <= min(upto, len(items) - 1):
                i = at["split"]
                tag, src, k, n = items[i]
                load_more()
                raw = RAW[:, (i % NRAW) * 2048:(i % NRAW) * 2048 + k * n]
                hi, lo = [x[:, 0:k * n] for x in places[place[i]]]
                used = [None if before[i] is None else free_half[before[i]], free["m"] if place[i] == NSPLIT else None]
                for c in (slice(0, k * n // 2), slice(k * n // 2, k * n)):
                    a = av(hi[:, c], raw[:, c], ACT.Copy, [landed[i], used])
                    halves[i] = tt(lo[:, c], raw[:, c], hi[:, c].bitcast(F32), ALU.subtract, [landed[i], a])
                free_raw[i] = [halves[i]]
                at["split"] += 1
            load_more()

        def take(tag, ahead=AHEAD):
            i = at["use"]
            assert items[i][0] == tag, (items[i][0], tag)
            at["use"] += 1
            split_more(i + ahead)
            k, n = items[i][2:4]
            hi, lo = [x[:, 0:k * n] for x in places[place[i]]]
            return hi.rearrange("p (k n) -> p k n", k=k), lo.rearrange("p (k n) -> p k n", k=k), halves[i], i

        def done(i, mark):
            free_half[i] = mark

        gains = []

        def gain_plan():
            def g(v):
                gains.append([(0, v)])
            for l in range(2):
                for n in ("ffn1_pre_g", "ffn1_post_g", "mix_pre_g"):
                    g(A[n][l, :])
                g(A["xa_mem_g"][l, :])
                gains.append([(0, A["ret_gn_g"][l, :]), (512, A["nsa_out_g"][l, :])])
                for n in ("mix_post_g", "xa_pre_g", "xa_post_g", "ffn2_pre_g", "ffn2_post_g"):
                    g(A[n][l, :])
            for l in range(2):
                for n in ("g_pre_mix_2", "g_post_mix_2", "g_pre_ffn_2", "g_post_ffn_2"):
                    g(A[n][l, :])

        gain_plan()
        gst = {"load": 0, "use": 0}
        guse = [0] * NG
        gfree = {}
        gmark = {}

        def gain_loads():
            while gst["load"] < len(gains):
                i = gst["load"]
                if i >= NG and i - NG not in gfree:
                    return
                s = i % NG
                for off, v in gains[i]:
                    n = v.shape[0]
                    o = GV[:, s * DM + off:s * DM + off + n]
                    pool.load(lambda e, o=o, v=v: e.dma_start(o, v.partition_broadcast(128)), [gfree.get(i - NG)], s_gv[s], 0)
                    guse[s] += 16
                gmark[i] = (s_gv[s], guse[s])
                gst["load"] += 1

        def gain():
            i = gst["use"]
            gst["use"] += 1
            return GV[:, (i % NG) * DM:(i % NG) * DM + DM], gmark[i], i

        def gain_done(i, mark):
            gfree[i] = mark
            gain_loads()

        def cload(k, o, s):
            return sp.load(lambda e: e.dma_start(o, s), [], s_c[k], 16)

        c_small = A["c_small"]
        def xload(m):
            a = cload(1 + m, X[:, m * DM:(m + 1) * DM], A["x"][0, m * 128:(m + 1) * 128, :])
            return [a, a]

        m_x = [xload(0)]
        m_cs = cload(0, CS[:, 0:128], c_small[:, 0:128])
        load_more(2)
        m_x.append(xload(1))
        load_more()
        m_mh = pool.add(lambda e: e.memset(MHALF, -0.5), [])
        gain_loads()

        def qload(k, o, s):
            return pool.load(lambda e: e.dma_start(o, s), [], s_c[k], 16)

        pe_in = R[0:64, 7168:7296]
        ps_in = R[0:8, 7296:7424]
        pos_in = R[0:2, 7424:7552].bitcast(I32)
        pos_row = R[0:2, 7552:7680]
        pe.wait([m_cs])
        S_EPS = EPS

        def keep_warm(n, bank):
            for _ in range(n):
                mm(PS[:, bank, 0:128], IDN, IDN, True, True, [BF[bank]])

        def to_halves(m, half, hi_t, lo_t, src_mark, old, bank, cols=None):
            t = turn_half(m, half, src_mark, bank)
            return split_of(m, half, t, hi_t, lo_t, old, bank), t

        def turn_half(m, half, src_mark, bank):
            for k in range(4):
                c = m * DM + (half * 4 + k) * 128
                t = tr(PS[:, bank, k * 128:(k + 1) * 128], XN[:, c:c + 128], IDN, [src_mark, BF[bank]], k == 3)
            return t

        def split_of(m, half, t, hi_t, lo_t, old, bank):
            v = PS[:, bank, :].rearrange("p (k n) -> p k n", k=4)
            hi = hi_t[:, :].rearrange("p (k n) -> p k n", k=8)[:, half * 4:half * 4 + 4, m * 128:(m + 1) * 128]
            lo = lo_t[:, :].rearrange("p (k n) -> p k n", k=8)[:, half * 4:half * 4 + 4, m * 128:(m + 1) * 128]
            a = av(hi, v, ACT.Copy, [t, old])
            d = tt(lo, v, hi.bitcast(F32), ALU.subtract, [a, t, old])
            BF[bank] = d
            return d

        SQ = R[:, 6144:7168]


        def half_root(m, w, times=1.0):
            v = var[:, m:m + 1]
            a = ts(v, ssq[:, 2 * m:2 * m + 1], ssq[:, 2 * m + 1:2 * m + 2], times ** -2.0 * S_EPS, ALU.add, ALU.add, [w])
            return tt(rstd[:, m:m + 1], v, MHALF[:, 0:1], ALU.pow, w=[a, m_mh], q=pool)

        def mean_root(dst, s, n, w, times=1.0):
            k = times ** -2.0
            a = ts(var[:, 0:1] if dst.shape[1] == 1 else rvar, s, k / n, k * S_EPS, ALU.mult, ALU.add, [w])
            n1 = dst.shape[1]
            return tt(dst, var[:, 0:1] if n1 == 1 else rvar, MHALF[:, 0:n1], ALU.pow, w=[a, m_mh], q=pool)

        def post_parts(y, times):
            g, mg, gi = gain()
            old = free["xn"]
            q, d, root = {}, {}, {}

            def square(m, h, w):
                q[m, h] = av(SQ[:, h * 512:h * 512 + 512], PS[:, 4 + 2 * m + h, :], ACT.Square, [w, free["region"]],
                             scale=1.0 / (32.0 * times), accum_out=ssq[:, 2 * m + h:2 * m + h + 1])

            def weigh(m, h, w):
                c = slice(m * DM + h * 512, m * DM + h * 512 + 512)
                d[m, h] = tt(XN[:, c], PS[:, 4 + 2 * m + h, :], g[:, h * 512:h * 512 + 512], ALU.mult, [w, mg, old])

            def first(m):
                square(m, 0, y[m])
                weigh(m, 1, y[m])
                square(m, 1, d[m, 1])

            def second(m):
                weigh(m, 0, q[m, 0])
                root[m] = half_root(m, q[m, 1], times)
                BF[4 + 2 * m] = d[m, 0]
                BF[5 + 2 * m] = q[m, 1]

            def third(m):
                o = []
                for h in range(2):
                    c = slice(m * DM + h * 512, m * DM + h * 512 + 512)
                    o.append(stt(X[:, c], XN[:, c], rstd[:, m:m + 1], X[:, c], ALU.mult, ALU.add, [d[m, 0], d[m, 1], root[m]]))
                return o

            return first, second, third, lambda: gain_done(gi, d[1, 0])

        def post_norm(y, times):
            first, second, third, finish = post_parts(y, times)
            out = []
            for m in range(2):
                first(m)
                second(m)
                out.append(third(m))
            finish()
            return out

        def turn_over(prev, product):
            y, times = prev
            if times is None:
                xm = {0: y[0], 1: y[1]}
            else:
                xm = {}
                first, second, third, finish = post_parts(y, times)
                first(0)
                second(0)
                xm[0] = third(0)
            g, mg, gi = gain()
            oldxn = free["xn"]

            def row_root(m):
                for h in range(2):
                    c = slice(h * 512, h * 512 + 512)
                    q = av(SQ[:, c], X[:, m * DM + h * 512:m * DM + h * 512 + 512], ACT.Square, [xm[m][h], free["region"]],
                           scale=1.0 / 32, accum_out=ssq[:, 2 * m + h:2 * m + h + 1])
                return half_root(m, q)

            def normed(m, r):
                out = []
                for h in range(2):
                    c = slice(m * DM + h * 512, m * DM + h * 512 + 512)
                    out.append(stt(XN[:, c], X[:, c], rstd[:, m:m + 1], g[:, h * 512:h * 512 + 512], ALU.mult, ALU.mult,
                                   [r, mg, oldxn]))
                return out

            def turn_of(m, half, x):
                return turn_half(m, half, x[half], 2 * m + half)

            def halves_of(m, half, x):
                return to_halves(m, half, AHI, ALO, x[half], free["a"][m], 2 * m + half)

            root = row_root(0)
            if times is not None:
                first(1)
                keep_warm(WARM_A, 3)
            x = normed(0, root)
            if times is None:
                split_more(0)
            h0, _ = halves_of(0, 0, x)
            if times is not None:
                second(1)
            h1, _ = halves_of(0, 1, x)
            keep_warm(WARM_B, 3)
            product(0, (h0, h1), 0)
            if times is not None:
                xm[1] = third(1)
            x = normed(1, row_root(1))
            last = turn_of(1, 0, x)
            t = turn_of(1, 1, x)
            product(0, None, 1)
            h0 = split_of(1, 0, last, AHI, ALO, free["a"][1], 2)
            h1 = split_of(1, 1, t, AHI, ALO, free["a"][1], 3)
            free["xn"] = t
            split_more(at["use"])
            product(1, (h0, h1), 0)
            product(1, None, 1)
            if times is not None:
                finish()
            gain_done(gi, x[1])
            return [h0, h1]

        def up(tag, bank, rdy, hi_t=AHI, lo_t=ALO, n=2):
            hi, lo, mark, i = take(tag)
            for f in range(n):
                t = up_tile(hi, lo, mark, f, bank, f, rdy, hi_t, lo_t)
            done(i, t)
            return t

        def up_tile(hi, lo, mark, f, bank, half, rdy, hi_t, lo_t):
            xh = hi_t[:, :].rearrange("p (k n) -> p k n", k=8)
            xl = lo_t[:, :].rearrange("p (k n) -> p k n", k=8)
            o = PS[:, bank, half * 256:(half + 1) * 256]
            for k in range(8):
                for s, (w, x) in enumerate(((hi, xh), (hi, xl), (lo, xh))):
                    t = mm(o, w[:, k, f * 128:(f + 1) * 128], x[:, k, :], k == 0 and s == 0, k == 7 and s == 2,
                           [mark, rdy[k // 4], BF[bank]], k == 7 and s == 2)
            return t

        def down_part(w, rdy, act_, m, kk, start, stop, inc):
            hi, lo, mark, _ = w
            ah, al = act_
            lh = ah[:, kk, m * 128:(m + 1) * 128]
            ll = al[:, kk, m * 128:(m + 1) * 128]
            for n in range(2):
                b = 4 + 2 * m + n
                for s, (x, v) in enumerate(((lh, hi), (lh, lo), (ll, hi))):
                    t = mm(PS[:, b, :], x, v[:, kk, n * 512:(n + 1) * 512], start and s == 0, stop and s == 2,
                           [mark, rdy, BF[b]], inc and n == 1 and s == 2)
            return t

        def down(tag, rdy, act_, first):
            w = take(tag)
            for m in range(2):
                for kk in range(2):
                    t = down_part(w, rdy, act_, m, kk, first and kk == 0, False, m == 1 and kk == 1)
            done(w[3], t)
            return t

        def last_downs(tag, rdy, acts, order, hooks={}):
            w = [take(tag) for _ in rdy]
            out = []
            for n, (i, m, kk) in enumerate(order):
                if n in hooks:
                    hooks[n]()
                t = down_part(w[i], rdy[i][m], acts[i], m, kk, False, i == 1 and kk == 1, kk == 1)
                if m == 1 and kk == 1:
                    done(w[i][3], t)
                if i == 1 and kk == 1:
                    out.append(t)
            return out

        EVEN = ((0, 0, 0), (0, 0, 1), (1, 0, 0), (1, 0, 1), (0, 1, 0), (0, 1, 1), (1, 1, 0), (1, 1, 1))

        def natural(tag, banks, rdy, n=512):
            xh = AHI[:, :].rearrange("p (k n) -> p k n", k=8)
            xl = ALO[:, :].rearrange("p (k n) -> p k n", k=8)
            for c in range(2):
                hi, lo, mark, i = take(tag)
                for kk in range(4):
                    k = 4 * c + kk
                    for m in range(2):
                        ms = slice(m * 128, (m + 1) * 128)
                        for s, (x, w) in enumerate(((xh, hi), (xh, lo), (xl, hi))):
                            t = mm(PS[:, banks[m], 0:n], x[:, k, ms], w[:, kk, :], k == 0 and s == 0, k == 7 and s == 2,
                                   [mark, rdy[c], BF[banks[m]]], kk == 3 and m == 1 and s == 2)
                done(i, t)
            return t

        def token_product(tags, by_k, n=256):
            w = []
            xh = AHI[:, :].rearrange("p (k n) -> p k n", k=8)
            xl = ALO[:, :].rearrange("p (k n) -> p k n", k=8)
            marks = []

            ready = {}

            def product(m, rdy, part):
                if rdy is not None:
                    ready[m] = rdy
                if not w:
                    w.extend([take(tags[0], 1), take(tags[1], 0)])
                ms = slice(m * 128, (m + 1) * 128)
                for i, (hi, lo, mark, num) in enumerate(w):
                    o = PS[:, m, 0:n] if by_k else PS[:, m, i * 256:(i + 1) * 256]
                    nk = hi.shape[1]
                    cut_ = nk - nk // 4
                    for kk in range(nk):
                        if (i == 1 and kk >= cut_) != (part == 1):
                            continue
                        k = 4 * i + kk if by_k else kk
                        for s, (x, v) in enumerate(((xh, hi), (xh, lo), (xl, hi))):
                            t = mm(o, x[:, k, ms], v[:, kk, :], k == 0 and s == 0, k == 7 and s == 2,
                                   [mark, ready[m][k // 4], BF[m]], kk == nk - 1 and s == 2)
                    if m == 1 and part == i:
                        done(num, t)
                if part == 1:
                    marks.append(t)

            return product, marks

        def turned(src, bank, marks, f0):
            for f in range(2):
                for m in range(2):
                    t = tr(PS[:, bank, f * 256 + m * 128:f * 256 + (m + 1) * 128], src[:, m, (f0 + f) * 128:(f0 + f + 1) * 128], IDN,
                           [marks, BF[bank]], f == 1 and m == 1)
            return t

        def eight(tag, bh, bl, rdy, order=(0, 1, 2, 3), between=None, hooks={}):
            hv = bh[:, :].rearrange("p (k n) -> p k n", k=8)
            lv = bl[:, :].rearrange("p (k n) -> p k n", k=8)
            acts = [(hv[:, 2 * c:2 * c + 2, :], lv[:, 2 * c:2 * c + 2, :]) for c in range(4)]
            for n, c in enumerate(order[:2]):
                down(tag, rdy[c][1], acts[c], n == 0)
                if n == 1:
                    split_more(at["use"] + 2)
                if between and n in between:
                    between[n]()
            return last_downs(tag, [rdy[c] for c in order[2:]], [acts[c] for c in order[2:]], EVEN, hooks)

        def ffn(prev, kind, beside={}):
            relu = kind == "relu2"
            nj, lag = (16, 2) if relu else (11, 1)
            H = R[:, 0:1024].rearrange("p (s n) -> p s n", s=2)
            G = R[:, 1024:3072].rearrange("p (s n) -> p s n", s=4)
            HN = R[:, 3072:4096].rearrange("p (m n) -> p m n", m=2)
            HH = [HHI[:, i * 512:(i + 1) * 512] for i in range(2)]
            HL = [HLO[:, i * 512:(i + 1) * 512] for i in range(2)]
            halves_h = [[x[i][:, :].rearrange("p (k n) -> p k n", k=2) for x in (HH, HL)] for i in range(2)]
            hfree = [free["h0"], free["h1"]]
            product, tm = token_product(("ff1", "ff1") if relu else ("gate", "up"), False)
            rdy = turn_over(prev, product)
            fr = free["region"]
            hm, hn = {}, []
            for m in range(2):
                if relu:
                    a = av(G[:, m, :], PS[:, m, :], ACT.Relu, [tm[m], fr])
                    d = tt(HN[:, m, :], G[:, m, :], PS[:, m, :], ALU.mult, [a])
                else:
                    a = av(G[:, m, 0:256], PS[:, m, 0:256], ACT.Tanh, [tm[m], fr], scale=0.5)
                    d = stt(G[:, 2 + m, 0:256], G[:, m, 0:256], 1.0, PS[:, m, 0:256], ALU.add, ALU.mult, [a])
                    d = stt(HN[:, m, 0:256], G[:, 2 + m, 0:256], 0.5, PS[:, m, 256:512], ALU.mult, ALU.mult, [d])
                BF[m] = d
                hn.append(d)

            def first_hidden(i):
                t = turned(HN, i, hn, 2 * i)
                a = av(HH[i], PS[:, i, :], ACT.Copy, [t, hfree[i]])
                BF[i] = hm[i] = tt(HL[i], PS[:, i, :], HH[i].bitcast(F32), ALU.subtract, [a, hfree[i]])

            tg = None
            for j in range(lag, nj):
                s = j % 2
                hf, hh, hl = H[:, s, :], HH[s], HL[s]
                if relu:
                    b = j % 4
                    tg = up("ff1", b, rdy)
                    if j == lag:
                        first_hidden(0)
                        first_hidden(1)
                    a = av(G[:, s, :], PS[:, b, :], ACT.Relu, [tg, fr])
                    d = tt(hf, G[:, s, :], PS[:, b, :], ALU.mult, [a, hm.get(j - 2)])
                    BF[b] = d
                    hfree[s] = down("ff2", hm[j - 2], halves_h[s], j == lag)
                else:
                    bg, bu = 2 * s, 2 * s + 1
                    tg = up("gate", bg, rdy)
                    if j == lag:
                        first_hidden(0)
                    tu = up("up", bu, rdy)
                    a = av(G[:, s, :], PS[:, bg, :], ACT.Tanh, [tg, fr], scale=0.5)
                    d = stt(G[:, 2 + s, :], G[:, s, :], 1.0, PS[:, bg, :], ALU.add, ALU.mult, [a])
                    BF[bg] = d
                    if j == nj - 1:
                        split_more(at["use"] + 2)
                    d = stt(hf, G[:, 2 + s, :], 0.5, PS[:, bu, :], ALU.mult, ALU.mult, [d, tu, hm.get(j - 2)])
                    BF[bu] = d
                    if j in beside:
                        beside[j]([tg, hm[0], hm[j - 1], m_rope, m_pet])
                    if j < nj - 1:
                        i = 1 - s
                        hfree[i] = down("down", hm[j - 1], halves_h[i], j == 1)
                    tg = tu
                a = av(hh, hf, ACT.Copy, [d, hfree[s]])
                hm[j] = tt(hl, hf, hh.bitcast(F32), ALU.subtract, [a], q=pool if j < nj - 1 else dve)
            free["a"] = [tg, tg]
            free["region"] = [hm[nj - 3], hm[nj - 2], hm[nj - 1], d, a]
            last = range(nj - 2, nj)
            t = last_downs("ff2" if relu else "down", [(hm[i], hm[i]) for i in last], [halves_h[i % 2] for i in last],
                           EVEN)
            free["h0"] = free["h1"] = t[1]
            return t, 1.0 if relu else 0.5

        def run_units(units, P2, PT2, fill, pace, before=0):
            n = len(units)
            marks = [None] * n
            pfree, tfree = [None, None], [None, None]

            def head(u):
                q = units[u]
                s = u % 2
                t = q["scores"](4 + 2 * s)
                P = P2[s]
                d = q["shift"](4 + 2 * s, P, [t, pfree[s], q["old"]])
                BF[4 + 2 * s] = BF[5 + 2 * s] = d
                P = P[:, :, 0:q["w"]]
                d = red(mx[:, 4 * s:4 * s + 4], P, ALU.max, [d])
                marks[u] = ts(nb[:, 4 * s:4 * s + 4], mx[:, 4 * s:4 * s + 4], -q["scale"], None, ALU.mult, w=[d])

            def exps(u):
                q = units[u]
                s = u % 2
                P = P2[s][:, :, 0:q["w"]]
                for i in range(4):
                    a = av(P[:, i, :], P[:, i, :], ACT.Exp, [marks[u]], scale=q["scale"], bias=nb[:, 4 * s + i:4 * s + i + 1],
                           accum_out=den[:, 4 * s + i:4 * s + i + 1])
                return a

            head(0)
            em = exps(0)
            for _ in range(before):
                fill.pop(0)()
            for u in range(n):
                q = units[u]
                s = u % 2
                nk = q["w"] // 128
                if u + 1 < n:
                    head(u + 1)
                for _ in range(pace[2 * u] if pace else 0):
                    if fill:
                        fill.pop(0)()
                evs = []
                for k in range(nk):
                    for i in range(4):
                        t = tr(PS[:, k, i * 128:(i + 1) * 128], P2[s][:, i, k * 128:(k + 1) * 128], IDN, [em, BF[k]], i == 3)
                    pt = PT2[s][:, k * 512:(k + 1) * 512]
                    if k:
                        e = cp(pt, PS[:, k, :], [t, tfree[s], q["old"]])
                    else:
                        e = av(pt, PS[:, k, :], ACT.Copy, [t, tfree[s], q["old"]])
                    BF[k] = e
                    evs.append(e)
                pfree[s] = t
                e_now = em
                if u + 1 < n:
                    em = exps(u + 1)
                for _ in range(pace[2 * u + 1] if pace else 0):
                    if fill:
                        fill.pop(0)()
                tfree[s] = q["values"](s, PT2[s], evs, e_now)
                if "after" in q:
                    q["after"]()
            while fill:
                fill.pop(0)()
            return [tfree[0], tfree[1]]

        def hybrid(l, prev):
            product, tm = token_product(("v_r", "v_r"), True, 512)
            rdy = turn_over(prev, product)
            fr = free["region"]
            qT = R[:, 0:1024].rearrange("p (k n) -> p k n", k=4)
            kvT = R[:, 1024:2048]
            vN = R[:, 2048:2560].rearrange("p (m n) -> p m n", m=2)
            gT = R[:, 2560:2816]
            Bk = R[:, 1024:1984]
            sTh = R[:, 2304:2432]
            tmp = R[:, 8128:8640]
            qrT = R[:, 4032:5056].rearrange("p (k n) -> p k n", k=4)
            krT = R[:, 5056:6080].rearrange("p (k n) -> p k n", k=4)
            ST = R[:, 6080:7616]
            DEC = R[:, 7616:9152]
            vr = R[:, 9152:10176]
            gr = R[:, 10176:11200]
            P2 = [R[:, 4032 + 1024 * i:5056 + 1024 * i].rearrange("p (h n) -> p h n", h=4) for i in range(2)]
            PT2 = [R[:, 6080 + 1024 * i:7104 + 1024 * i] for i in range(2)]
            O_ = R[:, 2816:3840]
            mkT = R[:, 9152:11200]
            mV = R[:, 11200:13248]
            w1_load(l, [(1, 15, 1, 2048)], fr)
            w1_m = (s_aux[2], auxn[2])
            for m in range(2):
                BF[m] = av(vr[:, m * 512:(m + 1) * 512], PS[:, m, :], ACT.Copy, [tm[m], fr])
            vrm = BF[1]

            t = up("cmp", 2, rdy)
            for kv in range(2):
                Bv = Bk[:, kv * 480:(kv + 1) * 480].rearrange("p (k g n) -> p k g n", k=16, g=2)
                for g in range(2):
                    src = PS[g * 64:(g + 1) * 64, 2, kv * 256:(kv + 1) * 256]
                    for par in range(2):
                        for hi16 in range(2):
                            v = src.rearrange("p (n k a) -> p k n a", k=8, a=2)[:, :, hi16:hi16 + 15, par]
                            c0 = (l * 2 + kv) * 16 + hi16 * 8
                            pt = PET[par * 64:(par + 1) * 64, c0:c0 + 8]
                            d = tt(Bv[par * 64:(par + 1) * 64, hi16 * 8:hi16 * 8 + 8, g, :], v, bc(pt, 15), ALU.add, [t, m_pet, fr])
            BF[2] = bm_ = d

            for c in range(2):
                b = c
                t = up("q_n", b, rdy)
                BF[b] = av(qT[:, 2 * c:2 * c + 2, :].rearrange("p k n -> p (k n)"), PS[:, b, :], ACT.Copy, [t, fr])
            q_m = BF[1]
            t = up("gates", 3, rdy, n=1)
            a = av(gT[0:24, :], PS[0:24, 3, 0:256], ACT.Tanh, [t, fr], scale=0.5)
            BF[3] = gt_m = a
            pool.load(lambda e: e.dma_start(XN[:, :].rearrange("p (m n) -> p m n", m=2), A["mem"][0, :, :].rearrange("(m p) n -> p m n", p=128)),
                      [free["xn"]], s_aux[1], 0)
            auxn[1] += 16
            mem_in = (s_aux[1], auxn[1])

            def hidden(kv):
                Bv = Bk[:, kv * 480:(kv + 1) * 480].rearrange("p (k c) -> p k c", k=16)
                for c, k0, nk, raw in w1_in[l]:
                    for k in range(k0, k0 + nk) if c == kv else ():
                        t = mm(PS[0:30, 4 + kv, 0:256], Bv[:, k, :], raw[:, k - k0, :], k == 0, k == 15,
                               [w1_m, bm_, BF[4 + kv]], k == 15)
                sv, sh = hn1[0:30, kv * 256:(kv + 1) * 256], hn2[0:30, kv * 256:(kv + 1) * 256]
                pv = PS[0:30, 4 + kv, 0:256]
                a = av(sv, pv, ACT.Tanh, [t, fr], scale=0.5)
                BF[4 + kv] = stt(sh, sv, 1.0, pv, ALU.add, ALU.mult, [a])
                return BF[4 + kv]

            def hidden_T(kv, ready):
                for ht in range(2):
                    t = tr(PS[:, 6 + kv, ht * 32:ht * 32 + 30], hn2[0:30, kv * 256 + ht * 128:kv * 256 + (ht + 1) * 128],
                           CS[0:30, 0:30], [ready, BF[6 + kv]], ht == 1)
                return t

            hn1, hn2 = R[:, 6144:6656], R[:, 6656:7168]
            kh_m = hidden(0)
            vh_m = hidden(1)
            fr = [fr, vh_m]
            pool.load(lambda e: e.dma_start(DEC, A["c_decay"]), [fr], s_aux[0], 0)
            auxn[0] += 16
            aux = (s_aux[0], auxn[0])
            kh = sTh[:, 0:60].rearrange("p (h c) -> p h c", h=2)
            t = hidden_T(0, kh_m)
            BF[6] = kh_m = cp(kh, PS[:, 6, 0:64].rearrange("p (h c) -> p h c", h=2)[:, :, 0:30], [t, fr])
            scv = SC[:, :].rearrange("p (h g n) -> p h g n", h=2, g=2)[:, :, :, 0:15]
            t = hidden_T(1, vh_m)
            for ht in range(2):
                vh_m = cp(scv[:, ht], PS[:, 7, ht * 32:ht * 32 + 30].rearrange("p (g n) -> p g n", g=2), [t, m_sc, free_kc[0]])
            BF[7] = vh_m
            for m in range(2):
                t = tr(PS[:, 0, m * 24:m * 24 + 24], gT[0:24, m * 128:(m + 1) * 128], CS[0:24, 0:24], [gt_m, BF[0]], m == 1)
            g_m = ts(gates.rearrange("p m c -> p (m c)"), PS[:, 0, 0:48], 1.0, 0.5, ALU.add, ALU.mult, [t])
            BF[0] = g_m

            def q_r(c):
                b = 1 + c
                t = up("q_r", b, rdy)
                BF[b] = av(qrT[:, 2 * c:2 * c + 2, :].rearrange("p k n -> p (k n)"), PS[:, b, :], ACT.Copy, [t, fr])

            def k_r(c):
                b = (3, 0)[c]
                t = up("k_r", b, rdy)
                BF[b] = av(krT[:, 2 * c:2 * c + 2, :].rearrange("p k n -> p (k n)"), PS[:, b, :], ACT.Copy, [t, fr])

            pc = PC[:, :].rearrange("p (h n) -> p h n", h=8)[:, :, 0:15]
            cst = {}

            def cmp_scores(m):
                gm = gates[:, m, :].rearrange("p (h b) -> p h b", b=3)
                for h in range(8):
                    r = slice(0, 64) if h < 4 else slice(64, 128)
                    t = mm(PS[:, 4 + h // 4, (h % 4) * 16:(h % 4) * 16 + 15], qT[r, h % 4, m * 128:(m + 1) * 128], kcT[r, 0:15],
                           True, True, [q_m, k_m, BF[4], BF[5]], h == 7)
                cbv = CB[:, m, :].rearrange("p (h n) -> p h n", h=8)
                cmv = CM[:, m, :].rearrange("p (h n) -> p h n", h=8)
                for g in range(2):
                    d = stt(pc[:, 4 * g:4 * g + 4, :], PS[:, 4 + g, 0:64].rearrange("p (h n) -> p h n", h=4)[:, :, 0:15], 0.125,
                            cbv[:, 4 * g:4 * g + 4, :], ALU.mult, ALU.add, [t, m_pc, free_kc[0]])
                BF[4] = BF[5] = d
                d = red(mx, pc, ALU.max, [d])
                d = tt(pc, pc, bc(mx, 15), ALU.subtract, [d])
                a = av(pc, pc, ACT.Exp, [d])
                d = tt(pc, pc, cmv, ALU.mult, [a])
                cst["p"] = d
                d = red(den, pc, ALU.add, [d])
                d2 = ts(den, den, 1e-30, None, ALU.max, w=[d])
                d2 = rcp(den, den, [d2])
                cst["c"] = tt(coef, den, gm[:, :, 0], ALU.mult, [d2, g_m])

            def cmp_turn(m):
                for g in range(2):
                    t = tr(PS[:, 6, g * 128:(g + 1) * 128], PC[:, g * 128:(g + 1) * 128], IDN, [cst["p"], BF[6]], g == 1)
                free_kc[0] = t
                BF[6] = cst["t"] = cp(gT, PS[:, 6, 0:256], [t, cst.get("o"), g_m])

            def cmp_out(m, banks):
                om = O_[:, m * 512:(m + 1) * 512].rearrange("p (h d) -> p h d", h=8)
                for h in range(8):
                    i4, g = h % 4, h // 4
                    b = banks + i4
                    t = mm(PS[:, b, g * 64:(g + 1) * 64], gT[32 * i4:32 * i4 + 15, g * 128:(g + 1) * 128],
                           vcR[32 * i4:32 * i4 + 15, g * 64:(g + 1) * 64], True, True, [cst["t"], v_m, BF[b]], h == 7)
                cst["o"] = t
                for g in range(2):
                    d = tt(om[:, 4 * g:4 * g + 4, :], PS[:, banks:banks + 4, g * 64:(g + 1) * 64], bc(coef[:, 4 * g:4 * g + 4], 64),
                           ALU.mult, [t, cst["c"], k_m, v_m])
                for b in range(banks, banks + 4):
                    BF[b] = d

            q_r(0)
            for g in range(2):
                for ht in range(2):
                    w0 = ((l * 2) * 2 + ht) * 64
                    t = mm(PS[g * 64:(g + 1) * 64, 6, 0:15], W2C[:, w0:w0 + 64], kh[:, ht, g * 15:(g + 1) * 15],
                           ht == 0, ht == 1, [kh_m, m_w2, BF[6]], g == 1 and ht == 1)
            for i4 in range(4):
                for g in range(2):
                    for ht in range(2):
                        w0 = ((l * 2 + 1) * 2 + ht) * 64
                        t2 = mm(PS[32 * i4:32 * i4 + 32, 7, g * 64:(g + 1) * 64], SC[:, (ht * 2 + g) * 32:(ht * 2 + g + 1) * 32],
                                W2C[:, w0:w0 + 64], ht == 0, ht == 1, [vh_m, BF[7]], i4 == 3 and g == 1 and ht == 1)
            BF[6] = k_m = ts(kcT[:, 0:15], PS[:, 6, 0:15], 0.5, None, ALU.mult, w=[t, free_kc[0]])
            BF[7] = v_m = ts(vcR, PS[:, 7, 0:128], 0.5, None, ALU.mult, w=[t2])
            q_r(1)
            cmp_scores(0)
            k_r(0)
            cmp_turn(0)
            k_r(1)
            qk = BF[0]
            cmp_out(0, 0)
            t = up("slc", 7, rdy)
            BF[7] = av(kvT[:, 0:512], PS[:, 7, :], ACT.Copy, [t, fr])
            cmp_scores(1)

            g, mg, gi = gain()
            mn = []
            for m in range(2):
                x = XN[:, m * DM:(m + 1) * DM]
                a = av(R[:, 12224:13248], x, ACT.Square, [mem_in, fr], accum_out=ssq[:, m:m + 1])
                q = mean_root(rstd[:, m:m + 1], ssq[:, m:m + 1], DM, a)
                mn.append(stt(x, x, rstd[:, m:m + 1], g, ALU.mult, ALU.mult, [q, mg]))
            gain_done(gi, mn[1])
            t = natural("g_r", (3, 0), rdy)
            for m in range(2):
                b = (3, 0)[m]
                a = av(gr[:, m * 512:(m + 1) * 512], PS[:, b, :], ACT.Tanh, [t, fr], scale=0.5)
                g2 = stt(gr[:, m * 512:(m + 1) * 512], gr[:, m * 512:(m + 1) * 512], 1.0, PS[:, b, :], ALU.add, ALU.mult, [a])
                BF[b] = g2
            cmp_turn(1)
            for h in range(4):
                b = 4 + h // 2
                t = mm(PS[:, b, (h % 2) * 256:(h % 2) * 256 + 256], krT[:, h, 0:128], qrT[:, h, :], True, True, [qk, BF[b]])
            for h in range(4):
                t = mm(PS[:, 7, h * 128:(h + 1) * 128], krT[:, h, 128:256], qrT[:, h, 128:256], True, True, [BF[7]], h == 3)
            d = tt(ST[:, 0:1024], PS[:, 4:6, :].rearrange("p b n -> p (b n)"), DEC[:, 0:1024], ALU.mult, [t, aux, fr])
            BF[4] = BF[5] = d
            BF[7] = st_m = tt(ST[:, 1024:1536], PS[:, 7, :], DEC[:, 1024:1536], ALU.mult, [t])
            t = up("win", 2, rdy)
            BF[2] = kv_m = av(kvT[:, 512:1024], PS[:, 2, :], ACT.Copy, [t, fr])
            free["a"] = [t, t]
            cmp_out(1, 0)
            free_kc[0] = cst["o"]
            rm = []
            old_m = [free_half[i] for i in range(at["use"]) if place[i] == NSPLIT][-1]
            for m in range(2):
                for half in range(2):
                    h_, t = to_halves(m, half, MHI, MLO, mn[m], old_m, 1 + half)
                    rm.append(h_)
            free["xn"] = t
            rm = rm[2:]
            s0 = ST[:, 0:1024].rearrange("p (h n) -> p h n", h=4)
            s1 = ST[:, 1024:1536].rearrange("p (h n) -> p h n", h=4)
            t_o = []
            for m in range(2):
                for h in range(4):
                    ob = PS[:, 6 + m, h * 128:(h + 1) * 128]
                    if m == 0:
                        t = mm(ob, s0[:, h, 0:128], vr[:, h * 128:(h + 1) * 128], True, True, [st_m, vrm, BF[6]], h == 3)
                    else:
                        mm(ob, s0[:, h, 128:256], vr[:, h * 128:(h + 1) * 128], True, False, [st_m, vrm, BF[7]])
                        t = mm(ob, s1[:, h, :], vr[:, 512 + h * 128:512 + (h + 1) * 128], False, True, [], h == 3)
                t_o.append(t)
            ret_pe = t

            gg, mg, gi = gain()
            xr = XN[:, :].rearrange("p (m a h n) -> p m a h n", m=2, a=2, h=4)
            d = red(rsum, PS[:, 6:8, :].rearrange("p m (h n) -> p m h n", h=4), ALU.add, [t_o])
            d = ts(rsum, rsum, 1.0 / 128, None, ALU.mult, w=[d])
            for m in range(2):
                d = tt(xr[:, m, 1], PS[:, 6 + m, :].rearrange("p (h n) -> p h n", h=4), bc(rsum[:, 4 * m:4 * m + 4], 128),
                       ALU.subtract, [d, free["xn"]])
            BF[6] = BF[7] = cen = d
            ret = {}

            def ret_norm():
                for m in range(2):
                    a = av(XN[:, m * DM:m * DM + 512], XN[:, m * DM + 512:(m + 1) * DM], ACT.Square, [cen])
                d = red(rsum, xr[:, :, 0], ALU.add, [a])
                ret["x"] = []
                q = [None, None]
                for m in range(2):
                    xn = XN[:, m * DM + 512:(m + 1) * DM]
                    q[m] = tt(xn, xn, gg[:, 0:512], ALU.mult, [cen, a, mg], q=pool)
                    q[m] = tt(xn, xn, gr[:, m * 512:(m + 1) * 512], ALU.mult, [q[m], g2], q=pool)
                ret["m"] = mean_root(rsum, rsum, 128, d, 0.5), q

            def ret_scale():
                d, q = ret["m"]
                for m in range(2):
                    ret["x"].append(tt(xr[:, m, 1], xr[:, m, 1], bc(rsum[:, 4 * m:4 * m + 4], 128), ALU.mult, [d, q[m]]))
                mem_done[l]["late"] = ret["x"]

            kvv = kvT.rearrange("p (b n) -> p b n", b=4)
            for br in range(2):
                for m in range(2):
                    t = tr(PS[:, 1, (m * 2 + br) * 128:(m * 2 + br + 1) * 128], kvv[:, 2 * br + 1, m * 128:(m + 1) * 128], IDN,
                           [kv_m, BF[1]], br == 1 and m == 1)
            BF[1] = vn_m = av(vN.rearrange("p m n -> p (m n)"), PS[:, 1, :], ACT.Copy, [t, fr])
            memory_products(l, rm, mkT, mV, [fr, ret_pe])
            wrdy = [[None, None] for _ in range(4)]

            def ret_tiles():
                for m in range(2):
                    d, t = to_halves(m, 1, AHI, ALO, ret["x"][m], free["a"][m], m)
                    wrdy[2][m] = wrdy[3][m] = d

            for at_, piece in RET_AT:
                fills.insert(at_, (ret_norm, ret_scale, ret_tiles)[piece])

            units = []
            om_m = [None]

            def unit(m, g, br):
                w = 128 * (m + 1)
                rs = slice(g * 64, g * 64 + 64)
                kT = kvv[:, 2 * br, :]
                al = ALIBI[:, 0:128] if m == 0 else ALIBI[:, 128:384]
                gm = gates[:, m, :].rearrange("p (h b) -> p h b", b=3)
                om = O_[:, m * 512 + g * 256:m * 512 + g * 256 + 256].rearrange("p (h d) -> p h d", h=4)

                def scores(b):
                    for i in range(4):
                        t = mm(PS[:, b + i // 2, (i % 2) * 256:(i % 2) * 256 + w], qT[rs, i, m * 128:(m + 1) * 128], kT[rs, 0:w],
                               True, True, [q_m, kv_m, BF[b + i // 2]], i == 3)
                    return t

                def shift(b, P, marks):
                    for i in range(4):
                        d = stt(P[:, i, 0:w], al, 8.0 * SLOPES[4 * g + i], PS[:, b + i // 2, (i % 2) * 256:(i % 2) * 256 + w],
                                ALU.mult, ALU.add, marks)
                    return d

                def values(s, PT, evs, em):
                    d2 = rcp(den[:, 4 * s:4 * s + 4], den[:, 4 * s:4 * s + 4], [em])
                    d2 = tt(coef[:, 4 * s:4 * s + 4], den[:, 4 * s:4 * s + 4], gm[:, 4 * g:4 * g + 4, 1 + br], ALU.mult, [d2])
                    for i in range(4):
                        for k in range(m + 1):
                            t = mm(PS[:, 2, s * 256 + i * 64:s * 256 + (i + 1) * 64], PT[:, (k * 4 + i) * 128:(k * 4 + i + 1) * 128],
                                   vN[:, k, br * 128 + g * 64:br * 128 + (g + 1) * 64], k == 0, k == m,
                                   [evs, vn_m, BF[2]], i == 3 and k == m)
                    tm = tmp[:, s * 256:(s + 1) * 256]
                    d = tt(tm.rearrange("p (h d) -> p h d", h=4), PS[:, 2, s * 256:(s + 1) * 256].rearrange("p (h d) -> p h d", h=4),
                           bc(coef[:, 4 * s:4 * s + 4], 64), ALU.mult, [t, d2, om_m[0]])
                    BF[2] = d
                    om_m[0] = tt(om, om, tm.rearrange("p (h d) -> p h d", h=4), ALU.add, [d], q=pool)
                    omr[m] = om_m[0]
                    return t

                units.append({"scores": scores, "shift": shift, "values": values, "scale": 0.125, "w": w,
                              "old": [ret_pe, st_m]})

            omr = [None, None]
            for m in range(2):
                for g in range(2):
                    for br in range(2):
                        unit(m, g, br)
            fin = {}

            def fin_norm(m):
                xn = XN[:, m * DM:m * DM + 512]
                of = O_[:, m * 512:(m + 1) * 512]
                a = av(xn, of, ACT.Square, [omr[m], ret["x"]], accum_out=ssq[:, m:m + 1])
                q = mean_root(rstd[:, m:m + 1], ssq[:, m:m + 1], 512, a)
                fin[m] = stt(xn, of, rstd[:, m:m + 1], gg[:, 512:1024], ALU.mult, ALU.mult, [q])

            def fin_tile(m):
                d, t = to_halves(m, 0, AHI, ALO, fin[m], free["a"][m], m)
                wrdy[0][m] = wrdy[1][m] = d
                free["xn"] = t

            units[3]["after"] = lambda: fin_norm(0)
            units[4]["after"] = lambda: fin_tile(0)
            tf = run_units(units, P2, PT2, fills, PACE, BEFORE)
            fin_norm(1)
            gain_done(gi, fin[1])
            y = eight("w_out", AHI, ALO, wrdy, (2, 3, 0, 1), None, {4: lambda: fin_tile(1)})
            free["region"] = [tf, fin[1], free["xn"], wrdy[0][1]]
            free["a"] = y
            return y

        auxn = [0, 0, 0]
        w1_in = [[], []]

        def w1_load(l, parts, marks):
            for c, k0, nk, o0 in parts:
                dst = R[:, o0:o0 + nk * 256].rearrange("p (k n) -> p k n", k=nk)
                src = rows(A["cmp_w1"][l, c, :, :], k0, k0 + nk, 0, 256)
                pool.load(lambda e, o=dst, s=src: e.dma_start(o, s), marks, s_aux[2], 0)
                auxn[2] += 16
                w1_in[l].append((c, k0, nk, dst))

        def w1_ahead(l, marks):
            w1_load(l, [(0, 0, 8, 4096), (0, 8, 7, 7168), (0, 15, 1, 3072), (1, 0, 3, 3328), (1, 3, 12, 10176)], marks)

        free_kc = [None]
        fills = []
        mem_done = {}

        def memory_products(l, rm, mkT, mV, old):
            if l in mem_done:
                return
            mem_done[l] = {}

            def key(c, f, st_):
                def go():
                    if f == 0:
                        st_["w"] = take("wk")
                    hi, lo, mark, i = st_["w"]
                    t = up_tile(hi, lo, mark, f, 3, 0, rm, MHI, MLO)
                    if f == 1:
                        done(i, t)
                    BF[3] = av(mkT[:, (2 * c + f) * 256:(2 * c + f + 1) * 256], PS[:, 3, 0:256], ACT.Copy, [t, old, mem_done[l]["late"] if c >= 2 else None])
                    mem_done[l]["k"] = BF[3]
                return go

            def value(n, m, c, st_):
                def go():
                    if m == 0:
                        st_[c] = take("wv", AHEAD - c)
                    hi, lo, mark, i = st_[c]
                    xh = MHI[:, :].rearrange("p (k n) -> p k n", k=8)
                    xl = MLO[:, :].rearrange("p (k n) -> p k n", k=8)
                    ms = slice(m * 128, (m + 1) * 128)
                    for kk in range(4):
                        k = 4 * c + kk
                        for s, (x, w) in enumerate(((xh, hi), (xh, lo), (xl, hi))):
                            t = mm(PS[:, 3, :], x[:, k, ms], w[:, kk, :], k == 0 and s == 0, k == 7 and s == 2,
                                   [mark, rm, BF[3]], kk == 3 and s == 2)
                    if m == 1:
                        done(i, t)
                    if c == 1:
                        BF[3] = av(mV[:, m * DM + n * 512:m * DM + (n + 1) * 512], PS[:, 3, :], ACT.Copy, [t, old])
                        mem_done[l]["v"] = BF[3]
                    free["m"] = t
                return go

            for c in range(4):
                st_ = {}
                for f in range(2):
                    fills.append(key(c, f, st_))
            for n in range(2):
                st_ = {}
                for m in range(2):
                    for c in range(2):
                        fills.append(value(n, m, c, st_))

        def memory(l, prev):
            product, tm = token_product(("wq", "wq"), False)
            rdy = turn_over(prev, product)
            fr = free["region"]
            kT = R[:, 9152:11200]
            V = R[:, 11200:13248]
            km, vm = mem_done[l]["k"], mem_done[l]["v"]
            qT = R[:, 0:2048]
            P_ = R[:, 2048:4096].rearrange("p (s m n) -> p s m n", s=4, m=2)
            PT_ = R[:, 4096:6144].rearrange("p (h k n) -> p h k n", k=2, h=4)
            QN = R[:, 6144:7168].rearrange("p (m n) -> p m n", m=2)
            qv = qT.rearrange("p (k n) -> p k n", k=8)
            kv = kT.rearrange("p (k n) -> p k n", k=8)
            pm, ordy = {}, [[None, None] for _ in range(4)]

            def scores(c):
                b = c % 2
                for m in range(2):
                    for k in range(2):
                        t = mm(PS[:, b, m * 256:(m + 1) * 256], qv[:, 2 * c + k, m * 128:(m + 1) * 128], kv[:, 2 * c + k, :],
                               k == 0, k == 1, [qm[c], km, BF[b]], m == 1 and k == 1)
                S = PS[:, b, :].rearrange("p (m n) -> p m n", m=2)
                o = 2 * (c % 2)
                d = red(mx[:, o:o + 2], S, ALU.max, [t])
                d = ts(nb[:, o:o + 2], mx[:, o:o + 2], -0.0625, None, ALU.mult, w=[d])
                for m in range(2):
                    a = av(P_[:, c, m, :], S[:, m, :], ACT.Exp, [d, fr], scale=0.0625, bias=nb[:, o + m:o + m + 1],
                           accum_out=den[:, o + m:o + m + 1])
                BF[b] = a
                d = rcp(den[:, o:o + 2], den[:, o:o + 2], [a])
                for m in range(2):
                    d = ts(P_[:, c, m, :], P_[:, c, m, :], den[:, o + m:o + m + 1], None, ALU.mult, w=[d])
                pm[c] = d

            def turn(c):
                b = (2, 2, 2, 0)[c]
                for m in range(2):
                    for k in range(2):
                        t = tr(PS[:, b, (k * 2 + m) * 128:(k * 2 + m + 1) * 128], P_[:, c, m, k * 128:(k + 1) * 128], IDN,
                               [pm[c], BF[b]], m == 1 and k == 1)
                BF[b] = pm[c] = av(PT_[:, c, :, :].rearrange("p k n -> p (k n)"), PS[:, b, :], ACT.Copy, [t, fr])

            def outs(c):
                b = (3, 3, 3, 1)[c]
                for j in range(2):
                    f = 2 * c + j
                    for k in range(2):
                        t = mm(PS[:, b, j * 256:(j + 1) * 256], V[:, k * DM + f * 128:k * DM + (f + 1) * 128],
                               PT_[:, c, k, :], k == 0, k == 1, [pm[c], vm, BF[b]], j == 1 and k == 1)
                hi, lo = AHI[:, c * 512:(c + 1) * 512], ALO[:, c * 512:(c + 1) * 512]
                a = av(hi, PS[:, b, :], ACT.Copy, [t, free["a"]])
                BF[b] = tt(lo, PS[:, b, :], hi.bitcast(F32), ALU.subtract, [a, free["a"]])
                ordy[c][0] = ordy[c][1] = BF[b]
                free["region"] = [t]

            qm = {}

            def query(c, bank, t):
                BF[bank] = qm[c] = av(qT[:, c * 512:(c + 1) * 512], PS[:, bank, :], ACT.Copy, [t, fr])

            qn = []
            for m in range(2):
                BF[m] = av(QN[:, m, :], PS[:, m, :], ACT.Copy, [tm[m], fr])
                qn.append(BF[m])
            t2 = up("wq", 2, rdy)
            for c in range(2):
                query(c, c, turned(QN, c, qn, 2 * c))
            query(2, 2, t2)
            hi, lo, mark, i = take("wq")
            up_tile(hi, lo, mark, 0, 3, 0, rdy, AHI, ALO)
            scores(0)
            t = up_tile(hi, lo, mark, 1, 3, 1, rdy, AHI, ALO)
            done(i, t)
            free["a"] = [t, t]
            query(3, 3, t)
            scores(1)
            turn(0)
            scores(2)
            outs(0)
            turn(1)
            scores(3)

            def beside_0():
                outs(1)
                turn(2)
                turn(3)

            def beside_1():
                outs(2)
                outs(3)

            y = eight("wo", AHI, ALO, ordy, (0, 1, 2, 3), {0: beside_0, 1: beside_1})
            free["a"] = y
            return y, 1.0

        def sparse(l, prev):
            product, tm = token_product(("q", "q"), True, 512)
            rdy = turn_over(prev, product)
            fr = free["region"]
            qn = R[:, 0:1024]
            kn = R[:, 1024:2048]
            iqn = R[:, 2048:3072]
            P2 = [R[:, 1024 * i:1024 * i + 1024].rearrange("p (h n) -> p h n", h=4) for i in range(2)]
            V = R[:, 3072:4096]
            U = R[:, 4096:5120]
            ikn = R[:, 5120:5376]
            ikT = R[:, 5376:5632]
            iqT = R[:, 5632:6656].rearrange("p (k n) -> p k n", k=4)
            qT = R[:, 6656:7680].rearrange("p (k n) -> p k n", k=4)
            kT = R[:, 7680:8704].rearrange("p (k n) -> p k n", k=4)
            PT2 = [R[:, 5120:6144], R[:, 2048:3072]]
            SCO = R[:, 10752:11136]
            PM = R[:, 8704:10240]
            WP = R[:, 10240:10752]
            pool.load(lambda e: e.dma_start(PM, A["c_pool"]), [fr], s_aux[0], 0)
            pool.load(lambda e: e.dma_start(WP.rearrange("p (g n) -> p g n", g=4), A["w_pool_2"][l, :, :, :].rearrange("g p n -> p g n")),
                      [fr], s_aux[0], 0)
            auxn[0] += 32
            aux = (s_aux[0], auxn[0])
            cosv = COS.rearrange("p (m j) -> p m j", m=2)
            sinv = SIN.rearrange("p (m j) -> p m j", m=2)
            rt = [XN[:, i * 128:(i + 1) * 128] for i in range(4)]

            def rope(v, h, w):
                def sh(i):
                    return rt[i][:, 0:2 * h * 8].rearrange("p (m h j) -> p m h j", m=2, h=h)
                c = cosv.unsqueeze(2).broadcast_to([128, 2, h, 8])
                s = sinv.unsqueeze(2).broadcast_to([128, 2, h, 8])
                x1, x2 = v[:, :, :, 0:8], v[:, :, :, 8:16]
                ws = [w, m_rope, free["xn"], rope_last[0]]
                tt(sh(0), x1, c, ALU.mult, ws, q=pool)
                tt(sh(1), x2, s, ALU.mult, q=pool)
                tt(sh(2), x2, c, ALU.mult, q=pool)
                p = tt(sh(3), x1, s, ALU.mult, q=pool)
                tt(x1, sh(0), sh(1), ALU.subtract, [p], q=pool)
                p = tt(x2, sh(2), sh(3), ALU.add, q=pool)
                rope_last[0] = p
                return p

            def heads_T(src, dst, ready, bank, w):
                outs = []
                for m in range(2):
                    b = bank + m
                    for k in range(4):
                        t = tr(PS[:, b, k * 128:(k + 1) * 128], src[:, m * 512 + k * 128:m * 512 + (k + 1) * 128], IDN,
                               [ready, BF[b]], k == 3)
                    e = av(dst[:, :, m * 128:(m + 1) * 128], PS[:, b, :].rearrange("p (k n) -> p k n", k=4), ACT.Copy, [t, w])
                    BF[b] = e
                    outs.append(e)
                return outs, t

            for m in range(2):
                e = av(qn[:, m * 512:(m + 1) * 512], PS[:, m, :], ACT.Copy, [tm[m], fr])
                BF[m] = e
            q_in = e
            t = natural("iq", (2, 3), rdy, 292)
            for m in range(2):
                e = av(iqn[:, m * 512:m * 512 + 292], PS[:, 2 + m, 0:292], ACT.Copy, [t, fr])
                BF[2 + m] = e
            t = natural("iq", (0, 1), rdy, 292)
            for m in range(2):
                a = av(iqn[:, m * 512 + 292:(m + 1) * 512], PS[:, m, 0:220], ACT.Copy, [t, fr])
                d = cp(ikn[:, m * 128:m * 128 + 64], PS[:, m, 220:284], [a, t, fr])
                e = av(iw[:, m, :], PS[:, m, 284:292], ACT.Copy, [d], scale=8.0 ** -0.5)
                BF[m] = e
            iqm = rope(iqn.rearrange("p (m h d) -> p m h d", m=2, h=8), 8, e)
            ikv = ikn.rearrange("p (m h d) -> p m h d", m=2, h=2)
            ikm = rope(ikv[:, :, 0:1, :], 1, d)
            ikm = pool.add(lambda e: e.tensor_copy(ikv[:, :, 1, :], ikv[:, :, 0, :]), [ikm])
            qm = rope(qn.rearrange("p (m h d) -> p m h d", m=2, h=8), 8, q_in)
            t = natural("k", (2, 3), rdy)
            for m in range(2):
                e = av(kn[:, m * 512:(m + 1) * 512], PS[:, 2 + m, :], ACT.Copy, [t, fr])
                BF[2 + m] = e
            km = rope(kn.rearrange("p (m h d) -> p m h d", m=2, h=8), 8, e)
            rope_pool = km
            for m in range(2):
                t = tr(PS[:, 4, m * 128:(m + 1) * 128], ikn[:, m * 128:(m + 1) * 128], IDN, [ikm, BF[4]], m == 1)
            BF[4] = ikt = cp(ikT, PS[:, 4, 0:256], [t, fr])
            iqt, t_i = heads_T(iqn, iqT, iqm, 5, fr)
            t = natural("v", (2, 3), rdy)
            for m in range(2):
                e = av(V[:, m * 512:(m + 1) * 512], PS[:, 2 + m, :], ACT.Copy, [t, fr])
                BF[2 + m] = e
            vm = e

            qt, t_q = heads_T(qn, qT, qm, 0, fr)
            rls, relu_m = [], []
            for m in range(2):
                w = 128 * (m + 1)
                RL = R[:, 0:1024] if m == 0 else R[:, 11136:13184]
                rl = RL.rearrange("p (b a n) -> p b a n", b=4, a=2)
                for h in range(8):
                    b = 4 + h % 4
                    c = (h // 4) * 256
                    r = slice((h % 2) * 64, (h % 2) * 64 + 64)
                    t = mm(PS[:, b, c:c + w], iqT[r, h // 2, m * 128:(m + 1) * 128], ikT[r, 0:w], True, True,
                           [ikt, iqt, BF[b]], h == 7)
                a = av(rl, PS[:, 4:8, :].rearrange("p b (a n) -> p b a n", a=2)[:, :, :, 0:w], ACT.Relu,
                       [t, t_q, fr], scale=0.125)
                for b in range(4, 8):
                    BF[b] = a
                t_ix = t
                rls.append(rl)
                relu_m.append(a)
            kt_, t_k = heads_T(kn, kT, km, 0, fr)
            sel = []

            def select(m):
                w = 128 * (m + 1)
                rl = rls[m]
                s = SCO[:, m * 128:m * 128 + w]
                ch = CH[:, 0:128] if m == 0 else CH[:, 128:384]
                for h in range(8):
                    rh = rl[:, h % 4, h // 4, :]
                    if h == 0:
                        d = stt(s, rh, iw[:, m, 0:1], ch, ALU.mult, ALU.add, [relu_m[m], fr])
                    else:
                        d = stt(s, rh, iw[:, m, h:h + 1], s, ALU.mult, ALU.add, [d])
                for _ in range(8):
                    d = dve.add(lambda e, s=s: e.max(top8, s), [d])
                    d = dve.add(lambda e, s=s: e.match_replace(s, top8, s, TAKEN), [d])
                sel.append(ts(PSC2[:, m * 128:m * 128 + w], s, TAKEN, NEG, ALU.not_equal, ALU.mult, [d]))

            select(0)
            DT = R[:, 11136:12160]
            uw, um, dt = {}, {}, {}

            def u_part(m, c):
                def go():
                    if m == 0:
                        uw[c] = take("u", AHEAD - c)
                    hi, lo, mark, i = uw[c]
                    ms = slice(m * 128, (m + 1) * 128)
                    for kk in range(4):
                        k = 4 * c + kk
                        for z, (x, w) in enumerate(((xh, hi), (xh, lo), (xl, hi))):
                            t = mm(PS[:, 3, :], x[:, k, ms], w[:, kk, :], k == 0 and z == 0, k == 7 and z == 2,
                                   [mark, rdy[c], BF[3]], kk == 3 and z == 2)
                    if m == 1:
                        done(i, t)
                    if c == 1:
                        BF[3] = um[m] = av(U[:, m * 512:(m + 1) * 512], PS[:, 3, :], ACT.Copy, [t, fr])
                        free["a"] = [t, t]
                return go

            def means(a):
                def go():
                    for g in (2 * a, 2 * a + 1):
                        o = PS[:, 3, (g % 2) * 256:(g % 2) * 256 + 256]
                        mm(o, U[:, g * 128:(g + 1) * 128], PM[:, g * 384:g * 384 + 256], True, False, [um[0], um[1], aux, BF[3]])
                        t = mm(o[:, 128:256], U[:, 512 + g * 128:512 + (g + 1) * 128], PM[:, g * 384 + 256:g * 384 + 384], False, True, [], g % 2 == 1)
                    BF[3] = dt[a] = av(DT[:, a * 512:a * 512 + 512], PS[:, 3, :], ACT.Copy, [t, sel[1], fr])
                return go

            def pooled(a):
                def go():
                    for g in (2 * a, 2 * a + 1):
                        t = mm(PS[:, 3, (g % 2) * 256:(g % 2) * 256 + 256], WP[:, g * 128:(g + 1) * 128], DT[:, g * 256:(g + 1) * 256],
                               True, True, [dt[a], BF[3]], g % 2 == 1)
                    free["pool"] = t
                    for g in (2 * a, 2 * a + 1):
                        y = PS[:, 3, (g % 2) * 256:(g % 2) * 256 + 256]
                        e = av(AHI[:, g * 256:(g + 1) * 256], y, ACT.Copy, [t, free["a"], m_pet], scale=PSC[:, l * 4 + g:l * 4 + g + 1])
                    for g in (2 * a, 2 * a + 1):
                        y = PS[:, 3, (g % 2) * 256:(g % 2) * 256 + 256]
                        hi, lo = AHI[:, g * 256:(g + 1) * 256], ALO[:, g * 256:(g + 1) * 256]
                        d = stt(lo, y, PSC[:, l * 4 + g:l * 4 + g + 1], hi.bitcast(F32), ALU.mult, ALU.subtract, [e, free["a"]])
                    BF[3] = d
                    wrdy[a][0] = wrdy[a][1] = d
                return go

            xh = AHI[:, :].rearrange("p (k n) -> p k n", k=8)
            xl = ALO[:, :].rearrange("p (k n) -> p k n", k=8)
            wrdy = [[None, None] for _ in range(4)]
            fill = [u_part(m, c) for m in range(2) for c in range(2)] + [means(0), means(1), pooled(0), pooled(1)]
            fill.insert(0, lambda: select(1))

            units, tl = [], []

            def unit(m, g):
                w = 128 * (m + 1)

                def scores(b):
                    for i in range(4):
                        r = slice((i % 2) * 64, (i % 2) * 64 + 64)
                        c = (i // 2) * 256
                        t = mm(PS[:, b + i % 2, c:c + w], qT[r, 2 * g + i // 2, m * 128:(m + 1) * 128],
                               kT[r, 2 * g + i // 2, 0:w], True, True, [qt, kt_, BF[b + i % 2]], i == 3)
                    return t

                def shift(b, P, marks):
                    bi = PSC2[:, m * 128:m * 128 + w]
                    for i in range(2):
                        sv = PS[:, b + i, :].rearrange("p (a n) -> p a n", a=2)[:, :, 0:w]
                        d = stt(P[:, 2 * i:2 * i + 2, 0:w], sv, 0.125, bm(bi, 2), ALU.mult, ALU.add, [marks, sel[m]])
                    return d

                def values(s, PT, evs, em):
                    d2 = rcp(den[:, 4 * s:4 * s + 4], den[:, 4 * s:4 * s + 4], [em])
                    for i in range(4):
                        h = 4 * g + 2 * (i % 2) + i // 2
                        for k in range(m + 1):
                            t = mm(PS[:, 2, s * 256 + i * 64:s * 256 + (i + 1) * 64], PT[:, (k * 4 + i) * 128:(k * 4 + i + 1) * 128],
                                   V[:, k * 512 + h * 64:k * 512 + (h + 1) * 64], k == 0, k == m,
                                   [evs, vm, BF[2]], i == 3 and k == m)
                    x0 = m * DM + 512 + g * 256
                    xo = XN[:, x0:x0 + 256].rearrange("p (a b d) -> p b a d", a=2, b=2)
                    ov = PS[:, 2, s * 256:(s + 1) * 256].rearrange("p (b a d) -> p b a d", b=2, a=2)
                    dn = den[:, 4 * s:4 * s + 4].rearrange("p (b a) -> p b a", a=2)
                    d = tt(xo, ov, bc(dn, 64), ALU.mult, [t, d2, rope_pool, free["xn"]])
                    BF[2] = d
                    tl.append(d)
                    return t

                units.append({"scores": scores, "shift": shift, "values": values, "scale": 1.0, "w": w,
                              "old": [t_i, t_q, t_k, t_ix]})

            for m in range(2):
                for g in range(2):
                    unit(m, g)
            def tile(m):
                e, t = to_halves(m, 1, AHI, ALO, tl[2 * m + 1], free["a"][m], m)
                wrdy[2][m] = wrdy[3][m] = e
                free["xn"] = t

            units[2]["after"] = lambda: tile(0)
            tf = run_units(units, P2, PT2, fill, PACE2, BEFORE2)
            y = eight("w_out2", AHI, ALO, wrdy, (0, 1, 2, 3), None, {4: lambda: tile(1)})
            free["region"] = [tf, free["pool"], wrdy[2], free["xn"]]
            free["a"] = y
            return y, 1.0

        rope_last = [None]
        m_pet = m_rope = m_sc = m_pc = m_pe = m_ps = m_w2 = m_pos = m_cs2 = m_cs3 = None

        def small_loads(marks):
            nonlocal m_sc, m_pc, m_pe, m_ps, m_w2, m_pos, m_cs2, m_cs3
            m_pe = qload(4, pe_in, A["cmp_pe"].rearrange("l c (k a) d -> (l c k) (a d)", a=2))
            m_ps = qload(5, ps_in, A["pool_scale_2"].rearrange("l (g p) -> (l g) p", p=128))
            m_w2 = qload(6, W2C[:, :].rearrange("p (a d) -> p a d", d=64),
                         A["cmp_w2"].rearrange("l c (k p) d -> p (l c k) d", p=128))
            m_pos = qload(7, pos_in, A["positions_2"].rearrange("o (m p) -> (o m) p", p=128))
            m_cs2 = qload(3, small[:, 0:392], c_small[:, 992:1384])
            m_cs3 = qload(8, CS[:, 128:992], c_small[:, 128:992])
            m_sc = pool.add(lambda e: e.memset(SC[:, :], 0.0), [])
            m_pc = pool.add(lambda e: e.memset(PC[:, :], 0.0), [])

        def small_setup(marks):
            nonlocal m_pet, m_rope
            dve.wait([m_cs2, m_cs3])
            t1 = tr(PS[:, 0, 0:64], pe_in, CS[0:64, 0:64], [m_pe, BF[0]])
            t1 = tr(PS[:, 0, 64:72], ps_in, CS[0:8, 0:8], [m_ps], True)
            m_pet = cp(SM[:, 0:72], PS[:, 0, 0:72], [t1])
            BF[0] = m_pet
            p = cp(pos_row, pos_in, [m_pos])
            t1 = tr(PS[:, 0, 128:130], pos_row, CS[0:2, 0:2], [p, m_pet], True)
            p = cp(posf, PS[:, 0, 128:130], [t1])
            BF[0] = p
            for shift, dst in ((0.0, SIN), (0.25 * TWO_PI, COS)):
                a = tt(ang.rearrange("p (m j) -> p m j", m=2), bc(posf, 8), bm(INV, 2), ALU.mult, [p, m_cs2])
                a = ts(nrd, ang, 1.0 / TWO_PI, shift / TWO_PI, ALU.mult, ALU.add, [a])
                a = ts(nrd, nrd, ROUND, None, ALU.add, w=[a])
                a = ts(nrd, nrd, ROUND, None, ALU.subtract, w=[a])
                for c in (PI_A, PI_B, PI_C):
                    a = stt(ang, nrd, -c, ang, ALU.mult, ALU.add, [a])
                a = ts(ang, ang, shift, None, ALU.add, w=[a])
                a = ts(ang, ang, 3.14159, -3.14159, ALU.min, ALU.max, [a])
                p = av(dst, ang, ACT.Sin, [a])
            m_rope = p

        prev = m_x, None
        for l in range(2):
            beside = {5: lambda marks, l=l: w1_ahead(l, marks)}
            if l == 0:
                beside[1] = small_loads
                beside[3] = small_setup
            prev = ffn(prev, "swiglu", beside)
            prev = hybrid(l, prev), 1.0
            prev = memory(l, prev)
            prev = ffn(prev, "swiglu")
        for l in range(2):
            prev = sparse(l, prev)
            prev = ffn(prev, "relu2")
        xm = post_norm(*prev)
        for m in range(2):
            for h in range(2):
                c = slice(h * 512, h * 512 + 512)
                o, i = out[0, m * 128:(m + 1) * 128, c], X[:, m * DM + h * 512:m * DM + h * 512 + 512]
                sp.load(lambda e, o=o, i=i: e.dma_start(o, i), [xm[m][h]], s_out, 0)
        sp.wait([(s_out, 64)])
        assert at["use"] == len(items) and gst["use"] == len(gains)

        block = ctx.enter_context(nc.Block())

        @block.sync
        def _(e):
            sp.play(e)

        @block.gpsimd
        def _(e):
            pool.play(e)

        @block.scalar
        def _(e):
            act.play(e)

        @block.vector
        def _(e):
            dve.play(e)

        @block.tensor
        def _(e):
            pe.play(e)


_INS = ["x", "mem", "ffn1_pre_g", "ffn1_w_gate", "ffn1_w_up", "ffn1_w_down", "ffn1_post_g", "mix_pre_g", "w_in",
        "cmp_pe", "cmp_w1", "cmp_w2", "nsa_out_g", "ret_gn_g", "w_out", "mix_post_g", "xa_pre_g", "xa_mem_g", "xa_wq",
        "xa_wk", "xa_wv", "xa_wo", "xa_post_g", "ffn2_pre_g", "ffn2_w_gate", "ffn2_w_up", "ffn2_w_down",
        "ffn2_post_g", "positions_2", "g_pre_mix_2", "w_in_2", "w_pool_2", "pool_scale_2", "w_out_2",
        "g_post_mix_2", "g_pre_ffn_2", "w_ff1_2", "w_ff2_2", "g_post_ffn_2"]


def kernel(**inputs):
    import concourse.bacc as bacc
    from concourse.bass_utils import run_bass_kernel_spmd as run

    nc = bacc.Bacc("TRN2", target_bir_lowering=False, num_devices=1)
    arrays, aps = {}, {}
    for name in _INS:
        arrays[name] = np.ascontiguousarray(inputs[name])
    arrays.update(constants())
    for name, a in arrays.items():
        aps[name] = nc.dram_tensor(name, a.shape, mybir.dt.from_np(a.dtype), kind="ExternalInput").ap()
    out = nc.dram_tensor("out", (1, T, DM), F32, kind="ExternalOutput").ap()
    build(nc, aps, out)
    r = run(nc, [arrays], core_ids=[0])
    return r.results[0]["out"]
```
